# Optimizing a Trainium2 kernel written in Bass

```python
import math
import jax, jax.numpy as jnp
from jax import lax
import numpy as np

D_MODEL = 1024
BATCH = 1
SEQ = 256
DEPTH = 2

GRID_W = 64
CTX_LEN = 256
HEAD_DIM = 64
Q_BLOCK = 128
ROPE_THETA = 10000.0
EPS = 1e-6
N_MOD = 6

POOL_GROUPS = 4
POOL_WINDOWS = (2, 4, 8, 16)
POOL_GROUP_DIM = 64
POOL_WIDTH = POOL_GROUPS * POOL_GROUP_DIM
DIFF_HEADS = 6
DIFF_V_DIM = 2 * HEAD_DIM
DIFF_QK_WIDTH = DIFF_HEADS * 2 * HEAD_DIM
DIFF_WIDTH = DIFF_HEADS * DIFF_V_DIM
EVEN_IN_SIZES = (POOL_WIDTH, DIFF_QK_WIDTH, DIFF_QK_WIDTH, DIFF_WIDTH)
EVEN_OUT = POOL_WIDTH + DIFF_WIDTH
GQA_HEADS = 8
GQA_KV_HEADS = 2
GQA_REP = GQA_HEADS // GQA_KV_HEADS
NA_HEADS = 8
NA_WIN_ROWS = 8
NA_WIN_COLS = 16
ODD_IN_SIZES = (GQA_HEADS * HEAD_DIM, GQA_KV_HEADS * HEAD_DIM, GQA_KV_HEADS * HEAD_DIM,
                NA_HEADS * HEAD_DIM, NA_HEADS * HEAD_DIM, NA_HEADS * HEAD_DIM)
ODD_OUT = (GQA_HEADS + NA_HEADS) * HEAD_DIM
PEER_HEADS = 8
PEER_N_KEYS = 128
PEER_N_EXPERTS = PEER_N_KEYS * PEER_N_KEYS
PEER_KEY_DIM = 128
PEER_TOPK = 16
PEER_BLOCK = 128

kernel_name = "hybrid_pool_diff_gqa_na_peer_dit"

def rms_norm(x, g):
    xf = x.astype(jnp.float32)
    y = xf * lax.rsqrt(jnp.mean(xf * xf, axis=-1, keepdims=True) + EPS)
    return (y * g.astype(jnp.float32)).astype(x.dtype)

def split_cols(p, sizes):
    return jnp.split(p, [int(s) for s in np.cumsum(sizes)[:-1]], axis=-1)

def to_heads(p, n_heads):
    B, L, _ = p.shape
    return p.reshape(B, L, n_heads, -1).transpose(0, 2, 1, 3)

def merge_heads(o):
    B, H, L, d = o.shape
    return o.transpose(0, 2, 1, 3).reshape(B, L, H * d)

def modulation(cvec, ada_w, ada_b):
    return jnp.split(jax.nn.silu(cvec) @ ada_w + ada_b, N_MOD, axis=-1)

def modulate(x, g, shift, scale):
    return rms_norm(x, g) * (1.0 + scale[:, None]) + shift[:, None]

def axial_rope_tables(T):
    t = jnp.arange(T, dtype=jnp.int32)
    pos = jnp.stack([t // GRID_W, t % GRID_W], axis=-1).astype(jnp.float32)
    n_freq = HEAD_DIM // 4
    inv_freq = ROPE_THETA ** (-jnp.arange(n_freq, dtype=jnp.float32) / n_freq)
    ang = pos[:, :, None] * inv_freq
    return jnp.cos(ang), jnp.sin(ang)

def apply_axial_rope(x, cos, sin):
    shp = x.shape
    x4 = x.astype(jnp.float32).reshape(shp[:-1] + (2, 2, HEAD_DIM // 4))
    x1, x2 = x4[..., 0, :], x4[..., 1, :]
    out = jnp.stack([x1 * cos - x2 * sin, x2 * cos + x1 * sin], axis=-2)
    return out.reshape(shp).astype(x.dtype)

def sweep_query_blocks(fn, q):
    T = q.shape[-2]
    nb = T // Q_BLOCK
    qb = jnp.moveaxis(q.reshape(q.shape[:-2] + (nb, Q_BLOCK, q.shape[-1])), -3, 0)
    out = jnp.moveaxis(lax.map(fn, qb), 0, -3)
    return out.reshape(out.shape[:-3] + (T, out.shape[-1]))

def diff_attend(q, k, v, lam):
    s = jnp.einsum("bhiqd,bhind->bhiqn", q, k, preferred_element_type=jnp.float32) * (HEAD_DIM ** -0.5)
    a = jax.nn.softmax(s, axis=-1)
    w = a[:, :, 0] - lam * a[:, :, 1]
    return jnp.einsum("bhqn,bhnv->bhqv", w.astype(v.dtype), v)

def gqa_attend(q, k, v):
    s = jnp.einsum("bgrqd,bgnd->bgrqn", q, k, preferred_element_type=jnp.float32) * (HEAD_DIM ** -0.5)
    a = jax.nn.softmax(s, axis=-1)
    return jnp.einsum("bgrqn,bgnd->bgrqd", a.astype(v.dtype), v)

def multiscale_pool(u, w, scale):
    B, L, _ = u.shape
    uf = u.astype(jnp.float32)
    cs = jnp.concatenate([jnp.zeros((B, 1, POOL_WIDTH), jnp.float32), jnp.cumsum(uf, axis=1)], axis=1)
    t = jnp.arange(L, dtype=jnp.int32)
    outs = []
    for g, win in enumerate(POOL_WINDOWS):
        lo = jnp.clip(t - win // 2, 0, L)
        hi = jnp.clip(t + win // 2, 0, L)
        sl = slice(g * POOL_GROUP_DIM, (g + 1) * POOL_GROUP_DIM)
        csg = cs[:, :, sl]
        mean = (csg[:, hi] - csg[:, lo]) / (hi - lo).astype(jnp.float32)[:, None]
        outs.append(mean - uf[:, :, sl])
    p = jnp.stack(outs, axis=2).astype(u.dtype)
    y = jnp.einsum("blgc,gcd->blgd", p, w).reshape(B, L, POOL_WIDTH)
    return y * scale

def neighbourhood_attend(q, k, v, k_ctx, v_ctx, rpb):
    B, H, T, d = q.shape
    rows = T // GRID_W
    kr = min(NA_WIN_ROWS, rows)
    kc = NA_WIN_COLS
    kg = k.reshape(B, H, rows, GRID_W, d)
    vg = v.reshape(B, H, rows, GRID_W, d)
    cols = jnp.arange(GRID_W, dtype=jnp.int32)
    col_idx = jnp.clip(cols - kc // 2, 0, GRID_W - kc)[:, None] + jnp.arange(kc, dtype=jnp.int32)[None]
    dc = col_idx - cols[:, None] + (NA_WIN_COLS - 1)
    q_rows = jnp.moveaxis(q.reshape(B, H, rows, GRID_W, d), 2, 0)
    scale = d ** -0.5

    def one_row(args):
        q_r, r = args
        r0 = jnp.clip(r - kr // 2, 0, rows - kr)
        k_nb = lax.dynamic_slice_in_dim(kg, r0, kr, axis=2)[:, :, :, col_idx]
        v_nb = lax.dynamic_slice_in_dim(vg, r0, kr, axis=2)[:, :, :, col_idx]
        dr = r0 + jnp.arange(kr, dtype=jnp.int32) - r + (NA_WIN_ROWS - 1)
        bias = rpb[:, dr[:, None, None], dc[None]].astype(jnp.float32)
        s_nb = jnp.einsum("bhcd,bhrckd->bhcrk", q_r, k_nb, preferred_element_type=jnp.float32) * scale
        s_nb = s_nb + jnp.transpose(bias, (0, 2, 1, 3))[None]
        s_ctx = jnp.einsum("bhcd,bhnd->bhcn", q_r, k_ctx, preferred_element_type=jnp.float32) * scale
        s = jnp.concatenate([s_nb.reshape(B, H, GRID_W, kr * kc), s_ctx], axis=-1)
        a = jax.nn.softmax(s, axis=-1).astype(v.dtype)
        a_nb = a[..., :kr * kc].reshape(B, H, GRID_W, kr, kc)
        return (jnp.einsum("bhcrk,bhrckd->bhcd", a_nb, v_nb)
                + jnp.einsum("bhcn,bhnd->bhcd", a[..., kr * kc:], v_ctx))

    out = lax.map(one_row, (q_rows, jnp.arange(rows, dtype=jnp.int32)))
    return jnp.moveaxis(out, 0, 2).reshape(B, H, T, d)

def mixer_pool_diff(p_lat, p_ctx, cos, sin, lam_init, pool_w, pool_scale, qn, kn,
                    lq1, lk1, lq2, lk2, subln, need_ctx):
    u_l, q_l, k_l, v_l = split_cols(p_lat, EVEN_IN_SIZES)
    u_c, q_c, k_c, v_c = split_cols(p_ctx, EVEN_IN_SIZES)

    def qk_heads(p, g):
        B, L, _ = p.shape
        return rms_norm(p.reshape(B, L, DIFF_HEADS, 2, HEAD_DIM).transpose(0, 2, 3, 1, 4), g)

    q_l = apply_axial_rope(qk_heads(q_l, qn), cos, sin)
    k_l = apply_axial_rope(qk_heads(k_l, kn), cos, sin)
    k_c = qk_heads(k_c, kn)
    v_c = to_heads(v_c, DIFF_HEADS)
    k_all = jnp.concatenate([k_c, k_l], axis=3)
    v_all = jnp.concatenate([v_c, to_heads(v_l, DIFF_HEADS)], axis=2)
    f32 = jnp.float32
    lam = (jnp.exp(jnp.sum(lq1.astype(f32) * lk1.astype(f32)))
           - jnp.exp(jnp.sum(lq2.astype(f32) * lk2.astype(f32))) + lam_init)

    def post(o):
        return merge_heads(rms_norm(o, subln) * (1.0 - lam_init))

    o_l = sweep_query_blocks(lambda qb: diff_attend(qb, k_all, v_all, lam), q_l)
    y_lat = jnp.concatenate([multiscale_pool(u_l, pool_w, pool_scale), post(o_l)], axis=-1)
    if not need_ctx:
        return y_lat, None
    o_c = diff_attend(qk_heads(q_c, qn), k_c, v_c, lam)
    y_ctx = jnp.concatenate([multiscale_pool(u_c, pool_w, pool_scale), post(o_c)], axis=-1)
    return y_lat, y_ctx

def mixer_gqa_na(p_lat, p_ctx, cos, sin, gqa_qn, gqa_kn, na_qn, na_kn, rpb, need_ctx):
    cq_l, ck_l, cv_l, nq_l, nk_l, nv_l = split_cols(p_lat, ODD_IN_SIZES)
    cq_c, ck_c, cv_c, nq_c, nk_c, nv_c = split_cols(p_ctx, ODD_IN_SIZES)
    B, T, _ = p_lat.shape
    C = p_ctx.shape[1]
    q = apply_axial_rope(rms_norm(to_heads(cq_l, GQA_HEADS), gqa_qn), cos, sin)
    q = q.reshape(B, GQA_KV_HEADS, GQA_REP, T, HEAD_DIM)
    kc = rms_norm(to_heads(ck_c, GQA_KV_HEADS), gqa_kn)
    vc = to_heads(cv_c, GQA_KV_HEADS)
    kl = apply_axial_rope(rms_norm(to_heads(ck_l, GQA_KV_HEADS), gqa_kn), cos, sin)
    k_all = jnp.concatenate([kc, kl], axis=2)
    v_all = jnp.concatenate([vc, to_heads(cv_l, GQA_KV_HEADS)], axis=2)
    o_gqa = sweep_query_blocks(lambda qb: gqa_attend(qb, k_all, v_all), q).reshape(B, GQA_HEADS, T, HEAD_DIM)
    nkc = rms_norm(to_heads(nk_c, NA_HEADS), na_kn)
    nvc = to_heads(nv_c, NA_HEADS)
    o_na = neighbourhood_attend(rms_norm(to_heads(nq_l, NA_HEADS), na_qn),
                                rms_norm(to_heads(nk_l, NA_HEADS), na_kn),
                                to_heads(nv_l, NA_HEADS), nkc, nvc, rpb)
    y_lat = jnp.concatenate([merge_heads(o_gqa), merge_heads(o_na)], axis=-1)
    if not need_ctx:
        return y_lat, None
    qcc = rms_norm(to_heads(cq_c, GQA_HEADS), gqa_qn).reshape(B, GQA_KV_HEADS, GQA_REP, C, HEAD_DIM)
    o_gqa_c = gqa_attend(qcc, kc, vc).reshape(B, GQA_HEADS, C, HEAD_DIM)
    o_na_c = gqa_attend(rms_norm(to_heads(nq_c, NA_HEADS), na_qn)[:, :, None], nkc, nvc)[:, :, 0]
    y_ctx = jnp.concatenate([merge_heads(o_gqa_c), merge_heads(o_na_c)], axis=-1)
    return y_lat, y_ctx

def peer_ffn(h, wq, sub_keys, u, v):
    B, L, D = h.shape
    nb = L // PEER_BLOCK
    hb = jnp.moveaxis(h.reshape(B, nb, PEER_BLOCK, D), 1, 0)

    def block(x):
        q = (x @ wq).reshape(B, PEER_BLOCK, PEER_HEADS, 2, PEER_KEY_DIM)
        s = jnp.einsum("bthpd,hpnd->bthpn", q, sub_keys, preferred_element_type=jnp.float32)
        sv, si = lax.top_k(s, PEER_TOPK)
        cand_s = (sv[..., 0, :, None] + sv[..., 1, None, :]).reshape(B, PEER_BLOCK, PEER_HEADS, PEER_TOPK * PEER_TOPK)
        cand_i = (si[..., 0, :, None] * PEER_N_KEYS + si[..., 1, None, :]).reshape(B, PEER_BLOCK, PEER_HEADS, PEER_TOPK * PEER_TOPK)
        top_s, pos = lax.top_k(cand_s, PEER_TOPK)
        idx = jnp.take_along_axis(cand_i, pos, axis=-1)
        g = jax.nn.softmax(top_s, axis=-1).astype(x.dtype)
        act = jax.nn.gelu(jnp.einsum("bthkd,btd->bthk", u[idx], x), approximate=False)
        return jnp.einsum("bthk,bthkd->btd", g * act, v[idx])

    out = lax.map(block, hb)
    return jnp.moveaxis(out, 0, 1).reshape(B, L, D)

def setup_inputs(seed: int = 0) -> dict:
    key = jax.random.key(seed)
    keys = iter(jax.random.split(key, 64))

    def nrm(shape, scale):
        return jax.random.normal(next(keys), shape, jnp.float32) * scale

    def gain(n):
        return 1.0 + nrm((n,), 0.1)

    D = D_MODEL
    inp = {}
    inp["x"] = nrm((BATCH, SEQ, D), 1.0)
    inp["c"] = nrm((BATCH, D), 1.0)
    inp["ctx"] = nrm((BATCH, CTX_LEN, D), 1.0)
    inp["c_ctx"] = nrm((D,), 1.0)
    inp["l0_ada_w"] = nrm((D, N_MOD * D), D ** -0.5)
    inp["l0_ada_b"] = nrm((N_MOD * D,), 0.02)
    inp["l0_norm1"] = gain(D)
    inp["l0_norm2"] = gain(D)
    inp["l0_w_in"] = nrm((D, sum(EVEN_IN_SIZES)), D ** -0.5)
    inp["l0_w_out"] = nrm((EVEN_OUT, D), EVEN_OUT ** -0.5)
    inp["l0_pool_w"] = nrm((POOL_GROUPS, POOL_GROUP_DIM, POOL_GROUP_DIM), POOL_GROUP_DIM ** -0.5)
    inp["l0_pool_scale"] = gain(POOL_WIDTH)
    inp["l0_diff_qnorm"] = gain(HEAD_DIM)
    inp["l0_diff_knorm"] = gain(HEAD_DIM)
    inp["l0_lambda_q1"] = nrm((HEAD_DIM,), 0.1)
    inp["l0_lambda_k1"] = nrm((HEAD_DIM,), 0.1)
    inp["l0_lambda_q2"] = nrm((HEAD_DIM,), 0.1)
    inp["l0_lambda_k2"] = nrm((HEAD_DIM,), 0.1)
    inp["l0_diff_subln"] = gain(DIFF_V_DIM)
    inp["l0_peer_wq"] = nrm((D, PEER_HEADS * 2 * PEER_KEY_DIM), D ** -0.5)
    inp["l0_peer_keys"] = nrm((PEER_HEADS, 2, PEER_N_KEYS, PEER_KEY_DIM), PEER_KEY_DIM ** -0.5)
    inp["l0_peer_u"] = nrm((PEER_N_EXPERTS, D), D ** -0.5)
    inp["l0_peer_v"] = nrm((PEER_N_EXPERTS, D), 0.5)
    inp["l1_ada_w"] = nrm((D, N_MOD * D), D ** -0.5)
    inp["l1_ada_b"] = nrm((N_MOD * D,), 0.02)
    inp["l1_norm1"] = gain(D)
    inp["l1_norm2"] = gain(D)
    inp["l1_w_in"] = nrm((D, sum(ODD_IN_SIZES)), D ** -0.5)
    inp["l1_w_out"] = nrm((ODD_OUT, D), ODD_OUT ** -0.5)
    inp["l1_gqa_qnorm"] = gain(HEAD_DIM)
    inp["l1_gqa_knorm"] = gain(HEAD_DIM)
    inp["l1_na_qnorm"] = gain(HEAD_DIM)
    inp["l1_na_knorm"] = gain(HEAD_DIM)
    inp["l1_na_rpb"] = nrm((NA_HEADS, 2 * NA_WIN_ROWS - 1, 2 * NA_WIN_COLS - 1), 0.1)
    inp["l1_peer_wq"] = nrm((D, PEER_HEADS * 2 * PEER_KEY_DIM), D ** -0.5)
    inp["l1_peer_keys"] = nrm((PEER_HEADS, 2, PEER_N_KEYS, PEER_KEY_DIM), PEER_KEY_DIM ** -0.5)
    inp["l1_peer_u"] = nrm((PEER_N_EXPERTS, D), D ** -0.5)
    inp["l1_peer_v"] = nrm((PEER_N_EXPERTS, D), 0.5)
    return inp

def reference(x, c, ctx, c_ctx,
              l0_ada_w, l0_ada_b, l0_norm1, l0_norm2, l0_w_in, l0_w_out, l0_pool_w, l0_pool_scale,
              l0_diff_qnorm, l0_diff_knorm, l0_lambda_q1, l0_lambda_k1, l0_lambda_q2, l0_lambda_k2,
              l0_diff_subln, l0_peer_wq, l0_peer_keys, l0_peer_u, l0_peer_v,
              l1_ada_w, l1_ada_b, l1_norm1, l1_norm2, l1_w_in, l1_w_out, l1_gqa_qnorm, l1_gqa_knorm,
              l1_na_qnorm, l1_na_knorm, l1_na_rpb, l1_peer_wq, l1_peer_keys, l1_peer_u, l1_peer_v):
    T = x.shape[1]
    cos, sin = axial_rope_tables(T)
    layers = [
        dict(ada_w=l0_ada_w, ada_b=l0_ada_b, norm1=l0_norm1, norm2=l0_norm2, w_in=l0_w_in, w_out=l0_w_out,
             mix=(l0_pool_w, l0_pool_scale, l0_diff_qnorm, l0_diff_knorm, l0_lambda_q1, l0_lambda_k1,
                  l0_lambda_q2, l0_lambda_k2, l0_diff_subln),
             peer=(l0_peer_wq, l0_peer_keys, l0_peer_u, l0_peer_v)),
        dict(ada_w=l1_ada_w, ada_b=l1_ada_b, norm1=l1_norm1, norm2=l1_norm2, w_in=l1_w_in, w_out=l1_w_out,
             mix=(l1_gqa_qnorm, l1_gqa_knorm, l1_na_qnorm, l1_na_knorm, l1_na_rpb),
             peer=(l1_peer_wq, l1_peer_keys, l1_peer_u, l1_peer_v)),
    ]
    xc = ctx
    for i in range(DEPTH):
        lp = layers[i]
        need_ctx = i < DEPTH - 1
        sh1, sc1, g1, sh2, sc2, g2 = modulation(c, lp["ada_w"], lp["ada_b"])
        csh1, csc1, cg1, csh2, csc2, cg2 = modulation(c_ctx[None], lp["ada_w"], lp["ada_b"])
        p_lat = modulate(x, lp["norm1"], sh1, sc1) @ lp["w_in"]
        p_ctx = modulate(xc, lp["norm1"], csh1, csc1) @ lp["w_in"]
        if i % 2 == 0:
            y, yc = mixer_pool_diff(p_lat, p_ctx, cos, sin, 0.8 - 0.6 * math.exp(-0.3 * i), *lp["mix"], need_ctx)
        else:
            y, yc = mixer_gqa_na(p_lat, p_ctx, cos, sin, *lp["mix"], need_ctx)
        x = x + g1[:, None] * (y @ lp["w_out"])
        x = x + g2[:, None] * peer_ffn(modulate(x, lp["norm2"], sh2, sc2), *lp["peer"])
        if need_ctx:
            xc = xc + cg1[:, None] * (yc @ lp["w_out"])
            xc = xc + cg2[:, None] * peer_ffn(modulate(xc, lp["norm2"], csh2, csc2), *lp["peer"])
    return x


_drawn_inputs = setup_inputs


def setup_inputs(seed=0):
    import zlib

    import numpy as np

    out = dict(_drawn_inputs(seed))
    spreads = {}
    factors = {'l0_lambda_q1': 4.345,
     'l1_gqa_qnorm': 4.199,
     'l1_gqa_knorm': 3.291,
     'l1_na_qnorm': 4.633,
     'l1_na_knorm': 3.968,
     'l1_na_rpb': 6.823}
    for name, (base, spread) in spreads.items():
        noise = np.random.default_rng([zlib.crc32(name.encode()), seed]).standard_normal(out[name].shape)
        drawn = base * np.exp(spread * noise) if base else spread * noise
        out[name] = __import__('jax').numpy.asarray(drawn.astype(out[name].dtype))
    for name, factor in factors.items():
        out[name] = (out[name] * factor).astype(out[name].dtype)
    return out
```

```python
from contextlib import ExitStack

import numpy as np

import concourse.bass as bass
from concourse import mybir

F32 = mybir.dt.float32
F32R = mybir.dt.float32r
U32 = mybir.dt.uint32
ALU = mybir.AluOpType
ACT = mybir.ActivationFunctionType
AX_X = mybir.AxisListType.X
ds = bass.ds

P = 128
D = 1024
KT = D // P
NCTX, NLAT = 256, 256
NT = NCTX + NLAT
HD = 64
EPS = 1e-6
LAM_INIT = 0.2
HEADS = 8
KEYS = 128
TOPK = 16
NEG = -3.0e38

CW = 256
CHUNK = KT * CW
RAW = 4
ADA_CH = 6 * D // CW
IN_CH = (10, 9)
OUT_CH = D // CW
WQ_CH = HEADS
PEER_CH = 128
GROUPS = PEER_CH // 2

PARTS = [("ada", 0, ADA_CH), ("in", 0, IN_CH[0]), ("out", 0, OUT_CH), ("wq", 0, WQ_CH), ("ada", 1, ADA_CH),
         ("peer", 0, PEER_CH), ("in", 1, IN_CH[1]), ("out", 1, OUT_CH), ("wq", 1, WQ_CH), ("peer", 1, PEER_CH)]
N0, M0, KIND = {}, {}, []
_m = 0
for _what, _l, _k in PARTS:
    N0[_what, _l], M0[_what, _l] = len(KIND), _m
    KIND += [(_what, _l, _j) for _j in range(_k)]
    _m += 0 if _what == "ada" else _k
N_CHUNKS = len(KIND)
N_OF_M = [n for n, k in enumerate(KIND) if k[0] != "ada"]

SMALL_SIZES = [("c", KT * 2), ("ada_b", 2 * 48), ("norm", 4 * KT), ("gain", 6), ("subln", 1), ("pscale", 2),
               ("poolw", 2 * HD), ("lam", 4), ("ident", P), ("blockones", P), ("rotT", P), ("iota", P),
               ("ones", P), ("namask", 64), ("eps", 2)]
SMALL, _at = {}, 0
for _n, _w in SMALL_SIZES:
    SMALL[_n] = (_at, _at + _w)
    _at += _w
SMALL_W = _at

ARENA = 18432
A_Q, A_K0, A_V0, A_U, A_YP = 0, 3072, 6144, 9216, 10240
A_K1, A_V1, A_BIAS = 2048, 4608, 7168
A_CS, A_TMP, A_POOLM = 11264, 11776, 15872
A_QJ, A_KEYS, A_REP, A_CAND, A_CREP, A_EQ = 0, 1024, 3072, 3584, 4608, 5632
A_SMALL, A_IDXG, A_IDXT = 7680, 8704, 10240
A_WCH, A_ONEHOT, A_CUR = 0, 11776, 13824
A_WG, A_GE, A_PT, A_ACC = 0, 4096, 5120, 14336
TL = 32
NA_COLS, GRID_W = 16, 64

TILES = {
    0: [("q", True, 0, False)] * 6 + [("k", True, 1, False)] * 6,
    1: [("q", True, 2, True)] * 4 + [("q", False, 4, True)] * 4 + [("k", True, 3, False)] + [("k", False, 5, False)] * 4,
}
VUNITS = {
    0: [(6, 0, 256, 0, False), (7, 0, 256, 256, False), (8, 0, 256, 512, False), (9, 0, 256, 0, True)],
    1: [(6, 128, 128, 0, False), (7, 0, 256, 128, False), (8, 0, 256, 384, False)],
}


UNITS, DONE = {}, {}
_post = _v = 0
for _l in range(2):
    for _c in range(IN_CH[_l]):
        _units = [("t", _j) for _j in (2 * _c, 2 * _c + 1) if _j < len(TILES[_l])]
        _units += [("v", _j) for _j, _u in enumerate(VUNITS[_l]) if _u[0] == _c]
        UNITS[_l, _c] = _units
        for _w, _j in _units:
            for _tt in range(1 if _w == "t" else 4):
                if (_w, _j) == _units[-1] and _tt == (0 if _w == "t" else 3):
                    DONE[_l, _w, _j, _tt] = ("split_used", M0["in", _l] + _c + 1)
                elif _w == "t":
                    _post += 1
                    DONE[_l, _w, _j, _tt] = ("post_in", _post)
                else:
                    _v += 1
                    DONE[_l, _w, _j, _tt] = ("v_in", _v)


class Steps:

    def __init__(self, sem):
        self.sem, self.n = sem, 0

    def inc(self):
        self.n += 1
        return self.sem, 1

    def restart(self):
        self.n = 0


def backbone(nc, xT, small, stream, poolm, cs, bias, keys, out):
    with ExitStack() as ctx:
        def sb(name, shape, dt=F32):
            return ctx.enter_context(nc.sbuf_tensor(name, shape, dt))

        sems = {}

        def sem(name):
            if name not in sems:
                sems[name] = ctx.enter_context(nc.semaphore(name))
            return sems[name]

        wdram = nc.dram_tensor("gate_matrix", (P, NT // TL, KEYS, TL), F32, kind="Internal").ap()

        x = sb("x", [P, KT, NT])
        h_hi = sb("h_hi", [P, KT, NT], F32R)
        h_lo = sb("h_lo", [P, KT, NT], F32R)
        raw = sb("raw", [P, RAW, CHUNK])
        w_hi = sb("w_hi", [P, 2, CHUNK], F32R)
        w_lo = sb("w_lo", [P, 2, CHUNK], F32R)
        p_hi = sb("p_hi", [P, 4, NT], F32R)
        p_lo = sb("p_lo", [P, 4, NT], F32R)
        sm = sb("sm", [P, SMALL_W])
        mod = sb("mod", [P, 2, 48, 2])
        gainmod = sb("gainmod", [P, 4, KT, 2])
        silu_c = sb("silu_c", [P, KT, 2])
        lamv = sb("lamv", [P, 8])
        sub8 = sb("sub8", [P, 1])
        stats = sb("stats", [P, 2, 8])
        gate = sb("gate", [P, 1])
        arena = sb("arena", [P, ARENA])
        bank = [ctx.enter_context(nc.psum_tensor(f"bank{i}", [P, 512], F32)) for i in range(8)]

        def view(at, *shape):
            n = int(np.prod(shape))
            v = arena[:, at:at + n]
            if len(shape) == 2:
                v = v.rearrange("p (a b) -> p a b", a=shape[0])
            elif len(shape) == 3:
                v = v.rearrange("p (a b c) -> p a b c", a=shape[0], b=shape[1])
            return v

        def small_of(name, a=0, b=None):
            lo, hi = SMALL[name]
            return sm[:, lo + a:(hi if b is None else lo + b)]

        ident, blockones, rotT, iota, ones = (small_of(n) for n in ("ident", "blockones", "rotT", "iota", "ones"))
        c_in = small_of("c").rearrange("p (a s) -> p a s", s=2)
        rw = [raw[:, s, :].rearrange("p (k n) -> p k n", k=KT) for s in range(RAW)]
        wsplit = [(w_hi[:, s, :], w_lo[:, s, :]) for s in range(2)]
        wk = [tuple(w.rearrange("p (k n) -> p k n", k=KT) for w in pair) for pair in wsplit]

        tmp = [view(A_TMP + 512 * i, 512) for i in range(8)]
        sq, qg, std = tmp[0:2], tmp[2:4], tmp[4:6]
        t1, t2 = [tmp[6][:, 0:256], tmp[6][:, 256:512]], [tmp[7][:, 0:256], tmp[7][:, 256:512]]
        cos_sin = view(A_CS, 2, NLAT)
        q_of = {0: view(A_Q, 6, NT), 1: view(A_Q, 8, NLAT)}
        k_of = {0: view(A_K0, 6, NT), 1: view(A_K1, 5, NT)}
        v_of = {0: view(A_V0, 4, 768), 1: view(A_V1, 4, 640)}
        u_tok, y_pool, pool_m = view(A_U, 4, 256), view(A_YP, 2, NT), view(A_POOLM, 4, 2, 256)
        na_bias = view(A_BIAS, 16, 256)

        STREAMS = ((0, NCTX, NT), (1, 0, NCTX))

        def streams(c0):
            return [s for s in STREAMS if s[1] >= c0]

        def first_col(l, peer):
            return NCTX if l == 1 else 0

        def chunk_ready(eng, n, i=0):
            eng.wait_ge(sem(f"raw_ready{n % RAW}"), i * 16 + 16 * (n // RAW + 1))

        def split_hi(act, m, i=0, per=0):
            chunk_ready(act, N_OF_M[m], i * (per // RAW))
            if m >= 2:
                act.wait_ge(sem("split_used"), i * per + (m - 1))
            act.activation(w_hi[:, m % 2, :], raw[:, N_OF_M[m] % RAW, :], ACT.Copy).then_inc(sem("hi_done"), 1)

        def split_lo(dve, m, i=0, per=0):
            dve.wait_ge(sem("hi_done"), i * per + (m + 1))
            dve.tensor_tensor(w_lo[:, m % 2, :], raw[:, N_OF_M[m] % RAW, :], w_hi[:, m % 2, :],
                              ALU.subtract).then_inc(sem("lo_done"), 1)

        def split_ready(pe, m, i=0, per=0):
            pe.wait_ge(sem("lo_done"), i * per + (m + 1))

        def mm3(pe, dst, pairs):
            last = None
            for k, ((ah, al), (bh, bl)) in enumerate(pairs):
                pe.matmul(dst, ah, bh, start=(k == 0), stop=False)
                pe.matmul(dst, al, bh, start=False, stop=False)
                last = pe.matmul(dst, ah, bl, start=False, stop=(k == len(pairs) - 1))
            return last

        def feature_tile(pe, dst, slot, col, c0):
            return mm3(pe, dst, [((wk[slot][0][:, k, col:col + P], wk[slot][1][:, k, col:col + P]),
                                  (h_hi[:, k, c0:NT], h_lo[:, k, c0:NT])) for k in range(KT)])

        def mixer_out(l, kt):
            if l == 1:
                return q_of[1][:, kt, :]
            return y_pool[:, kt, :] if kt < 2 else q_of[0][:, kt - 2, :]

        def attention_units(l):
            if l == 0:
                return [(h, c, NT if c >= NCTX else NCTX, h, (P * h,), None)
                        for h in range(6) for c in (NCTX, NCTX + P, 0, P)]
            units = [(j, c, NT, 0, (0, HD), None) for j in range(4) for c in (0, P)]
            return units + [(4 + j, P * b, NT, 1 + j, (P + P * j, P + P * j + HD), (4 * j + b, 4 * j + 2 + b))
                            for j in range(4) for b in range(2)]

        def nh_count(q, kt):
            per = [2, 2, 2, 1]
            return KT * sum(per[:q]) + per[q] * (kt + 1)

        block = ctx.enter_context(nc.Block())

        @block.sync
        def _(sp):
            def raw_free(n, i=0, per=0):
                what, l, j = KIND[n - RAW]
                if what == "ada":
                    sp.wait_ge(sem("ada_used"), i * per + (ADA_CH * l + j + 1))
                else:
                    sp.wait_ge(sem("lo_done"), i * per + (M0[what, l] + j + 1))

            def load(n, i=0, per=0):
                if n >= RAW:
                    raw_free(n, i, per)
                src = stream[n] if isinstance(i, int) else stream[ds(i * per + n, 1)].rearrange("a p n -> (a p) n")
                sp.dma_start(raw[:, n % RAW, :], src).then_inc(sem(f"raw_ready{n % RAW}"), 16)

            sp.dma_start(sm[:], small).then_inc(sem("small_in"), 16)
            for n in range(RAW):
                load(n)
            sp.dma_start(x[:], xT).then_inc(sem("x_in"), 16)
            sp.dma_start(view(A_CS, 2 * NLAT), cs).then_inc(sem("cs_in0"), 16)
            sp.dma_start(view(A_POOLM, 2048), poolm).then_inc(sem("poolm_in"), 16)
            with sp.Fori(0, ADA_CH // RAW - 1) as i:
                for k in range(RAW):
                    load(RAW + k, i, RAW)
            for n in range(ADA_CH, N0["ada", 1] + RAW):
                load(n)
            with sp.Fori(0, ADA_CH // RAW - 1) as i:
                for k in range(RAW):
                    load(N0["ada", 1] + RAW + k, i, RAW)

            def peer(l):
                n0 = N0["peer", l]
                tokens = NT - first_col(l, True)
                for n in range(n0, n0 + RAW):
                    load(n)
                with sp.Fori(0, tokens // (2 * TL)) as i:
                    for c in range(2):
                        sp.wait_ge(sem(f"w_evac{l}"), i * 16 + (4 + 8 * c + 8))
                        sp.dma_start(wdram[:, ds(i * 2 + c, 1)].rearrange("p a b c -> p (a b c)"),
                                     view(A_WCH + 4096 * c, 4096)).then_inc(sem(f"w_out{l}_{c}"), 16)
                load(n0 + RAW)
                for c in range(2):
                    sp.wait_ge(sem(f"w_out{l}_{c}"), 16 + 16 * (tokens // (2 * TL)))

                def gates(w, b):
                    ntc = tokens // TL
                    sp.dma_start(view(A_WG + 2048 * b, 16, 4 * TL)[:, 0:ntc, :],
                                 wdram[:, 0:ntc, ds(w * 4, 4), :].rearrange("p a b c -> p a (b c)"))\
                      .then_inc(sem(f"w_in{l}_{b}"), 16)

                gates(0, 0)
                gates(1, 1)
                with sp.Fori(0, GROUPS // 4 - 1) as i:
                    for half in range(2):
                        for k in range(4):
                            load(n0 + RAW + 1 + 4 * half + k, i, 8)
                        sp.wait_ge(sem(f"pm_done{l}"), i * 8 + (2 + 4 * half + 4))
                        gates(i * 2 + (2 + half), half)
                for n in range(n0 + PEER_CH - 3, n0 + PEER_CH):
                    load(n)

            peer(0)
            for n in range(N0["in", 1], N0["peer", 1]):
                load(n)
            peer(1)
            sp.wait_ge(sem("x_done"), 2)
            sp.dma_start(out, x[:, :, NCTX:NT]).then_inc(sem("out_done"), 16)
            sp.wait_ge(sem("out_done"), 16)

        @block.tensor
        def _(pe):
            def ada(l):
                n0 = N0["ada", l]
                dst = bank[7]
                pe.wait_ge(sem("silu_done"), 1)
                with pe.Fori(0, ADA_CH // RAW) as i:
                    for k in range(RAW):
                        chunk_ready(pe, n0 + k, i)
                        for half in range(2):
                            for kt in range(KT):
                                last = pe.matmul(dst[:, ds(i * 16 + 4 * k + 2 * half, 2)],
                                                 rw[(n0 + k) % RAW][:, kt, half * P:half * P + P], silu_c[:, kt, :],
                                                 start=(kt == 0), stop=(kt == KT - 1))
                        last.then_inc(sem("ada_used"), 1)

            def norm(q):
                c0 = 0 if q < 3 else NCTX
                pe.wait_ge(sem("mod_done"), q // 2 + 1)
                for kt in range(KT):
                    pe.wait_ge(sem("nsq"), KT * q + kt + 1)
                    pe.matmul(bank[7][:, c0:NT], ones, sq[kt % 2][:, c0:NT], start=(kt == 0),
                              stop=(kt == KT - 1)).then_inc(sem("nsq_used"), 1)

            def project(l):
                m0 = M0["in", l]
                pe.wait_ge(sem("nlo"), KT * (2 * l + 1))
                tiles, vunits = TILES[l], VUNITS[l]
                nt = len(tiles)

                def heads_stats(j):
                    kind, rope, _, lat = tiles[j]
                    g, b, c0 = 13 * l + j - l, j % 2, NCTX if lat else 0
                    pe.wait_ge(sem("post_sq"), g + 1)
                    if j >= 2:
                        pe.wait_ge(sem("post_std"), g - 1)
                    pe.matmul(bank[2 + b][:, c0:NT], blockones, sq[b][:, c0:NT], start=True,
                              stop=True).then_inc(sem("post_ss"), 1)
                    pe.wait_ge(sem("post_qg"), g + 1)
                    if j >= 2:
                        pe.wait_ge(sem("post_done"), g - 1)
                    pe.matmul(bank[4 + b][:, 0:NLAT], rotT, qg[b][:, NCTX:NT], start=True,
                              stop=True).then_inc(sem("post_rot"), 1)

                for c in range(IN_CH[l]):
                    m = m0 + c
                    split_ready(pe, m)
                    for what, j in UNITS[l, c]:
                        if what == "t":
                            g = 13 * l + j - l
                            if j >= 2:
                                pe.wait_ge(sem("post_qg"), g - 1)
                            c0 = NCTX if tiles[j][3] else 0
                            last = feature_tile(pe, bank[j % 2][:, c0:NT], m % 2, P * (j % 2), c0)
                            last.then_inc(sem(DONE[l, "t", j, 0][0]), 1)
                            if j >= 1:
                                heads_stats(j - 1)
                        else:
                            _, col, width, _, _ = vunits[j]
                            if j == 0:
                                heads_stats(nt - 1)
                            for tt in range(4):
                                e = 16 * l + 4 * j + tt
                                if 4 * j + tt >= 2:
                                    pe.wait_ge(sem("v_evac"), e - 1)
                                tok = slice(P * tt, P * tt + P)
                                last = mm3(pe, bank[6 + tt % 2][:, 0:width],
                                           [((h_hi[:, k, tok], h_lo[:, k, tok]),
                                             (wk[m % 2][0][:, k, col:col + width], wk[m % 2][1][:, k, col:col + width]))
                                            for k in range(KT)])
                                last.then_inc(sem(DONE[l, "v", j, tt][0]), 1)

            def pool():
                pe.wait_ge(sem("v_evac"), 16)
                pe.wait_ge(sem("poolm_in"), 16)
                for pr in range(2):
                    for gi in range(2):
                        for s in range(2):
                            for tt in range(2):
                                last = pe.matmul(bank[6 + pr][HD * gi:HD * gi + HD, 256 * s:256 * s + 256],
                                                 u_tok[:, 2 * s + tt, (2 * pr + gi) * HD:(2 * pr + gi + 1) * HD],
                                                 pool_m[:, 2 * pr + gi, tt, :], start=(tt == 0), stop=(tt == 1))
                    last.then_inc(sem("pool_mean"), 1)
                poolw = small_of("poolw").rearrange("p (a b) -> p a b", a=2)
                pe.wait_ge(sem("post_done"), 12)
                for pr in range(2):
                    pe.wait_ge(sem("pool_evac"), pr + 1)
                    for gi in range(2):
                        rows = slice(HD * gi, HD * gi + HD)
                        last = pe.matmul(bank[4 + pr][rows, :], poolw[rows, pr, :], y_pool[rows, pr, :],
                                         start=True, stop=True)
                    last.then_inc(sem("pool_y"), 1)

            def attention(l):
                units, base = attention_units(l), 32 * l - 8 * l
                pe.wait_ge(sem("post_done"), 12 + 13 * l)
                pe.wait_ge(sem("v_evac"), 16 + 12 * l)
                if l == 0:
                    pe.wait_ge(sem("pool_evac"), 4)
                qv, kv, vv = q_of[l], k_of[l], v_of[l]

                def scores(u):
                    j, qc, nk, kj, _, _ = units[u]
                    if u >= 2:
                        pe.wait_ge(sem("exp_done"), 2 * (base + u - 1))
                    for i in range(2):
                        rows = slice(HD * i, HD * i + HD)
                        pe.matmul(bank[2 * (u % 2) + i][:, 0:nk], qv[rows, j, qc:qc + P], kv[rows, kj, 0:nk],
                                  start=True, stop=True).then_inc(sem("scores_done"), 1)

                def turn(u):
                    nk = units[u][2]
                    pe.wait_ge(sem("probs_done"), base + u + 1)
                    if u >= (2 if l == 0 else 1):
                        pe.wait_ge(sem("turned_evac"), base + u - 1 if l == 0 else base + u)
                    for i in range(1 + l):
                        for kb in range(nk // P):
                            dst = bank[4 + (u % 2 if l == 0 else i)][:, kb * P:kb * P + P]
                            last = pe.transpose(dst, tmp[2 * (u % 2) + i][:, kb * P:kb * P + P], ident)
                    last.then_inc(sem("turned"), 1)

                def values(u):
                    nk, cols = units[u][2], units[u][4]
                    pe.wait_ge(sem("turned_evac"), base + u + 1)
                    if u >= 2:
                        pe.wait_ge(sem("heads_evac"), base + u - 1)
                    wt = view(A_TMP + 2048 + 1024 * (u % 2), 2, 4, P)
                    for i in range(1 + l):
                        width = P if l == 0 else HD
                        for kb in range(nk // P):
                            last = pe.matmul(bank[6 + u % 2][width * i * l:width * i * l + width, 0:P],
                                             vv[:, kb, cols[i]:cols[i] + width], wt[:, i, kb, :],
                                             start=(kb == 0), stop=(kb == nk // P - 1))
                    last.then_inc(sem("heads_done"), 1)

                scores(0)
                for u in range(len(units)):
                    if u + 1 < len(units):
                        scores(u + 1)
                    turn(u)
                    if u:
                        values(u - 1)
                values(len(units) - 1)

            def subln():
                for h in range(6):
                    pe.wait_ge(sem("sub_sq"), h + 1)
                    if h >= 2:
                        pe.wait_ge(sem("sub_std"), h - 1)
                    pe.matmul(bank[h % 2][:], ones, sq[h % 2], start=True, stop=True).then_inc(sem("sub_ss"), 1)

            def project_out(l):
                c0 = first_col(l, True)
                pe.wait_ge(sem("ylo"), KT * (l + 1))
                for c in range(OUT_CH):
                    m = M0["out", l] + c
                    split_ready(pe, m)
                    for jj in range(2):
                        dt = 2 * c + jj
                        if dt >= 2:
                            pe.wait_ge(sem("out_evac"), KT * l + dt - 1)
                        last = feature_tile(pe, bank[dt % 2][:, c0:NT], m % 2, P * jj, c0)
                        last.then_inc(sem("split_used" if jj else "out_in"), 1)

            def choose(l):
                c0 = first_col(l, True)
                tokens = NT - c0
                m0, qj = M0["wq", l], view(A_QJ, 2, NT)
                kv = view(A_KEYS, 16, KEYS)
                pe.wait_ge(sem("nlo"), KT * (2 * l + 2))
                pe.wait_ge(sem(f"keys_in{l}"), 16)
                pe.sem_inc(sem(f"sc_done{l}"), 2)
                with pe.Fori(0, 2) as i:
                    def query(j):
                        if j % 2 == 0:
                            split_ready(pe, m0 + j // 2, i, 4)
                        pe.wait_ge(sem(f"qj_done{l}"), i * 8 + (j + 1))
                        last = feature_tile(pe, bank[j % 2][:, 0:tokens], (m0 + j // 2) % 2, P * (j % 2), c0)
                        last.then_inc(sem("split_used" if j % 2 else f"qj_in{l}"), 1)

                    def score(j):
                        pe.wait_ge(sem(f"qj_done{l}"), i * 8 + (j + 3))
                        pe.wait_ge(sem(f"sc_free{l}"), i * 8 + (j + 1))
                        for tt in range(tokens // P):
                            last = pe.matmul(bank[2 + j % 2][:, tt * P:tt * P + P], qj[:, j % 2, tt * P:tt * P + P],
                                             kv[:, ds(i * 8 + j, 1), :].rearrange("p a b -> p (a b)"),
                                             start=True, stop=True)
                        last.then_inc(sem(f"sc_done{l}"), 1)

                    query(0)
                    for j in range(1, 8):
                        query(j)
                        score(j - 1)
                    score(7)

            def turn_choices(l):
                ntt = (NT - first_col(l, True)) // P
                idxg = view(A_IDXG, 3, 4, P)
                pe.wait_ge(sem("chosen"), l + 1)
                for a in range(3):
                    for tt in range(ntt):
                        last = pe.transpose(bank[4 + a][:, tt * P:tt * P + P], idxg[:, a, tt, :], ident)
                    last.then_inc(sem("choices_turned"), 1)

            def build(l):
                tokens = NT - first_col(l, True)
                oh = view(A_ONEHOT, 4, 4, P)
                pe.sem_inc(sem(f"w_done{l}"), 2)
                with pe.Fori(0, tokens // (2 * TL)) as i:
                    for b in range(16):
                        pe.wait_ge(sem(f"onehots{l}"), i * 16 + (b + 2))
                        pe.wait_ge(sem(f"w_evac{l}"), i * 16 + (b + 1))
                        for t in range(4):
                            last = pe.matmul(bank[b % 4][:, t * P:t * P + P], oh[:, b % 2, t, :],
                                             oh[:, 2 + b % 2, t, :], start=True, stop=True)
                        last.then_inc(sem(f"w_done{l}"), 1)

            def experts(l):
                c0 = first_col(l, True)
                T = NT - c0
                m0 = M0["peer", l]

                pe.wait_ge(sem(f"w_evac{l}"), 4 + T // 4)

                def up(m, g, i, mi):
                    split_ready(pe, m, mi, 8)
                    for a in range(2):
                        e = 2 * g + a
                        pe.wait_ge(sem(f"ge_done{l}"), i * 8 + (e + 1))
                        last = feature_tile(pe, bank[e % 4][:, 0:T], m % 2, P * a, c0)
                        last.then_inc(sem("split_used" if a else f"h_done{l}"), 1)

                def down(m, g, i, mi):
                    split_ready(pe, m, mi, 8)
                    pe.wait_ge(sem(f"plo_done{l}"), i * 8 + (2 * g + 2 + 2))
                    hi, lo = wsplit[m % 2]
                    for dt in range(KT):
                        pe.wait_ge(sem(f"acc_done{l}"), i * 32 + (8 * g + dt + 1))
                        cols = [slice(D * a + P * dt, D * a + P * dt + P) for a in range(2)]
                        last = mm3(pe, bank[4 + dt % 4][:, 0:T],
                                   [((hi[:, cols[a]], lo[:, cols[a]]),
                                     (p_hi[:, (2 * g + a) % 4, 0:T], p_lo[:, (2 * g + a) % 4, 0:T])) for a in range(2)])
                        last.then_inc(sem(f"v_done{l}" if dt < KT - 1 else "split_used"), 1)

                up(m0, 0, 0, 0)
                with pe.Fori(0, GROUPS // 4 - 1) as i:
                    for g in range(4):
                        up(m0 + 1 + 2 * g, g + 1, i, i)
                        down(m0 + 2 + 2 * g, g, i, i)
                r = GROUPS // 4 - 1
                for g in range(4):
                    if g < 3:
                        up(m0 + 1 + 2 * g, g + 1, r, r)
                        down(m0 + 2 + 2 * g, g, r, r)
                    else:
                        down(m0 + PEER_CH - 1, 3, r, 0)

            pe.wait_ge(sem("small_in"), 16)
            pe.wait_ge(sem("lam_prod"), 1)
            pe.matmul(bank[6][:, 0:2], ones[0:HD, :], lamv[0:HD, 0:2], start=True, stop=True).then_inc(sem("lam_dot"), 1)
            ada(0)
            for l in range(2):
                norm(2 * l)
                project(l)
                if l == 0:
                    pool()
                attention(l)
                if l == 0:
                    subln()
                project_out(l)
                norm(2 * l + 1)
                choose(l)
                if l == 0:
                    ada(1)
                turn_choices(l)
                build(l)
                experts(l)

        @block.scalar
        def _(act):
            eps1, eps64 = small_of("eps", 0, 1), small_of("eps", 1, 2)

            def norm(q):
                c0, l, part = (0 if q < 3 else NCTX), q // 2, 3 * (q % 2)
                hh, rstd = tmp[5:7], tmp[2]
                for kt in range(KT):
                    if kt >= 2:
                        act.wait_ge(sem("nsq_used"), KT * q + kt - 1)
                    if q % 2:
                        act.wait_ge(sem("out_evac"), KT * l + kt + 1)
                    elif q == 2:
                        act.wait_ge(sem("x_done"), 1)
                    act.activation(sq[kt % 2][:, c0:NT], x[:, kt, c0:NT], ACT.Square).then_inc(sem("nsq"), 1)
                act.wait_ge(sem("nsq_used"), KT * (q + 1))
                act.activation(rstd[:, c0:NT], bank[7][:, c0:NT], ACT.Sqrt, bias=eps1,
                               scale=1.0 / D).then_inc(sem("nstd"), 1)
                for kt in range(KT):
                    act.wait_ge(sem("nt"), KT * q + kt + 1)
                    if kt >= 2:
                        act.wait_ge(sem("nlo"), KT * q + kt - 1)
                    for s, lo, hi in streams(c0):
                        act.activation(hh[kt % 2][:, lo:hi], tmp[3 + kt % 2][:, lo:hi], ACT.Identity,
                                       bias=mod[:, l, part * KT + kt, s:s + 1],
                                       scale=gainmod[:, q, kt, s:s + 1]).then_inc(sem("nh"), 1)
                    act.wait_ge(sem("nh"), nh_count(q, kt))
                    act.activation(h_hi[:, kt, c0:NT], hh[kt % 2][:, c0:NT], ACT.Copy).then_inc(sem("nhi"), 1)

            def project(l):
                tiles, vunits = TILES[l], VUNITS[l]
                nt = len(tiles)

                def deviation(j):
                    kind, _, _, lat = tiles[j]
                    g, b, c0 = 13 * l + j - l, j % 2, NCTX if lat else 0
                    act.wait_ge(sem("post_ss"), g + 1)
                    if j >= 2:
                        act.wait_ge(sem("post_done"), g - 1)
                    act.activation(std[b][:, c0:NT], bank[2 + b][:, c0:NT], ACT.Sqrt, bias=eps64 if kind == "q" else eps1,
                                   scale=1.0 if kind == "q" else 1.0 / HD).then_inc(sem("post_std"), 1)

                for c in range(IN_CH[l]):
                    split_hi(act, M0["in", l] + c + 1)
                    for what, j in UNITS[l, c]:
                        if what == "t":
                            _, _, gain, lat = tiles[j]
                            g, b, c0 = 13 * l + j - l, j % 2, NCTX if lat else 0
                            done, count = DONE[l, "t", j, 0]
                            act.wait_ge(sem(done), count)
                            if j >= 2:
                                act.wait_ge(sem("post_ss"), g - 1)
                            act.activation(sq[b][:, c0:NT], bank[b][:, c0:NT], ACT.Square).then_inc(sem("post_sq"), 1)
                            if j >= 2:
                                act.wait_ge(sem("post_done"), g - 1)
                                act.wait_ge(sem("post_rot"), g - 1)
                            act.activation(qg[b][:, c0:NT], bank[b][:, c0:NT], ACT.Identity,
                                           scale=small_of("gain", gain, gain + 1)).then_inc(sem("post_qg"), 1)
                            if j >= 1:
                                deviation(j - 1)
                        else:
                            _, _, width, at, is_pool = vunits[j]
                            if j == 0:
                                deviation(nt - 1)
                            for tt in range(4):
                                done, count = DONE[l, "v", j, tt]
                                act.wait_ge(sem(done), count)
                                dst = u_tok if is_pool else v_of[l]
                                act.activation(dst[:, tt, at:at + width], bank[6 + tt % 2][:, 0:width],
                                               ACT.Copy).then_inc(sem("v_evac"), 1)

            def pool():
                for pr in range(2):
                    act.wait_ge(sem("pool_mean"), pr + 1)
                    act.activation(y_pool[:, pr, :], bank[6 + pr][:], ACT.Copy).then_inc(sem("pool_evac"), 1)
                for pr in range(2):
                    act.wait_ge(sem("pool_y"), pr + 1)
                    act.activation(y_pool[:, pr, :], bank[4 + pr][:], ACT.Identity,
                                   scale=small_of("pscale", pr, pr + 1)).then_inc(sem("pool_evac"), 1)

            def attention(l):
                units, base = attention_units(l), 24 * l
                act.wait_ge(sem("post_done"), 12 + 13 * l)

                def exps(u):
                    nk, st = units[u][2], stats[:, u % 2, :]
                    if u >= 2:
                        act.wait_ge(sem("turned"), base + u - 1)
                    for i in range(2):
                        act.wait_ge(sem("max_done"), 2 * (base + u) + i + 1)
                        act.activation(tmp[2 * (u % 2) + i][:, 0:nk], bank[2 * (u % 2) + i][:, 0:nk], ACT.Exp,
                                       bias=st[:, i:i + 1], accum_out=st[:, 2 + i:3 + i]).then_inc(sem("exp_done"), 1)

                def evac(u):
                    nk = units[u][2]
                    act.wait_ge(sem("turned"), base + u + 1)
                    if u >= 2:
                        act.wait_ge(sem("heads_done"), base + u - 1)
                    for i in range(1 + l):
                        wt = view(A_TMP + 2048 + 1024 * (u % 2) + 512 * i, 512)
                        last = act.activation(wt[:, 0:nk], bank[4 + (u % 2 if l == 0 else i)][:, 0:nk], ACT.Copy)
                    last.then_inc(sem("turned_evac"), 1)

                exps(0)
                for u in range(len(units)):
                    if u + 1 < len(units):
                        exps(u + 1)
                    evac(u)

            def subln():
                def deviation(h):
                    act.wait_ge(sem("sub_ss"), h + 1)
                    if h >= 2:
                        act.wait_ge(sem("sub_done"), h - 1)
                    act.activation(std[h % 2], bank[h % 2][:], ACT.Sqrt, bias=eps1, scale=1.0 / P)\
                       .then_inc(sem("sub_std"), 1)

                act.wait_ge(sem("heads_evac"), 24)
                for h in range(6):
                    if h >= 2:
                        act.wait_ge(sem("sub_ss"), h - 1)
                    act.activation(sq[h % 2], q_of[0][:, h, :], ACT.Square).then_inc(sem("sub_sq"), 1)
                    if h:
                        deviation(h - 1)
                deviation(5)

            def mixed(l):
                c0 = first_col(l, True)
                for kt in range(KT):
                    if l == 0:
                        if kt >= 2:
                            act.wait_ge(sem("sub_done"), kt - 1)
                        else:
                            act.wait_ge(sem("pool_evac"), 4)
                    else:
                        act.wait_ge(sem("heads_evac"), 40)
                    act.activation(h_hi[:, kt, c0:NT], mixer_out(l, kt), ACT.Copy).then_inc(sem("yhi"), 1)

            def project_out(l):
                for c in range(OUT_CH - 1):
                    split_hi(act, M0["out", l] + c + 1)

            def choose(l):
                tokens = NT - first_col(l, True)
                m0, qj = M0["wq", l], view(A_QJ, 2, NT)
                act.sem_inc(sem(f"qj_done{l}"), 2)
                with act.Fori(0, 2) as i:
                    split_hi(act, m0, i, 4)
                    for h in range(4):
                        if h < 3:
                            split_hi(act, m0 + h + 1, i, 4)
                        for p in range(2):
                            j = 2 * h + p
                            if p:
                                act.wait_ge(sem("split_used"), i * 4 + (m0 + h + 1))
                            else:
                                act.wait_ge(sem(f"qj_in{l}"), i * 4 + (h + 1))
                            act.wait_ge(sem(f"sc_done{l}"), i * 8 + (j + 1))
                            act.activation(qj[:, p, 0:tokens], bank[p][:, 0:tokens], ACT.Copy)\
                               .then_inc(sem(f"qj_done{l}"), 1)
                        act.wait_ge(sem(f"gd_done{l}"), i * 4 + (h + 1))
                        gd = view(A_SMALL + 576, 64)
                        act.activation(gd[:, 0:tokens // P * TOPK], gd[:, 0:tokens // P * TOPK], ACT.Exp)\
                           .then_inc(sem(f"gexp_done{l}"), 1)

            def turn_choices(l):
                tokens = NT - first_col(l, True)
                idxt = view(A_IDXT, 3, NT)
                for a in range(3):
                    act.wait_ge(sem("choices_turned"), 3 * l + a + 1)
                    act.activation(idxt[:, a, 0:tokens], bank[4 + a][:, 0:tokens], ACT.Copy)\
                       .then_inc(sem("choices_evac"), 1)

            def build(l):
                tokens = NT - first_col(l, True)
                act.sem_inc(sem(f"w_evac{l}"), 4)
                for c in range(2):
                    act.sem_inc(sem(f"w_out{l}_{c}"), 16)
                with act.Fori(0, tokens // (2 * TL)) as i:
                    for b in range(16):
                        c = b // 8
                        if b % 8 == 0:
                            act.wait_ge(sem(f"w_out{l}_{c}"), i * 16 + 16)
                        act.wait_ge(sem(f"w_done{l}"), i * 16 + (b + 1 + 2))
                        piece = view(A_WCH + 4096 * c, KEYS, TL)[:, :, 4 * (b % 8):4 * (b % 8) + 4]
                        act.activation(piece.rearrange("p n t -> p t n"),
                                       bank[b % 4][:].rearrange("p (t n) -> p t n", t=4), ACT.Copy)\
                           .then_inc(sem(f"w_evac{l}"), 1)

            def experts(l):
                T = NT - first_col(l, True)
                m0 = M0["peer", l]
                ge, pt = view(A_GE, 2, NT), view(A_PT, 2, NT)
                act.sem_inc(sem(f"ge_done{l}"), 4)

                def gelu(e, i):
                    if e % 2:
                        act.wait_ge(sem("split_used"), i * 8 + (m0 + max(e - 2, 0) + 1))
                    else:
                        act.wait_ge(sem(f"h_done{l}"), i * 4 + (e // 2 + 1))
                    act.wait_ge(sem(f"pm_done{l}"), i * 8 + (e + 1))
                    act.activation(ge[:, e % 2, 0:T], bank[e % 4][:, 0:T], ACT.Gelu).then_inc(sem(f"ge_done{l}"), 1)
                    act.wait_ge(sem(f"pm_done{l}"), i * 8 + (e + 3))
                    act.wait_ge(sem("split_used"), i * 8 + (m0 - 1 + 2 * (e // 2)))
                    act.activation(p_hi[:, e % 4, 0:T], pt[:, e % 2, 0:T], ACT.Copy).then_inc(sem(f"phi_done{l}"), 1)

                def step(g, i):
                    split_hi(act, m0 + 2 + 2 * g, i, 8)
                    gelu(2 * g + 2, i)
                    split_hi(act, m0 + 3 + 2 * g, i, 8)
                    gelu(2 * g + 3, i)

                for c in range(2):
                    act.wait_ge(sem(f"w_out{l}_{c}"), 16 + 16 * (T // (2 * TL)))
                split_hi(act, m0)
                split_hi(act, m0 + 1)
                gelu(0, 0)
                gelu(1, 0)
                with act.Fori(0, GROUPS // 4 - 1) as i:
                    for g in range(4):
                        step(g, i)
                for g in range(3):
                    step(g, GROUPS // 4 - 1)
                if l == 0:
                    split_hi(act, M0["in", 1])

            act.wait_ge(sem("small_in"), 16)
            act.activation(silu_c[:], c_in, ACT.Silu).then_inc(sem("silu_done"), 1)
            act.wait_ge(sem("lam_dot"), 1)
            act.activation(lamv[:, 2:4], bank[6][:, 0:2], ACT.Exp).then_inc(sem("lam_exp"), 1)
            split_hi(act, 0)
            act.wait_ge(sem("x_in"), 16)
            for l in range(2):
                norm(2 * l)
                project(l)
                if l == 0:
                    pool()
                attention(l)
                if l == 0:
                    subln()
                mixed(l)
                project_out(l)
                norm(2 * l + 1)
                choose(l)
                turn_choices(l)
                build(l)
                experts(l)

        @block.vector
        def _(dve):
            st = Steps(sem("dve_step"))

            def settle():
                dve.wait_ge(st.sem, st.n)

            def modulation(l):
                dve.wait_ge(sem("ada_used"), ADA_CH * (l + 1))
                adab = small_of("ada_b", 48 * l, 48 * l + 48).rearrange("p (j s) -> p j s", s=1).broadcast_to([P, 48, 2])
                dve.tensor_tensor(mod[:, l], bank[7][:, 0:96].rearrange("p (j s) -> p j s", s=2), adab,
                                  ALU.add).then_inc(*st.inc())
                settle()
                for w in range(2):
                    g = small_of("norm", KT * (2 * l + w), KT * (2 * l + w) + KT)
                    g = g.rearrange("p (j s) -> p j s", s=1).broadcast_to([P, KT, 2])
                    part = 3 * w + 1
                    last = dve.scalar_tensor_tensor(gainmod[:, 2 * l + w], mod[:, l, part * KT:part * KT + KT, :], 1.0, g,
                                                    ALU.add, ALU.mult)
                last.then_inc(sem("mod_done"), 1)

            def norm(q):
                c0 = 0 if q < 3 else NCTX
                hh, rstd = tmp[5:7], tmp[2]
                dve.wait_ge(sem("nstd"), q + 1)
                dve.reciprocal(rstd[:, c0:NT], rstd[:, c0:NT]).then_inc(*st.inc())
                settle()

                def low(kt):
                    dve.wait_ge(sem("nhi"), KT * q + kt + 1)
                    dve.tensor_tensor(h_lo[:, kt, c0:NT], hh[kt % 2][:, c0:NT], h_hi[:, kt, c0:NT],
                                      ALU.subtract).then_inc(sem("nlo"), 1)

                for kt in range(KT):
                    if kt >= 2:
                        dve.wait_ge(sem("nh"), nh_count(q, kt - 2))
                    dve.tensor_tensor(tmp[3 + kt % 2][:, c0:NT], x[:, kt, c0:NT], rstd[:, c0:NT],
                                      ALU.mult).then_inc(sem("nt"), 1)
                    if kt:
                        low(kt - 1)
                low(KT - 1)

            def project(l):
                tiles, vunits = TILES[l], VUNITS[l]
                nt = len(tiles)
                dve.wait_ge(sem(f"cs_in{l}"), 16)

                def finish(j):
                    kind, rope, _, lat = tiles[j]
                    g, b, c0 = 13 * l + j - l, j % 2, NCTX if lat else 0
                    slot = sum(t[0] == kind for t in tiles[:j])
                    dst = (q_of if kind == "q" else k_of)[l][:, slot, :]
                    dlat = dst[:, 0:NLAT] if lat and l == 1 else dst[:, NCTX:NT]
                    dve.wait_ge(sem("post_std"), g + 1)
                    dve.reciprocal(std[b][:, c0:NT], std[b][:, c0:NT]).then_inc(*st.inc())
                    dve.wait_ge(sem("post_rot"), g + 1)
                    if rope:
                        dve.tensor_tensor(t1[b], qg[b][:, NCTX:NT], cos_sin[:, 0, :], ALU.mult).then_inc(*st.inc())
                        dve.tensor_tensor(t2[b], bank[4 + b][:, 0:NLAT], cos_sin[:, 1, :], ALU.mult).then_inc(*st.inc())
                        settle()
                        dve.tensor_tensor(t1[b], t1[b], t2[b], ALU.add).then_inc(*st.inc())
                        if not lat:
                            dve.tensor_tensor(dst[:, 0:NCTX], qg[b][:, 0:NCTX], std[b][:, 0:NCTX], ALU.mult)
                        settle()
                        dve.tensor_tensor(dlat, t1[b], std[b][:, NCTX:NT], ALU.mult).then_inc(sem("post_done"), 1)
                    else:
                        settle()
                        width = NT - c0
                        dve.tensor_tensor(dst[:, 0:width], qg[b][:, c0:NT], std[b][:, c0:NT],
                                          ALU.mult).then_inc(sem("post_done"), 1)

                for c in range(IN_CH[l]):
                    split_lo(dve, M0["in", l] + c + 1)
                    for j in (2 * c, 2 * c + 1):
                        if j < nt and j:
                            finish(j - 1)
                    if vunits[0][0] == c:
                        finish(nt - 1)

            def attention(l):
                units, base = attention_units(l), 24 * l
                if l == 1:
                    dve.wait_ge(sem("bias_in"), 16)
                    mask = small_of("namask").rearrange("p (a k) -> p a k", a=1).broadcast_to([P, 64, 64])
                    biasv = view(A_BIAS, 64, 64)
                    dve.tensor_tensor(biasv, biasv, mask, ALU.add).then_inc(*st.inc())
                    settle()

                def maxima(u):
                    nk, bj, stt = units[u][2], units[u][5], stats[:, u % 2, :]
                    for i in range(2):
                        dve.wait_ge(sem("scores_done"), 2 * (base + u) + i + 1)
                        s = bank[2 * (u % 2) + i]
                        if bj is not None:
                            dve.tensor_tensor(s[:, NCTX:NT], s[:, NCTX:NT], na_bias[:, bj[i], :],
                                              ALU.add).then_inc(*st.inc())
                            settle()
                        dve.tensor_reduce(stt[:, i:i + 1], s[:, 0:nk], AX_X, ALU.max, negate=True)\
                           .then_inc(sem("max_done"), 1)

                def probs(u):
                    nk, stt = units[u][2], stats[:, u % 2, :]
                    e = [tmp[2 * (u % 2) + i][:, 0:nk] for i in range(2)]
                    dve.wait_ge(sem("exp_done"), 2 * (base + u) + 2)
                    dve.reciprocal(stt[:, 4:6], stt[:, 2:4]).then_inc(*st.inc())
                    settle()
                    if l == 0:
                        dve.tensor_scalar(stt[:, 6:7], stt[:, 5:6], lamv[:, 4:5], None, ALU.mult).then_inc(*st.inc())
                        dve.tensor_scalar(e[0], e[0], stt[:, 4:5], None, ALU.mult).then_inc(*st.inc())
                        settle()
                        dve.scalar_tensor_tensor(e[0], e[1], stt[:, 6:7], e[0], ALU.mult, ALU.add)\
                           .then_inc(sem("probs_done"), 1)
                    else:
                        for i in range(2):
                            last = dve.tensor_scalar(e[i], e[i], stt[:, 4 + i:5 + i], None, ALU.mult)
                        last.then_inc(sem("probs_done"), 1)

                def heads(u):
                    j, qc = units[u][:2]
                    dve.wait_ge(sem("heads_done"), base + u + 1)
                    dve.tensor_copy(q_of[l][:, j, qc:qc + P], bank[6 + u % 2][:, 0:P]).then_inc(sem("heads_evac"), 1)

                maxima(0)
                for u in range(len(units)):
                    if u + 1 < len(units):
                        maxima(u + 1)
                    probs(u)
                    if u >= 2:
                        heads(u - 2)
                heads(len(units) - 2)
                heads(len(units) - 1)

            def subln():
                for h in range(6):
                    dve.wait_ge(sem("sub_std"), h + 1)
                    dve.reciprocal(std[h % 2], std[h % 2]).then_inc(*st.inc())
                    settle()
                    dve.scalar_tensor_tensor(q_of[0][:, h, :], q_of[0][:, h, :], sub8[:, 0:1], std[h % 2], ALU.mult,
                                             ALU.mult).then_inc(sem("sub_done"), 1)

            def mixed(l):
                c0 = first_col(l, True)
                for kt in range(KT):
                    dve.wait_ge(sem("yhi"), KT * l + kt + 1)
                    dve.tensor_tensor(h_lo[:, kt, c0:NT], mixer_out(l, kt), h_hi[:, kt, c0:NT],
                                      ALU.subtract).then_inc(sem("ylo"), 1)

            def residual(src, l, part, dt, c0):
                for s, lo, hi in streams(c0):
                    last = dve.scalar_tensor_tensor(x[:, dt, lo:hi], src(lo, hi),
                                                    mod[:, l, part * KT + dt, s:s + 1], x[:, dt, lo:hi], ALU.mult, ALU.add)
                return last

            def project_out(l):
                c0 = first_col(l, True)
                for c in range(OUT_CH):
                    if c + 1 < OUT_CH:
                        split_lo(dve, M0["out", l] + c + 1)
                    for dt in (2 * c, 2 * c + 1):
                        if dt % 2:
                            dve.wait_ge(sem("split_used"), M0["out", l] + c + 1)
                        else:
                            dve.wait_ge(sem("out_in"), 4 * l + c + 1)
                        residual(lambda lo, hi: bank[dt % 2][:, lo:hi], l, 2, dt, c0).then_inc(sem("out_evac"), 1)

            def choose(l):
                tokens = NT - first_col(l, True)
                ntt = tokens // P
                m0 = M0["wq", l]
                rep, cand, crep = view(A_REP, 4, KEYS), view(A_CAND, 4, 256), view(A_CREP, 4, 256)
                eq = [view(A_EQ + 1024 * a, 64, TOPK)[:, 0:ntt * TOPK, :] for a in range(2)]
                sv = view(A_SMALL, 4, 2, TOPK)
                si = view(A_SMALL + 128, 128).bitcast(U32).rearrange("p (t s k) -> p t s k", t=4, s=2)
                tv = view(A_SMALL + 256, 4, TOPK)
                tp = view(A_SMALL + 320, 64).bitcast(U32).rearrange("p (t k) -> p t k", t=4)
                pab = [view(A_SMALL + 384 + 64 * a, 64).bitcast(U32) for a in range(2)]
                gsum = view(A_SMALL + 512, 4)
                gd = view(A_SMALL + 576, 4, TOPK)[:, 0:ntt, :]
                idxg = view(A_IDXG, 3, 4, P)
                ts = Steps(sem(f"tk_step{l}"))

                def top16(src, again, vals, idxs, after_reads=None):
                    for tt in range(ntt):
                        dve.max(vals(tt)[:, 0:8], src(tt)).then_inc(*ts.inc())
                    dve.wait_ge(ts.sem, ts.n)
                    for tt in range(ntt):
                        dve.max_index(idxs(tt)[:, 0:8], vals(tt)[:, 0:8], src(tt)).then_inc(*ts.inc())
                        dve.match_replace(again(tt), vals(tt)[:, 0:8], src(tt), NEG).then_inc(*ts.inc())
                    dve.wait_ge(ts.sem, ts.n)
                    for tt in range(ntt):
                        last = dve.max(vals(tt)[:, 8:16], again(tt)).then_inc(*ts.inc())
                    if after_reads is not None:
                        dve.tensor_copy(gate[:], ones[:, 0:1]).then_inc(after_reads, 1)
                    dve.wait_ge(ts.sem, ts.n)
                    for tt in range(ntt):
                        dve.max_index(idxs(tt)[:, 8:16], vals(tt)[:, 8:16], again(tt)).then_inc(*ts.inc())

                dve.sem_inc(sem(f"sc_free{l}"), 2)
                with dve.Fori(0, 2) as i:
                    dve.sem_clear(ts.sem)
                    ts.restart()
                    split_lo(dve, m0, i, 4)
                    for h in range(4):
                        if h < 3:
                            split_lo(dve, m0 + h + 1, i, 4)
                        for p in range(2):
                            j = 2 * h + p
                            dve.wait_ge(sem(f"sc_done{l}"), i * 8 + (j + 1 + 2))
                            dve.tensor_copy(gate[:], ones[:, 0:1])
                            top16(lambda tt: bank[2 + p][:, tt * P:tt * P + P], lambda tt: rep[:, tt, :],
                                  lambda tt: sv[:, tt, p, :], lambda tt: si[:, tt, p, :], sem(f"sc_free{l}"))
                            dve.wait_ge(ts.sem, ts.n)
                        dve.tensor_tensor(cand[:, 0:ntt, :].rearrange("p t (a b) -> p t a b", a=TOPK),
                                          sv[:, 0:ntt, 0, :].rearrange("p t (a b) -> p t a b", b=1)
                                          .broadcast_to([P, ntt, TOPK, TOPK]),
                                          sv[:, 0:ntt, 1, :].rearrange("p t (a b) -> p t a b", a=1)
                                          .broadcast_to([P, ntt, TOPK, TOPK]), ALU.add).then_inc(*ts.inc())
                        dve.wait_ge(ts.sem, ts.n)
                        top16(lambda tt: cand[:, tt, :], lambda tt: crep[:, tt, :], lambda tt: tv[:, tt, :],
                              lambda tt: tp[:, tt, :])
                        dve.wait_ge(ts.sem, ts.n)
                        dve.tensor_tensor(gd, tv[:, 0:ntt, :], tv[:, 0:ntt, 0:1].broadcast_to([P, ntt, TOPK]),
                                          ALU.subtract).then_inc(sem(f"gd_done{l}"), 1)
                        tpf = tp[:, 0:ntt, :].rearrange("p t k -> p (t k)")
                        dve.tensor_scalar(pab[0][:, 0:ntt * TOPK], tpf, 4, None, ALU.logical_shift_right).then_inc(*ts.inc())
                        dve.tensor_scalar(pab[1][:, 0:ntt * TOPK], tpf, 15, None, ALU.bitwise_and).then_inc(*ts.inc())
                        dve.wait_ge(ts.sem, ts.n)
                        for a in range(2):
                            dve.tensor_tensor(eq[a], pab[a][:, 0:ntt * TOPK].rearrange("p (k a) -> p k a", a=1)
                                              .broadcast_to([P, ntt * TOPK, TOPK]),
                                              iota[:, 0:TOPK].rearrange("p (k a) -> p k a", k=1)
                                              .broadcast_to([P, ntt * TOPK, TOPK]), ALU.is_equal).then_inc(*ts.inc())
                        dve.wait_ge(ts.sem, ts.n)
                        for a in range(2):
                            e4 = eq[a].rearrange("p (t k) a -> p t k a", t=ntt)
                            dve.tensor_tensor(e4, e4, si[:, 0:ntt, a, :].rearrange("p t (k a) -> p t k a", k=1)
                                              .broadcast_to([P, ntt, TOPK, TOPK]), ALU.mult).then_inc(*ts.inc())
                        dve.wait_ge(ts.sem, ts.n)
                        col = ds(i * 64 + TOPK * h, TOPK)
                        for a in range(2):
                            dve.tensor_reduce(idxg[:, a, 0:ntt, col], eq[a].rearrange("p (t k) a -> p t k a", t=ntt),
                                              AX_X, ALU.add).then_inc(*ts.inc())
                        dve.wait_ge(sem(f"gexp_done{l}"), i * 4 + (h + 1))
                        dve.tensor_reduce(gsum[:, 0:ntt], gd, AX_X, ALU.add).then_inc(*ts.inc())
                        dve.wait_ge(ts.sem, ts.n)
                        dve.reciprocal(gsum[:, 0:ntt], gsum[:, 0:ntt]).then_inc(*ts.inc())
                        dve.wait_ge(ts.sem, ts.n)
                        dve.tensor_tensor(idxg[:, 2, 0:ntt, col], gd,
                                          gsum[:, 0:ntt].rearrange("p (t k) -> p t k", k=1)
                                          .broadcast_to([P, ntt, TOPK]), ALU.mult).then_inc(*ts.inc())
                        dve.wait_ge(ts.sem, ts.n)
                dve.tensor_copy(gate[:], ones[:, 0:1]).then_inc(sem("chosen"), 1)

            def build(l):
                tokens = NT - first_col(l, True)
                idxt, cur = view(A_IDXT, 3, NT), view(A_CUR, 3, 2 * TL)
                oh = view(A_ONEHOT, 4, 4, P)
                dve.wait_ge(sem("choices_evac"), 3 * (l + 1))
                bs = sem(f"cur_done{l}")
                dve.sem_inc(sem(f"onehots{l}"), 1)
                with dve.Fori(0, tokens // (2 * TL)) as i:
                    dve.wait_ge(sem(f"onehots{l}"), i * 16 + 1)
                    dve.tensor_copy(cur, idxt[:, :, ds(i * (2 * TL), 2 * TL)]).then_inc(bs, 1)
                    dve.wait_ge(bs, i + 1)
                    for b in range(16):
                        dve.wait_ge(sem(f"w_done{l}"), i * 16 + (b + 1))
                        for t in range(4):
                            tok = 4 * b + t
                            dve.tensor_scalar(oh[:, b % 2, t, :], iota, cur[:, 0, tok:tok + 1], None, ALU.is_equal)
                            last = dve.tensor_scalar(oh[:, 2 + b % 2, t, :], iota, cur[:, 1, tok:tok + 1],
                                                     cur[:, 2, tok:tok + 1], ALU.is_equal, ALU.mult)
                        last.then_inc(sem(f"onehots{l}"), 1)

            def experts(l):
                c0 = first_col(l, True)
                T = NT - c0
                m0, acc = M0["peer", l], view(A_ACC, KT, NT)
                done = sem(f"acc_done{l}")
                dve.memset(acc, 0.0).then_inc(done, 4)

                def add(g, i, dts, m):
                    for dt in dts:
                        if dt < KT - 1:
                            dve.wait_ge(sem(f"v_done{l}"), i * 28 + (7 * g + dt + 1))
                        else:
                            dve.wait_ge(sem("split_used"), i * 8 + (m + 1))
                        dve.tensor_tensor(acc[:, dt, 0:T], acc[:, dt, 0:T], bank[4 + dt % 4][:, 0:T],
                                          ALU.add).then_inc(done, 1)

                def step(g, i):
                    split_lo(dve, m0 + 2 + 2 * g, i, 8)
                    dve.wait_ge(done, i * 32 + (8 * g + 4))
                    add(g, i, range(2), m0 + 2 + 2 * g)
                    split_lo(dve, m0 + 3 + 2 * g, i, 8)
                    add(g, i, range(2, KT), m0 + 2 + 2 * g)

                split_lo(dve, m0)
                split_lo(dve, m0 + 1)
                with dve.Fori(0, GROUPS // 4 - 1) as i:
                    for g in range(4):
                        step(g, i)
                r = GROUPS // 4 - 1
                for g in range(3):
                    step(g, r)
                dve.wait_ge(done, 32 * r + 8 * 3 + 4)
                add(3, r, range(KT), m0 + 2 + 5)
                if l == 0:
                    split_lo(dve, M0["in", 1])
                dve.wait_ge(done, 32 * r + 32 + 4)
                for dt in range(KT):
                    last = residual(lambda lo, hi: acc[:, dt, lo - c0:hi - c0], l, 5, dt, c0)
                last.then_inc(sem("x_done"), 1)

            dve.wait_ge(sem("small_in"), 16)
            lam = small_of("lam")
            dve.tensor_tensor(lamv[0:HD, 0:2], lam[0:HD, 0:2], lam[0:HD, 2:4], ALU.mult).then_inc(sem("lam_prod"), 1)
            dve.tensor_scalar(sub8[:], small_of("subln"), 1.0 - LAM_INIT, None, ALU.mult).then_inc(*st.inc())
            dve.wait_ge(sem("lam_exp"), 1)
            dve.tensor_tensor(lamv[:, 5:6], lamv[:, 3:4], lamv[:, 2:3], ALU.subtract).then_inc(*st.inc())
            settle()
            dve.tensor_scalar(lamv[:, 4:5], lamv[:, 5:6], -LAM_INIT, None, ALU.add).then_inc(*st.inc())
            split_lo(dve, 0)
            modulation(0)
            dve.wait_ge(sem("x_in"), 16)
            for l in range(2):
                norm(2 * l)
                project(l)
                attention(l)
                if l == 0:
                    subln()
                mixed(l)
                project_out(l)
                norm(2 * l + 1)
                choose(l)
                if l == 0:
                    modulation(1)
                build(l)
                experts(l)

        @block.gpsimd
        def _(pool):
            def load_keys(l):
                pool.wait_ge(sem("ylo"), KT * (l + 1))
                pool.dma_start(view(A_KEYS, 2048), keys[l]).then_inc(sem(f"keys_in{l}"), 16)

            def experts(l):
                T = NT - first_col(l, True)
                ntc = T // TL
                ge, pt = view(A_GE, 2, NT), view(A_PT, 2, NT)
                pool.sem_inc(sem(f"pm_done{l}"), 2)
                pool.sem_inc(sem(f"plo_done{l}"), 2)

                def gated(e, i, wr):
                    w = e // 4
                    if e % 4 == 0:
                        pool.wait_ge(sem(f"w_in{l}_{w % 2}"), wr * 16 + 16 * (w // 2 + 1))
                    pool.wait_ge(sem(f"ge_done{l}"), i * 8 + (e + 5))
                    pool.wait_ge(sem(f"plo_done{l}"), i * 8 + (e + 1))
                    wg = view(A_WG + 2048 * (w % 2), 16, 4, TL)[:, 0:ntc, e % 4, :]
                    pool.tensor_tensor(pt[:, e % 2, 0:T].rearrange("p (a b) -> p a b", b=TL),
                                       ge[:, e % 2, 0:T].rearrange("p (a b) -> p a b", b=TL), wg,
                                       ALU.mult).then_inc(sem(f"pm_done{l}"), 1)
                    pool.wait_ge(sem(f"phi_done{l}"), i * 8 + (e + 1))
                    pool.tensor_tensor(p_lo[:, e % 4, 0:T], pt[:, e % 2, 0:T], p_hi[:, e % 4, 0:T],
                                       ALU.subtract).then_inc(sem(f"plo_done{l}"), 1)

                with pool.Fori(0, GROUPS // 4) as i:
                    for e in range(8):
                        gated(e, i, i)

            load_keys(0)
            for c in range(2):
                pool.wait_ge(sem(f"w_out0_{c}"), 16 + 16 * (NT // (2 * TL)))
            pool.dma_start(view(A_CS, 2 * NLAT), cs).then_inc(sem("cs_in1"), 16)
            pool.dma_start(view(A_BIAS, 4096), bias).then_inc(sem("bias_in"), 16)
            experts(0)
            load_keys(1)
            experts(1)


def constants():
    f = np.float32
    ident = np.eye(P, dtype=f)
    r = np.arange(P)
    blockones = (r[:, None] // HD == r[None, :] // HD).astype(f)
    rot = np.zeros((P, P), f)
    for m in range(P):
        if m % 32 < 16:
            rot[m, m + 16] = -1.0
        else:
            rot[m, m - 16] = 1.0
    t = np.arange(NLAT)
    inv = (f(10000.0) ** (-np.arange(16, dtype=f) / f(16))).astype(f)
    pos = np.where((r[:, None] % HD) // 32 == 0, t[None] // GRID_W, t[None] % GRID_W).astype(f)
    ang = (pos * inv[r % 16][:, None]).astype(f)
    cs = np.stack([np.cos(ang), np.sin(ang)], 1).astype(f).reshape(P, 2 * NLAT)
    poolm = np.zeros((4, 256, 256), f)
    for g, win in enumerate((2, 4, 8, 16)):
        for i in range(256):
            lo, hi = max(i - win // 2, 0), min(i + win // 2, 256)
            poolm[g, lo:hi, i] = f(1.0) / f(hi - lo)
            poolm[g, i, i] -= f(1.0)
    poolm = np.ascontiguousarray(poolm.reshape(4, 2, P, 256).transpose(2, 0, 1, 3)).reshape(P, 2048)
    qc, kc = np.arange(P)[:, None] % GRID_W, np.arange(GRID_W)[None]
    start = np.clip(qc - NA_COLS // 2, 0, GRID_W - NA_COLS)
    namask = np.where((kc >= start) & (kc < start + NA_COLS), 0.0, -1e30).astype(f)
    iota = np.broadcast_to(np.arange(P, dtype=f), (P, P))
    eps = np.broadcast_to(np.array([EPS, EPS * HD], f), (P, 2))
    return dict(ident=ident, blockones=blockones, rotT=rot.T, iota=iota, ones=np.ones((P, P), f), namask=namask,
                eps=eps), cs, poolm


def chunks_of(w):
    n = w.shape[1] // CW
    return w.reshape(KT, P, n, CW).transpose(2, 1, 0, 3).reshape(n, P, CHUNK)


def pair_heads(w, axis):
    order = np.concatenate([np.arange(h * HD, h * HD + HD) for j in range(4) for h in (j, j + 4)])
    return np.take(w, order, axis)


def lay_out(a):
    f = np.float32
    cols = lambda v: np.asarray(v).reshape(-1, P).T
    parts = []
    for what, l, _ in PARTS:
        g = lambda n: np.asarray(a[f"l{l}_{n}"])
        if what == "ada":
            parts.append(chunks_of(g("ada_w")))
        elif what == "in":
            w = g("w_in")
            if l == 0:
                w = np.concatenate([w[:, 256:], w[:, :256]], 1)
            else:
                cq, ck, cv, nq, nk, nv = np.split(w, [512, 640, 768, 1280, 1792], 1)
                w = np.concatenate([pair_heads(cq, 1), nq, ck, nk, cv, nv], 1)
            parts.append(chunks_of(w))
        elif what == "out":
            w = g("w_out")
            if l == 1:
                w = np.concatenate([pair_heads(w[:512], 0), w[512:]], 0)
            parts.append(chunks_of(w))
        elif what == "wq":
            parts.append(chunks_of(g("peer_wq")))
        else:
            u = g("peer_u").reshape(P, GROUPS, 2, KT, P).transpose(1, 4, 3, 2, 0).reshape(GROUPS, P, CHUNK)
            v = g("peer_v").reshape(P, GROUPS, 2, D).transpose(1, 0, 2, 3).reshape(GROUPS, P, CHUNK)
            order = np.empty((PEER_CH, P, CHUNK), f)
            order[0] = u[0]
            order[1:PEER_CH - 1:2] = u[1:]
            order[2:PEER_CH - 1:2] = v[:-1]
            order[PEER_CH - 1] = v[-1]
            parts.append(order)
    stream = np.concatenate(parts, 0)
    x = np.concatenate([np.asarray(a["ctx"])[0], np.asarray(a["x"])[0]], 0)
    xT = np.ascontiguousarray(x.T.reshape(KT, P, NT).transpose(1, 0, 2))
    consts, cs, poolm = constants()
    c2 = np.stack([np.asarray(a["c"])[0], np.asarray(a["c_ctx"])], 1)
    lam = np.zeros((P, 4), f)
    for i, n in enumerate(("q1", "q2", "k1", "k2")):
        lam[:HD, i] = a[f"l0_lambda_{n}"]
    twice = lambda v: np.concatenate([v, v])
    pw = np.asarray(a["l0_pool_w"]).reshape(2, 2, HD, HD).transpose(1, 2, 0, 3).reshape(P, 2 * HD)
    fields = dict(
        consts,
        c=c2.reshape(KT, P, 2).transpose(1, 0, 2).reshape(P, KT * 2),
        ada_b=np.concatenate([cols(a["l0_ada_b"]), cols(a["l1_ada_b"])], 1),
        norm=np.concatenate([cols(a[n]) for n in ("l0_norm1", "l0_norm2", "l1_norm1", "l1_norm2")], 1),
        gain=np.stack([twice(np.asarray(a[n])) for n in ("l0_diff_qnorm", "l0_diff_knorm", "l1_gqa_qnorm", "l1_gqa_knorm",
                                                         "l1_na_qnorm", "l1_na_knorm")], 1),
        subln=np.asarray(a["l0_diff_subln"])[:, None], pscale=cols(a["l0_pool_scale"]), poolw=pw, lam=lam)
    small = np.concatenate([np.asarray(fields[n], f).reshape(P, w) for n, w in SMALL_SIZES], 1)
    keys = np.stack([np.asarray(a[f"l{l}_peer_keys"]).reshape(16, KEYS, P).transpose(2, 0, 1).reshape(P, 2048)
                     for l in range(2)])
    t = np.arange(NLAT)
    dr = t[None] // GRID_W - t[:, None] // GRID_W + 7
    dc = t[None] % GRID_W - t[:, None] % GRID_W + NA_COLS - 1
    far = (dc < 0) | (dc > 2 * NA_COLS - 2)
    rpb = np.asarray(a["l1_na_rpb"])[:, dr, np.where(far, 0, dc)]
    rpb = np.where(far[None], f(0), rpb)
    bias = rpb.reshape(8, 2, P, 256).transpose(2, 0, 1, 3).reshape(P, 4096)
    return dict(xT=xT, small=small, stream=stream, poolm=poolm, cs=cs, bias=np.ascontiguousarray(bias),
                keys=np.ascontiguousarray(keys))


def kernel(**inputs):
    import concourse.bacc as bacc
    from concourse.bass_utils import run_bass_kernel_spmd

    arrays = {k: np.ascontiguousarray(v) for k, v in lay_out(inputs).items()}
    nc = bacc.Bacc("TRN2", target_bir_lowering=False, num_devices=1)
    args = {k: nc.dram_tensor(k, v.shape, F32, kind="ExternalInput").ap() for k, v in arrays.items()}
    out = nc.dram_tensor("y", (P, KT, NLAT), F32, kind="ExternalOutput").ap()
    backbone(nc, **args, out=out)
    r = run_bass_kernel_spmd(nc, [arrays], core_ids=[0])
    y = r.results[0]["y"]
    return np.ascontiguousarray(y.transpose(2, 1, 0)).reshape(1, NLAT, D)
```

```python
from contextlib import ExitStack

import numpy as np

import concourse.bass as bass
from concourse import mybir

F32 = mybir.dt.float32
F32R = mybir.dt.float32r
U32 = mybir.dt.uint32
ALU = mybir.AluOpType
ACT = mybir.ActivationFunctionType
AX_X = mybir.AxisListType.X
ds = bass.ds

P = 128
D = 1024
KT = D // P
NCTX, NLAT = 256, 256
NT = NCTX + NLAT
HD = 64
EPS = 1e-6
LAM_INIT = 0.2
HEADS = 8
KEYS = 128
TOPK = 16
NEG = -3.0e38

CW = 256
CHUNK = KT * CW
RAW = 4
ADA_CH = 6 * D // CW
IN_CH = (10, 9)
OUT_CH = D // CW
WQ_CH = HEADS
PEER_CH = 128
GROUPS = PEER_CH // 2

PARTS = [("ada", 0, ADA_CH), ("in", 0, IN_CH[0]), ("out", 0, OUT_CH), ("wq", 0, WQ_CH), ("peer", 0, PEER_CH),
         ("in", 1, IN_CH[1]), ("out", 1, OUT_CH), ("wq", 1, WQ_CH), ("peer", 1, PEER_CH)]
ADA_BODY = ADA_CH // 2
ADA_ROUNDS = 4 * (1 + ADA_CH // HEADS) // RAW
ADA_HEAD = ADA_CH // HEADS
N0, M0, KIND = {}, {}, []
_m = 0
for _what, _l, _k in PARTS:
    N0[_what, _l], M0[_what, _l] = len(KIND), _m
    for _j in range(_k):
        KIND.append((_what, _l, _j))
        if (_what, _l) == ("wq", 0):
            KIND += [("ada", 1, ADA_HEAD * _j + _i) for _i in range(ADA_HEAD)]
    _m += 0 if _what == "ada" else _k
N_CHUNKS = len(KIND)
N_OF_M = [n for n, k in enumerate(KIND) if k[0] != "ada"]
N_OF_ADA = [[n for n, k in enumerate(KIND) if k[:2] == ("ada", l)] for l in range(2)]

SMALL_SIZES = [("c", KT * 2), ("ada_b", 2 * 48), ("norm", 4 * KT), ("gain", 6), ("subln", 1), ("pscale", 2),
               ("poolw", 2 * HD), ("lam", 4), ("ident", P), ("blockones", P), ("rotT", P), ("iota", P),
               ("ones", P), ("namask", 64), ("eps", 2)]
SMALL, _at = {}, 0
for _n, _w in SMALL_SIZES:
    SMALL[_n] = (_at, _at + _w)
    _at += _w
SMALL_W = _at

ARENA = 18432
A_Q, A_K0, A_V0, A_U, A_YP = 0, 3072, 6144, 9216, 10240
A_K1, A_V1, A_BIAS = 2048, 4608, 7168
A_CS, A_TMP, A_POOLM = 11264, 11776, 15872
A_QJ, A_KEYS, A_REP, A_CAND, A_CREP, A_EQ = 0, 1024, 3072, 3584, 4608, 5632
A_SMALL, A_IDXG, A_IDXT = 7680, 8704, 10240
A_WCH, A_ONEHOT = 0, 11776
A_WG, A_GE, A_PT, A_ACC = 0, 4096, 5120, 14336
A_EQ1 = 16384
A_WIDE, B_NARROW = 3, 4
N_CAND = A_WIDE * TOPK + (TOPK - A_WIDE) * B_NARROW
TL = 32
NA_COLS, GRID_W = 16, 64

TILES = {
    0: [("q", True, 0, False)] * 6 + [("k", True, 1, False)] * 6,
    1: [("q", True, 2, True)] * 4 + [("q", False, 4, True)] * 4 + [("k", True, 3, False)] + [("k", False, 5, False)] * 4,
}
VUNITS = {
    0: [(6, 0, 256, 0, False), (7, 0, 256, 256, False), (8, 0, 256, 512, False), (9, 0, 256, 0, True)],
    1: [(6, 128, 128, 0, False), (7, 0, 256, 128, False), (8, 0, 256, 384, False)],
}


UNITS, DONE = {}, {}
_post = _v = 0
for _l in range(2):
    for _c in range(IN_CH[_l]):
        _units = [("t", _j) for _j in (2 * _c, 2 * _c + 1) if _j < len(TILES[_l])]
        _units += [("v", _j) for _j, _u in enumerate(VUNITS[_l]) if _u[0] == _c]
        UNITS[_l, _c] = _units
        for _w, _j in _units:
            for _tt in range(1 if _w == "t" else 4):
                if (_w, _j) == _units[-1] and _tt == (0 if _w == "t" else 3):
                    DONE[_l, _w, _j, _tt] = ("split_used", M0["in", _l] + _c + 1)
                elif _w == "t":
                    _post += 1
                    DONE[_l, _w, _j, _tt] = ("post_in", _post)
                else:
                    _v += 1
                    DONE[_l, _w, _j, _tt] = ("v_in", _v)


class Steps:

    def __init__(self, sem):
        self.sem, self.n = sem, 0

    def inc(self):
        self.n += 1
        return self.sem, 1

    def restart(self):
        self.n = 0


def backbone(nc, xT, small, stream, poolm, cs, bias, keys, out):
    with ExitStack() as ctx:
        def sb(name, shape, dt=F32):
            return ctx.enter_context(nc.sbuf_tensor(name, shape, dt))

        sems = {}

        def sem(name):
            if name not in sems:
                sems[name] = ctx.enter_context(nc.semaphore(name))
            return sems[name]

        wdram = nc.dram_tensor("gate_matrix", (P, NT // TL, KEYS, TL), F32, kind="Internal").ap()

        x = sb("x", [P, KT, NT])
        h_hi = sb("h_hi", [P, KT, NT], F32R)
        h_lo = sb("h_lo", [P, KT, NT], F32R)
        raw = sb("raw", [P, RAW, CHUNK])
        w_hi = sb("w_hi", [P, 2, CHUNK], F32R)
        w_lo = sb("w_lo", [P, 2, CHUNK], F32R)
        p_hi = sb("p_hi", [P, 4, NT], F32R)
        p_lo = sb("p_lo", [P, 4, NT], F32R)
        sm = sb("sm", [P, SMALL_W])
        mod = sb("mod", [P, 2, 48, 2])
        gainmod = sb("gainmod", [P, 4, KT, 2])
        silu_c = sb("silu_c", [P, KT, 2])
        lamv = sb("lamv", [P, 8])
        sub8 = sb("sub8", [P, 1])
        ada_row = sb("ada_row", [2, 2, CW])
        stats = sb("stats", [P, 2, 8])
        gate = sb("gate", [P, 1])
        arena = sb("arena", [P, ARENA])
        bank = [ctx.enter_context(nc.psum_tensor(f"bank{i}", [P, 512], F32)) for i in range(8)]

        def view(at, *shape):
            n = int(np.prod(shape))
            v = arena[:, at:at + n]
            if len(shape) == 2:
                v = v.rearrange("p (a b) -> p a b", a=shape[0])
            elif len(shape) == 3:
                v = v.rearrange("p (a b c) -> p a b c", a=shape[0], b=shape[1])
            return v

        def small_of(name, a=0, b=None):
            lo, hi = SMALL[name]
            return sm[:, lo + a:(hi if b is None else lo + b)]

        ident, blockones, rotT, iota, ones = (small_of(n) for n in ("ident", "blockones", "rotT", "iota", "ones"))
        c_in = small_of("c").rearrange("p (a s) -> p a s", s=2)
        rw = [raw[:, s, :].rearrange("p (k n) -> p k n", k=KT) for s in range(RAW)]
        wsplit = [(w_hi[:, s, :], w_lo[:, s, :]) for s in range(2)]
        wk = [tuple(w.rearrange("p (k n) -> p k n", k=KT) for w in pair) for pair in wsplit]

        tmp = [view(A_TMP + 512 * i, 512) for i in range(8)]
        sq, qg, std = tmp[0:2], tmp[2:4], tmp[4:6]
        t1, t2 = [tmp[6][:, 0:256], tmp[6][:, 256:512]], [tmp[7][:, 0:256], tmp[7][:, 256:512]]
        cos_sin = view(A_CS, 2, NLAT)
        q_of = {0: view(A_Q, 6, NT), 1: view(A_Q, 8, NLAT)}
        k_of = {0: view(A_K0, 6, NT), 1: view(A_K1, 5, NT)}
        v_of = {0: view(A_V0, 4, 768), 1: view(A_V1, 4, 640)}
        u_tok, y_pool, pool_m = view(A_U, 4, 256), view(A_YP, 2, NT), view(A_POOLM, 4, 2, 256)
        na_bias = view(A_BIAS, 16, 256)

        STREAMS = ((0, NCTX, NT), (1, 0, NCTX))

        def streams(c0):
            return [s for s in STREAMS if s[1] >= c0]

        def first_col(l, peer):
            return NCTX if l == 1 else 0

        def chunk_ready(eng, n, i=0):
            eng.wait_ge(sem(f"raw_ready{n % RAW}"), i * 16 + 16 * (n // RAW + 1))

        def split_hi(act, m, i=0, per=0, rounds=None):
            chunk_ready(act, N_OF_M[m], i * (per // RAW if rounds is None else rounds))
            if m >= 2:
                act.wait_ge(sem("split_used"), i * per + (m - 1))
            act.activation(w_hi[:, m % 2, :], raw[:, N_OF_M[m] % RAW, :], ACT.Copy).then_inc(sem("hi_done"), 1)

        def split_lo(eng, m, i=0, per=0):
            eng.wait_ge(sem("hi_done"), i * per + (m + 1))
            eng.tensor_tensor(w_lo[:, m % 2, :], raw[:, N_OF_M[m] % RAW, :], w_hi[:, m % 2, :],
                              ALU.subtract).then_inc(sem("lo_done"), 1)

        def split_ready(pe, m, i=0, per=0):
            pe.wait_ge(sem("lo_done"), i * per + (m + 1))

        def mm3(pe, dst, pairs):
            last = None
            for k, ((ah, al), (bh, bl)) in enumerate(pairs):
                pe.matmul(dst, ah, bh, start=(k == 0), stop=False)
                pe.matmul(dst, al, bh, start=False, stop=False)
                last = pe.matmul(dst, ah, bl, start=False, stop=(k == len(pairs) - 1))
            return last

        def feature_tile(pe, dst, slot, col, c0, norm=None):
            if norm is not None:
                for k in range(KT):
                    pe.wait_ge(sem("nlo"), KT * norm + k + 1)
                    ah, al = (w[:, k, col:col + P] for w in wk[slot])
                    pe.matmul(dst, ah, h_hi[:, k, c0:NT], start=(k == 0), stop=False)
                    pe.matmul(dst, al, h_hi[:, k, c0:NT], start=False, stop=False)
                    last = pe.matmul(dst, ah, h_lo[:, k, c0:NT], start=False, stop=(k == KT - 1))
                return last
            return mm3(pe, dst, [((wk[slot][0][:, k, col:col + P], wk[slot][1][:, k, col:col + P]),
                                  (h_hi[:, k, c0:NT], h_lo[:, k, c0:NT])) for k in range(KT)])

        def norm_t(kt):
            return tmp[3 + kt % 3]

        def mixer_out(l, kt):
            if l == 1:
                return q_of[1][:, kt, :]
            return y_pool[:, kt, :] if kt < 2 else q_of[0][:, kt - 2, :]

        def masks(ntt):
            return [[view(at + 1024 * a, 64, TOPK)[:, 0:ntt * TOPK, :] for a in range(2)] for at in (A_EQ, A_EQ1)]

        def indices(b):
            return view(A_SMALL + 704 + 128 * b, 128).bitcast(U32).rearrange("p (t s k) -> p t s k", t=4, s=2)

        def attention_units(l):
            if l == 0:
                return [(h, c, NT if c >= NCTX else NCTX, h, (P * h,), None)
                        for h in range(6) for c in (NCTX, NCTX + P, 0, P)]
            units = [(j, c, NT, 0, (0, HD), None) for j in range(4) for c in (0, P)]
            return units + [(4 + j, P * b, NT, 1 + j, (P + P * j, P + P * j + HD), (4 * j + b, 4 * j + 2 + b))
                            for j in range(4) for b in range(2)]

        block = ctx.enter_context(nc.Block())

        @block.sync
        def _(sp):
            def raw_free(n, i=0, per=0):
                what, l, j = KIND[n - RAW]
                if what == "ada":
                    sp.wait_ge(sem("ada_used"), i * per + (ADA_CH * l + j + 1))
                else:
                    sp.wait_ge(sem("lo_done"), i * per + (M0[what, l] + j + 1))

            def load(n, i=0, per=0):
                if n >= RAW:
                    raw_free(n, i, per)
                src = stream[n] if isinstance(i, int) else stream[ds(i * per + n, 1)].rearrange("a p n -> (a p) n")
                sp.dma_start(raw[:, n % RAW, :], src).then_inc(sem(f"raw_ready{n % RAW}"), 16)

            sp.dma_start(sm[:], small).then_inc(sem("small_in"), 16)
            sp.dma_start(x[:], xT).then_inc(sem("x_in"), 16)
            for n in range(RAW):
                load(n)
            sp.dma_start(view(A_CS, 2 * NLAT), cs).then_inc(sem("cs_in0"), 16)
            sp.dma_start(view(A_POOLM, 2048), poolm).then_inc(sem("poolm_in"), 16)
            with sp.Fori(0, ADA_CH // RAW - 1) as i:
                for k in range(RAW):
                    load(RAW + k, i, RAW)
            for n in range(ADA_CH, N0["peer", 0]):
                load(n)

            def peer(l):
                n0 = N0["peer", l]
                tokens = NT - first_col(l, True)
                for n in range(n0, n0 + RAW):
                    load(n)
                with sp.Fori(0, tokens // (2 * TL)) as i:
                    for c in range(2):
                        sp.wait_ge(sem(f"w_evac{l}"), i * 16 + (4 + 8 * c + 8))
                        sp.dma_start(wdram[:, ds(i * 2 + c, 1)].rearrange("p a b c -> p (a b c)"),
                                     view(A_WCH + 4096 * c, 4096)).then_inc(sem(f"w_out{l}_{c}"), 16)
                load(n0 + RAW)
                for c in range(2):
                    sp.wait_ge(sem(f"w_out{l}_{c}"), 16 + 16 * (tokens // (2 * TL)))

                def gates(w, b):
                    ntc = tokens // TL
                    sp.dma_start(view(A_WG + 2048 * b, 16, 4 * TL)[:, 0:ntc, :],
                                 wdram[:, 0:ntc, ds(w * 4, 4), :].rearrange("p a b c -> p a (b c)"))\
                      .then_inc(sem(f"w_in{l}_{b}"), 16)

                gates(0, 0)
                gates(1, 1)
                with sp.Fori(0, GROUPS // 4 - 1) as i:
                    for half in range(2):
                        for k in range(4):
                            load(n0 + RAW + 1 + 4 * half + k, i, 8)
                        sp.wait_ge(sem(f"pm_done{l}"), i * 8 + (2 + 4 * half + 4))
                        gates(i * 2 + (2 + half), half)
                for n in range(n0 + PEER_CH - 3, n0 + PEER_CH):
                    load(n)

            peer(0)
            for n in range(N0["in", 1], N0["peer", 1]):
                load(n)
            peer(1)
            sp.wait_ge(sem("x_done"), 2)
            sp.dma_start(out, x[:, :, NCTX:NT]).then_inc(sem("out_done"), 16)
            sp.wait_ge(sem("out_done"), 16)

        @block.tensor
        def _(pe):
            def ada_chunk(l, c, i, rounds):
                n = N_OF_ADA[l][c]
                row = bank[6 if c % 2 else 4][0:2, 0:CW]
                chunk_ready(pe, n, i * rounds)
                pe.wait_ge(sem(f"row_evac{l}"), i * ADA_BODY + (c + 1))
                for kt in range(KT):
                    last = pe.matmul(row, silu_c[:, kt, :], rw[n % RAW][:, kt, :], start=(kt == 0), stop=(kt == KT - 1))
                last.then_inc(sem("ada_used"), 1)

            def ada_turn(l, c, i):
                if c == 0:
                    pe.wait_ge(sem(f"mod_evac{l}"), i + 1)
                pe.wait_ge(sem(f"row_evac{l}"), i * ADA_BODY + (c + 3))
                for half in range(2):
                    last = pe.matmul(bank[7][:, 4 * c + 2 * half:4 * c + 2 * half + 2],
                                     ada_row[0:2, c % 2, half * P:half * P + P], ident[0:2, 0:2], start=True, stop=True)
                last.then_inc(sem(f"mod_turned{l}"), 1)

            def ada(l):
                pe.wait_ge(sem("silu_done"), 1)
                pe.sem_inc(sem(f"mod_turned{l}"), 2)
                with pe.Fori(0, 2) as i:
                    ada_chunk(l, 0, i, ADA_BODY // RAW)
                    for c in range(1, ADA_BODY):
                        ada_chunk(l, c, i, ADA_BODY // RAW)
                        ada_turn(l, c - 1, i)
                    ada_turn(l, ADA_BODY - 1, i)

            def norm(q):
                c0 = 0 if q < 3 else NCTX
                for kt in range(KT):
                    pe.wait_ge(sem("nsq"), KT * q + kt + 1)
                    pe.matmul(bank[5][:, c0:NT], ones, sq[kt % 2][:, c0:NT], start=(kt == 0),
                              stop=(kt == KT - 1)).then_inc(sem("nsq_used"), 1)

            def project(l):
                m0 = M0["in", l]
                tiles, vunits = TILES[l], VUNITS[l]
                nt = len(tiles)

                def heads_stats(j):
                    kind, rope, _, lat = tiles[j]
                    g, b, c0 = 13 * l + j - l, j % 2, NCTX if lat else 0
                    pe.wait_ge(sem("post_sq"), g + 1)
                    if j >= 2:
                        pe.wait_ge(sem("post_std"), g - 1)
                    pe.matmul(bank[2 + b][:, c0:NT], blockones, sq[b][:, c0:NT], start=True,
                              stop=True).then_inc(sem("post_ss"), 1)
                    pe.wait_ge(sem("post_qg"), g + 1)
                    if j >= 2:
                        pe.wait_ge(sem("post_done"), g - 1)
                    pe.matmul(bank[4 + b][:, 0:NLAT], rotT, qg[b][:, NCTX:NT], start=True,
                              stop=True).then_inc(sem("post_rot"), 1)

                for c in range(IN_CH[l]):
                    m = m0 + c
                    split_ready(pe, m)
                    for what, j in UNITS[l, c]:
                        if what == "t":
                            g = 13 * l + j - l
                            if j >= 2:
                                pe.wait_ge(sem("post_qg"), g - 1)
                            c0 = NCTX if tiles[j][3] else 0
                            last = feature_tile(pe, bank[j % 2][:, c0:NT], m % 2, P * (j % 2), c0,
                                                2 * l if j == 0 else None)
                            last.then_inc(sem(DONE[l, "t", j, 0][0]), 1)
                            if j >= 1:
                                heads_stats(j - 1)
                        else:
                            _, col, width, _, _ = vunits[j]
                            if j == 0:
                                heads_stats(nt - 1)
                            for tt in range(4):
                                e = 16 * l + 4 * j + tt
                                if 4 * j + tt >= 2:
                                    pe.wait_ge(sem("v_evac"), e - 1)
                                tok = slice(P * tt, P * tt + P)
                                last = mm3(pe, bank[6 + tt % 2][:, 0:width],
                                           [((h_hi[:, k, tok], h_lo[:, k, tok]),
                                             (wk[m % 2][0][:, k, col:col + width], wk[m % 2][1][:, k, col:col + width]))
                                            for k in range(KT)])
                                last.then_inc(sem(DONE[l, "v", j, tt][0]), 1)

            def pool():
                pe.wait_ge(sem("v_evac"), 16)
                pe.wait_ge(sem("poolm_in"), 16)
                for pr in range(2):
                    for gi in range(2):
                        for s in range(2):
                            for tt in range(2):
                                last = pe.matmul(bank[6 + pr][HD * gi:HD * gi + HD, 256 * s:256 * s + 256],
                                                 u_tok[:, 2 * s + tt, (2 * pr + gi) * HD:(2 * pr + gi + 1) * HD],
                                                 pool_m[:, 2 * pr + gi, tt, :], start=(tt == 0), stop=(tt == 1))
                    last.then_inc(sem("pool_mean"), 1)
                poolw = small_of("poolw").rearrange("p (a b) -> p a b", a=2)
                pe.wait_ge(sem("post_done"), 12)
                for pr in range(2):
                    pe.wait_ge(sem("pool_evac"), pr + 1)
                    for gi in range(2):
                        rows = slice(HD * gi, HD * gi + HD)
                        last = pe.matmul(bank[4 + pr][rows, :], poolw[rows, pr, :], y_pool[rows, pr, :],
                                         start=True, stop=True)
                    last.then_inc(sem("pool_y"), 1)

            def attention(l):
                units, base = attention_units(l), 32 * l - 8 * l
                pe.wait_ge(sem("post_done"), 12 + 13 * l)
                pe.wait_ge(sem("v_evac"), 16 + 12 * l)
                if l == 0:
                    pe.wait_ge(sem("pool_evac"), 4)
                qv, kv, vv = q_of[l], k_of[l], v_of[l]

                def scores(u):
                    j, qc, nk, kj, _, _ = units[u]
                    if u >= 2:
                        pe.wait_ge(sem("exp_done"), 2 * (base + u - 1))
                    for i in range(2):
                        rows = slice(HD * i, HD * i + HD)
                        pe.matmul(bank[2 * (u % 2) + i][:, 0:nk], qv[rows, j, qc:qc + P], kv[rows, kj, 0:nk],
                                  start=True, stop=True).then_inc(sem("scores_done"), 1)

                def turn(u):
                    nk = units[u][2]
                    pe.wait_ge(sem("probs_done"), base + u + 1)
                    if u >= (2 if l == 0 else 1):
                        pe.wait_ge(sem("turned_evac"), base + u - 1 if l == 0 else base + u)
                    for i in range(1 + l):
                        for kb in range(nk // P):
                            dst = bank[4 + (u % 2 if l == 0 else i)][:, kb * P:kb * P + P]
                            last = pe.transpose(dst, tmp[2 * (u % 2) + i][:, kb * P:kb * P + P], ident)
                    last.then_inc(sem("turned"), 1)

                def values(u):
                    nk, cols = units[u][2], units[u][4]
                    pe.wait_ge(sem("turned_evac"), base + u + 1)
                    if u >= 2:
                        pe.wait_ge(sem("heads_evac"), base + u - 1)
                    wt = view(A_TMP + 2048 + 1024 * (u % 2), 2, 4, P)
                    for i in range(1 + l):
                        width = P if l == 0 else HD
                        for kb in range(nk // P):
                            last = pe.matmul(bank[6 + u % 2][width * i * l:width * i * l + width, 0:P],
                                             vv[:, kb, cols[i]:cols[i] + width], wt[:, i, kb, :],
                                             start=(kb == 0), stop=(kb == nk // P - 1))
                    last.then_inc(sem("heads_done"), 1)

                scores(0)
                for u in range(len(units)):
                    if u + 1 < len(units):
                        scores(u + 1)
                    turn(u)
                    if u:
                        values(u - 1)
                values(len(units) - 1)

            def subln():
                for h in range(6):
                    pe.wait_ge(sem("sub_sq"), h + 1)
                    if h >= 2:
                        pe.wait_ge(sem("sub_std"), h - 1)
                    pe.matmul(bank[h % 2][:], ones, sq[h % 2], start=True, stop=True).then_inc(sem("sub_ss"), 1)

            def project_out(l):
                c0 = first_col(l, True)
                pe.wait_ge(sem("ylo"), KT * (l + 1))
                for c in range(OUT_CH):
                    m = M0["out", l] + c
                    split_ready(pe, m)
                    for jj in range(2):
                        dt = 2 * c + jj
                        if dt >= 2:
                            pe.wait_ge(sem("out_evac"), KT * l + dt - 1)
                        last = feature_tile(pe, bank[dt % 2][:, c0:NT], m % 2, P * jj, c0)
                        last.then_inc(sem("split_used" if jj else "out_in"), 1)

            def choose(l):
                c0 = first_col(l, True)
                tokens = NT - c0
                m0, qj = M0["wq", l], view(A_QJ, 2, NT)
                kv = view(A_KEYS, 16, KEYS)
                pe.wait_ge(sem("nlo"), KT * (2 * l + 2))
                pe.wait_ge(sem(f"keys_in{l}"), 16)
                pe.sem_inc(sem(f"sc_done{l}"), 2)
                if l == 0:
                    pe.sem_inc(sem("mod_turned1"), 2)
                with pe.Fori(0, 2) as i:
                    def query(j):
                        if j % 2 == 0:
                            split_ready(pe, m0 + j // 2, i, 4)
                        pe.wait_ge(sem(f"qj_done{l}"), i * 8 + (j + 1))
                        last = feature_tile(pe, bank[j % 2][:, 0:tokens], (m0 + j // 2) % 2, P * (j % 2), c0)
                        last.then_inc(sem("split_used" if j % 2 else f"qj_in{l}"), 1)

                    def score(j):
                        pe.wait_ge(sem(f"qj_done{l}"), i * 8 + (j + 3))
                        pe.wait_ge(sem(f"sc_free{l}"), i * 8 + (j + 1))
                        for tt in range(tokens // P):
                            last = pe.matmul(bank[2 + j % 2][:, tt * P:tt * P + P], qj[:, j % 2, tt * P:tt * P + P],
                                             kv[:, ds(i * 8 + j, 1), :].rearrange("p a b -> p (a b)"),
                                             start=True, stop=True)
                        last.then_inc(sem(f"sc_done{l}"), 1)

                    def ada_of(h):
                        for c in range(ADA_HEAD * h, ADA_HEAD * h + ADA_HEAD):
                            ada_chunk(1, c, i, ADA_ROUNDS)
                            if c:
                                ada_turn(1, c - 1, i)

                    for h in range(4):
                        query(2 * h)
                        query(2 * h + 1)
                        if l == 0:
                            ada_of(h)
                        score(2 * h)
                        if l == 0 and h == 3:
                            ada_turn(1, ADA_BODY - 1, i)
                        score(2 * h + 1)

            def turn_choices(l):
                ntt = (NT - first_col(l, True)) // P
                idxg = view(A_IDXG, 3, 4, P)
                pe.wait_ge(sem(f"chosen{l}"), HEADS)
                for a in range(3):
                    for tt in range(ntt):
                        last = pe.transpose(bank[4 + a][:, tt * P:tt * P + P], idxg[:, a, tt, :], ident)
                    last.then_inc(sem("choices_turned"), 1)

            def build(l):
                tokens = NT - first_col(l, True)
                oh = view(A_ONEHOT, 4, 8, P)
                pe.sem_inc(sem(f"w_done{l}"), 4)
                with pe.Fori(0, tokens // (2 * TL)) as i:
                    for b in range(16):
                        pe.wait_ge(sem(f"oh_gated{l}"), i * 16 + (b + 1))
                        pe.wait_ge(sem(f"w_evac{l}"), i * 16 + (b + 1))
                        for t in range(4):
                            last = pe.matmul(bank[b % 4][:, t * P:t * P + P], oh[:, b % 4, t, :],
                                             oh[:, b % 4, 4 + t, :], start=True, stop=True)
                        last.then_inc(sem(f"w_done{l}"), 1)

            def experts(l):
                c0 = first_col(l, True)
                T = NT - c0
                m0 = M0["peer", l]

                pe.wait_ge(sem(f"w_evac{l}"), 4 + T // 4)

                def up(m, g, i, mi):
                    split_ready(pe, m, mi, 8)
                    for a in range(2):
                        e = 2 * g + a
                        pe.wait_ge(sem(f"ge_done{l}"), i * 8 + (e + 1))
                        last = feature_tile(pe, bank[e % 4][:, 0:T], m % 2, P * a, c0)
                        last.then_inc(sem("split_used" if a else f"h_done{l}"), 1)

                def down(m, g, i, mi):
                    split_ready(pe, m, mi, 8)
                    pe.wait_ge(sem(f"plo_done{l}"), i * 8 + (2 * g + 2 + 2))
                    hi, lo = wsplit[m % 2]
                    for dt in range(KT):
                        pe.wait_ge(sem(f"acc_done{l}"), i * 32 + (8 * g + dt + 1))
                        cols = [slice(D * a + P * dt, D * a + P * dt + P) for a in range(2)]
                        last = mm3(pe, bank[4 + dt % 4][:, 0:T],
                                   [((hi[:, cols[a]], lo[:, cols[a]]),
                                     (p_hi[:, (2 * g + a) % 4, 0:T], p_lo[:, (2 * g + a) % 4, 0:T])) for a in range(2)])
                        last.then_inc(sem(f"v_done{l}" if dt < KT - 1 else "split_used"), 1)

                up(m0, 0, 0, 0)
                with pe.Fori(0, GROUPS // 4 - 1) as i:
                    for g in range(4):
                        up(m0 + 1 + 2 * g, g + 1, i, i)
                        down(m0 + 2 + 2 * g, g, i, i)
                r = GROUPS // 4 - 1
                for g in range(4):
                    if g < 3:
                        up(m0 + 1 + 2 * g, g + 1, r, r)
                        down(m0 + 2 + 2 * g, g, r, r)
                    else:
                        down(m0 + PEER_CH - 1, 3, r, 0)

            pe.wait_ge(sem("small_in"), 16)
            pe.wait_ge(sem("lam_prod"), 1)
            pe.matmul(bank[6][:, 0:2], ones[0:HD, :], lamv[0:HD, 0:2], start=True, stop=True).then_inc(sem("lam_dot"), 1)
            norm(0)
            ada(0)
            for l in range(2):
                if l:
                    norm(2 * l)
                project(l)
                if l == 0:
                    pool()
                attention(l)
                if l == 0:
                    subln()
                project_out(l)
                norm(2 * l + 1)
                choose(l)
                turn_choices(l)
                build(l)
                experts(l)

        @block.scalar
        def _(act):
            eps1, eps64 = small_of("eps", 0, 1), small_of("eps", 1, 2)

            def row(l, c, i):
                act.wait_ge(sem("ada_used"), i * ADA_BODY + (ADA_CH * l + c + 1))
                act.wait_ge(sem(f"mod_turned{l}"), i * ADA_BODY + (c + 1))
                act.activation(ada_row[0:2, c % 2, :], bank[6 if c % 2 else 4][0:2, 0:CW], ACT.Copy)\
                   .then_inc(sem(f"row_evac{l}"), 1)

            def deviation_all(q):
                c0, l, rstd = (0 if q < 3 else NCTX), q // 2, tmp[2]
                for kt in range(KT):
                    if kt >= 2:
                        act.wait_ge(sem("nsq_used"), KT * q + kt - 1)
                    if q % 2:
                        act.wait_ge(sem("out_evac"), KT * l + kt + 1)
                    elif q == 2:
                        act.wait_ge(sem("x_done"), 1)
                    act.activation(sq[kt % 2][:, c0:NT], x[:, kt, c0:NT], ACT.Square).then_inc(sem("nsq"), 1)
                act.wait_ge(sem("nsq_used"), KT * (q + 1))
                act.activation(rstd[:, c0:NT], bank[5][:, c0:NT], ACT.Sqrt, bias=eps1,
                               scale=1.0 / D).then_inc(sem("nstd"), 1)

            def norm(q):
                c0, l, part = (0 if q < 3 else NCTX), q // 2, 3 * (q % 2)
                for kt in range(KT):
                    act.wait_ge(sem("nt"), KT * q + kt + 1)
                    for s, lo, hi in streams(c0):
                        last = act.activation(h_hi[:, kt, lo:hi], norm_t(kt)[:, lo:hi], ACT.Identity,
                                              bias=mod[:, l, part * KT + kt, s:s + 1])
                    last.then_inc(sem("nhi"), 1)

            def project(l):
                tiles, vunits = TILES[l], VUNITS[l]
                nt = len(tiles)

                def deviation(j):
                    kind, _, _, lat = tiles[j]
                    g, b, c0 = 13 * l + j - l, j % 2, NCTX if lat else 0
                    act.wait_ge(sem("post_ss"), g + 1)
                    if j >= 2:
                        act.wait_ge(sem("post_done"), g - 1)
                    act.activation(std[b][:, c0:NT], bank[2 + b][:, c0:NT], ACT.Sqrt, bias=eps64 if kind == "q" else eps1,
                                   scale=1.0 if kind == "q" else 1.0 / HD).then_inc(sem("post_std"), 1)

                for c in range(IN_CH[l]):
                    split_hi(act, M0["in", l] + c + 1)
                    for what, j in UNITS[l, c]:
                        if what == "t":
                            _, _, gain, lat = tiles[j]
                            g, b, c0 = 13 * l + j - l, j % 2, NCTX if lat else 0
                            done, count = DONE[l, "t", j, 0]
                            act.wait_ge(sem(done), count)
                            if j >= 2:
                                act.wait_ge(sem("post_ss"), g - 1)
                            act.activation(sq[b][:, c0:NT], bank[b][:, c0:NT], ACT.Square).then_inc(sem("post_sq"), 1)
                            if j >= 2:
                                act.wait_ge(sem("post_done"), g - 1)
                                act.wait_ge(sem("post_rot"), g - 1)
                            act.activation(qg[b][:, c0:NT], bank[b][:, c0:NT], ACT.Identity,
                                           scale=small_of("gain", gain, gain + 1)).then_inc(sem("post_qg"), 1)
                            if j >= 1:
                                deviation(j - 1)
                        else:
                            _, _, width, at, is_pool = vunits[j]
                            if j == 0:
                                deviation(nt - 1)
                            for tt in range(4):
                                done, count = DONE[l, "v", j, tt]
                                act.wait_ge(sem(done), count)
                                dst = u_tok if is_pool else v_of[l]
                                act.activation(dst[:, tt, at:at + width], bank[6 + tt % 2][:, 0:width],
                                               ACT.Copy).then_inc(sem("v_evac"), 1)

            def pool():
                for pr in range(2):
                    act.wait_ge(sem("pool_mean"), pr + 1)
                    act.activation(y_pool[:, pr, :], bank[6 + pr][:], ACT.Copy).then_inc(sem("pool_evac"), 1)
                for pr in range(2):
                    act.wait_ge(sem("pool_y"), pr + 1)
                    act.activation(y_pool[:, pr, :], bank[4 + pr][:], ACT.Identity,
                                   scale=small_of("pscale", pr, pr + 1)).then_inc(sem("pool_evac"), 1)

            def attention(l):
                units, base = attention_units(l), 24 * l
                act.wait_ge(sem("post_done"), 12 + 13 * l)

                def exps(u):
                    nk, st = units[u][2], stats[:, u % 2, :]
                    if u >= 2:
                        act.wait_ge(sem("turned"), base + u - 1)
                    for i in range(2):
                        act.wait_ge(sem("max_done"), 2 * (base + u) + i + 1)
                        act.activation(tmp[2 * (u % 2) + i][:, 0:nk], bank[2 * (u % 2) + i][:, 0:nk], ACT.Exp,
                                       bias=st[:, i:i + 1], accum_out=st[:, 2 + i:3 + i]).then_inc(sem("exp_done"), 1)

                def evac(u):
                    nk = units[u][2]
                    act.wait_ge(sem("turned"), base + u + 1)
                    if u >= 2:
                        act.wait_ge(sem("heads_done"), base + u - 1)
                    for i in range(1 + l):
                        wt = view(A_TMP + 2048 + 1024 * (u % 2) + 512 * i, 512)
                        last = act.activation(wt[:, 0:nk], bank[4 + (u % 2 if l == 0 else i)][:, 0:nk], ACT.Copy)
                    last.then_inc(sem("turned_evac"), 1)

                exps(0)
                for u in range(len(units)):
                    if u + 1 < len(units):
                        exps(u + 1)
                    evac(u)

            def subln():
                def deviation(h):
                    act.wait_ge(sem("sub_ss"), h + 1)
                    if h >= 2:
                        act.wait_ge(sem("sub_done"), h - 1)
                    act.activation(std[h % 2], bank[h % 2][:], ACT.Sqrt, bias=eps1, scale=1.0 / P)\
                       .then_inc(sem("sub_std"), 1)

                act.wait_ge(sem("heads_evac"), 24)
                for h in range(6):
                    if h >= 2:
                        act.wait_ge(sem("sub_ss"), h - 1)
                    act.activation(sq[h % 2], q_of[0][:, h, :], ACT.Square).then_inc(sem("sub_sq"), 1)
                    if h:
                        deviation(h - 1)
                deviation(5)

            def mixed(l):
                c0 = first_col(l, True)
                for kt in range(KT):
                    if l == 0:
                        if kt >= 2:
                            act.wait_ge(sem("sub_done"), kt - 1)
                        else:
                            act.wait_ge(sem("pool_evac"), 4)
                    else:
                        act.wait_ge(sem("heads_evac"), 40)
                    act.activation(h_hi[:, kt, c0:NT], mixer_out(l, kt), ACT.Copy).then_inc(sem("yhi"), 1)

            def project_out(l):
                for c in range(OUT_CH - 1):
                    split_hi(act, M0["out", l] + c + 1)

            def choose(l):
                tokens = NT - first_col(l, True)
                m0, qj = M0["wq", l], view(A_QJ, 2, NT)
                act.sem_inc(sem(f"qj_done{l}"), 2)
                if l == 0:
                    act.sem_inc(sem("row_evac1"), 2)

                def exps(h, i):
                    gd = view(A_SMALL + 576 + 64 * (h % 2), 64)
                    act.wait_ge(sem(f"gd_done{l}"), i * 4 + (h + 1))
                    act.activation(gd[:, 0:tokens // P * TOPK], gd[:, 0:tokens // P * TOPK], ACT.Exp)\
                       .then_inc(sem(f"gexp_done{l}"), 1)

                split_hi(act, m0)
                with act.Fori(0, 2) as i:
                    for h in range(4):
                        split_hi(act, m0 + h + 1, i, 4, ADA_ROUNDS if l == 0 else 1)
                        for p in range(2):
                            j = 2 * h + p
                            if p:
                                act.wait_ge(sem("split_used"), i * 4 + (m0 + h + 1))
                            else:
                                act.wait_ge(sem(f"qj_in{l}"), i * 4 + (h + 1))
                            act.wait_ge(sem(f"sc_done{l}"), i * 8 + (j + 1))
                            act.activation(qj[:, p, 0:tokens], bank[p][:, 0:tokens], ACT.Copy)\
                               .then_inc(sem(f"qj_done{l}"), 1)
                        if l == 0:
                            for c in range(ADA_HEAD * h, ADA_HEAD * h + ADA_HEAD):
                                row(1, c, i)
                        if h:
                            exps(h - 1, i)
                    exps(3, i)

            def turn_choices(l):
                tokens = NT - first_col(l, True)
                idxt = view(A_IDXT, 3, NT)
                for a in range(3):
                    act.wait_ge(sem("choices_turned"), 3 * l + a + 1)
                    act.activation(idxt[:, a, 0:tokens], bank[4 + a][:, 0:tokens], ACT.Copy)\
                       .then_inc(sem("choices_evac"), 1)

            def build(l):
                tokens = NT - first_col(l, True)
                act.sem_inc(sem(f"w_evac{l}"), 4)
                for c in range(2):
                    act.sem_inc(sem(f"w_out{l}_{c}"), 16)
                with act.Fori(0, tokens // (2 * TL)) as i:
                    for b in range(16):
                        c = b // 8
                        if b % 8 == 0:
                            act.wait_ge(sem(f"w_out{l}_{c}"), i * 16 + 16)
                        act.wait_ge(sem(f"w_done{l}"), i * 16 + (b + 1 + 4))
                        piece = view(A_WCH + 4096 * c, KEYS, TL)[:, :, 4 * (b % 8):4 * (b % 8) + 4]
                        act.activation(piece.rearrange("p n t -> p t n"),
                                       bank[b % 4][:].rearrange("p (t n) -> p t n", t=4), ACT.Copy)\
                           .then_inc(sem(f"w_evac{l}"), 1)

            def experts(l):
                T = NT - first_col(l, True)
                m0 = M0["peer", l]
                ge, pt = view(A_GE, 2, NT), view(A_PT, 2, NT)
                act.sem_inc(sem(f"ge_done{l}"), 4)

                def gelu(e, i):
                    if e % 2:
                        act.wait_ge(sem("split_used"), i * 8 + (m0 + max(e - 2, 0) + 1))
                    else:
                        act.wait_ge(sem(f"h_done{l}"), i * 4 + (e // 2 + 1))
                    act.wait_ge(sem(f"pm_done{l}"), i * 8 + (e + 1))
                    act.activation(ge[:, e % 2, 0:T], bank[e % 4][:, 0:T], ACT.Gelu).then_inc(sem(f"ge_done{l}"), 1)
                    act.wait_ge(sem(f"pm_done{l}"), i * 8 + (e + 3))
                    act.wait_ge(sem("split_used"), i * 8 + (m0 - 1 + 2 * (e // 2)))
                    act.activation(p_hi[:, e % 4, 0:T], pt[:, e % 2, 0:T], ACT.Copy).then_inc(sem(f"phi_done{l}"), 1)

                def step(g, i):
                    split_hi(act, m0 + 2 + 2 * g, i, 8)
                    gelu(2 * g + 2, i)
                    split_hi(act, m0 + 3 + 2 * g, i, 8)
                    gelu(2 * g + 3, i)

                for c in range(2):
                    act.wait_ge(sem(f"w_out{l}_{c}"), 16 + 16 * (T // (2 * TL)))
                split_hi(act, m0 + 1)
                gelu(0, 0)
                gelu(1, 0)
                with act.Fori(0, GROUPS // 4 - 1) as i:
                    for g in range(4):
                        step(g, i)
                for g in range(3):
                    step(g, GROUPS // 4 - 1)
                if l == 0:
                    split_hi(act, M0["in", 1])

            act.wait_ge(sem("small_in"), 16)
            act.activation(silu_c[:], c_in, ACT.Silu).then_inc(sem("silu_done"), 1)
            act.wait_ge(sem("lam_dot"), 1)
            act.activation(lamv[:, 2:4], bank[6][:, 0:2], ACT.Exp).then_inc(sem("lam_exp"), 1)
            act.wait_ge(sem("x_in"), 16)
            deviation_all(0)
            act.sem_inc(sem("row_evac0"), 2)
            with act.Fori(0, 2) as i:
                for c in range(ADA_BODY):
                    row(0, c, i)
            split_hi(act, 0)
            for l in range(2):
                if l:
                    deviation_all(2)
                norm(2 * l)
                project(l)
                if l == 0:
                    pool()
                attention(l)
                if l == 0:
                    subln()
                mixed(l)
                project_out(l)
                deviation_all(2 * l + 1)
                norm(2 * l + 1)
                choose(l)
                turn_choices(l)
                build(l)
                experts(l)

        @block.vector
        def _(dve):
            st = Steps(sem("dve_step"))

            def settle():
                dve.wait_ge(st.sem, st.n)

            def modulation(l, i):
                n = 2 * ADA_BODY
                dve.wait_ge(sem(f"mod_turned{l}"), i * ADA_BODY + (ADA_BODY + 2))
                adab = small_of("ada_b", 48 * l, 48 * l + 48)[:, ds(i * n, n)]
                dve.tensor_tensor(mod[:, l, ds(i * n, n), :], bank[7][:, 0:2 * n].rearrange("p (j s) -> p j s", s=2),
                                  adab.rearrange("p (j s) -> p j s", s=1).broadcast_to([P, n, 2]),
                                  ALU.add).then_inc(sem(f"mod_evac{l}"), 1)

            def gains(l):
                dve.wait_ge(sem(f"mod_evac{l}"), 3)
                for w in range(2):
                    g = small_of("norm", KT * (2 * l + w), KT * (2 * l + w) + KT)
                    g = g.rearrange("p (j s) -> p j s", s=1).broadcast_to([P, KT, 2])
                    part = 3 * w + 1
                    dve.scalar_tensor_tensor(gainmod[:, 2 * l + w], mod[:, l, part * KT:part * KT + KT, :], 1.0, g,
                                             ALU.add, ALU.mult).then_inc(*st.inc())
                settle()

            def inverse_deviation(q):
                c0, rstd = (0 if q < 3 else NCTX), tmp[2]
                dve.wait_ge(sem("nstd"), q + 1)
                dve.reciprocal(rstd[:, c0:NT], rstd[:, c0:NT]).then_inc(*st.inc())
                settle()

            def norm(q):
                c0, l, part, rstd = (0 if q < 3 else NCTX), q // 2, 3 * (q % 2), tmp[2]

                def low(kt):
                    dve.wait_ge(sem("nhi"), KT * q + kt + 1)
                    for s, lo, hi in streams(c0):
                        last = dve.scalar_tensor_tensor(h_lo[:, kt, lo:hi], norm_t(kt)[:, lo:hi],
                                                        mod[:, l, part * KT + kt, s:s + 1], h_hi[:, kt, lo:hi],
                                                        ALU.add, ALU.subtract)
                    last.then_inc(sem("nlo"), 1)

                for kt in range(KT):
                    if kt >= 3:
                        dve.wait_ge(sem("nlo"), KT * q + kt - 2)
                    for s, lo, hi in streams(c0):
                        last = dve.scalar_tensor_tensor(norm_t(kt)[:, lo:hi], x[:, kt, lo:hi],
                                                        gainmod[:, q, kt, s:s + 1], rstd[:, lo:hi], ALU.mult, ALU.mult)
                    last.then_inc(sem("nt"), 1)
                    if kt:
                        low(kt - 1)
                low(KT - 1)

            def project(l):
                tiles, vunits = TILES[l], VUNITS[l]
                nt = len(tiles)
                dve.wait_ge(sem(f"cs_in{l}"), 16)

                def finish(j):
                    kind, rope, _, lat = tiles[j]
                    g, b, c0 = 13 * l + j - l, j % 2, NCTX if lat else 0
                    slot = sum(t[0] == kind for t in tiles[:j])
                    dst = (q_of if kind == "q" else k_of)[l][:, slot, :]
                    dlat = dst[:, 0:NLAT] if lat and l == 1 else dst[:, NCTX:NT]
                    dve.wait_ge(sem("post_std"), g + 1)
                    dve.reciprocal(std[b][:, c0:NT], std[b][:, c0:NT]).then_inc(*st.inc())
                    dve.wait_ge(sem("post_rot"), g + 1)
                    if rope:
                        dve.tensor_tensor(t1[b], qg[b][:, NCTX:NT], cos_sin[:, 0, :], ALU.mult).then_inc(*st.inc())
                        dve.tensor_tensor(t2[b], bank[4 + b][:, 0:NLAT], cos_sin[:, 1, :], ALU.mult).then_inc(*st.inc())
                        settle()
                        dve.tensor_tensor(t1[b], t1[b], t2[b], ALU.add).then_inc(*st.inc())
                        if not lat:
                            dve.tensor_tensor(dst[:, 0:NCTX], qg[b][:, 0:NCTX], std[b][:, 0:NCTX], ALU.mult)
                        settle()
                        dve.tensor_tensor(dlat, t1[b], std[b][:, NCTX:NT], ALU.mult).then_inc(sem("post_done"), 1)
                    else:
                        settle()
                        width = NT - c0
                        dve.tensor_tensor(dst[:, 0:width], qg[b][:, c0:NT], std[b][:, c0:NT],
                                          ALU.mult).then_inc(sem("post_done"), 1)

                for c in range(IN_CH[l]):
                    split_lo(dve, M0["in", l] + c + 1)
                    for j in (2 * c, 2 * c + 1):
                        if j < nt and j:
                            finish(j - 1)
                    if vunits[0][0] == c:
                        finish(nt - 1)

            def attention(l):
                units, base = attention_units(l), 24 * l
                if l == 1:
                    dve.wait_ge(sem("bias_in"), 16)
                    mask = small_of("namask").rearrange("p (a k) -> p a k", a=1).broadcast_to([P, 64, 64])
                    biasv = view(A_BIAS, 64, 64)
                    dve.tensor_tensor(biasv, biasv, mask, ALU.add).then_inc(*st.inc())
                    settle()

                def maxima(u):
                    nk, bj, stt = units[u][2], units[u][5], stats[:, u % 2, :]
                    for i in range(2):
                        dve.wait_ge(sem("scores_done"), 2 * (base + u) + i + 1)
                        s = bank[2 * (u % 2) + i]
                        if bj is not None:
                            dve.tensor_tensor(s[:, NCTX:NT], s[:, NCTX:NT], na_bias[:, bj[i], :],
                                              ALU.add).then_inc(*st.inc())
                            settle()
                        dve.tensor_reduce(stt[:, i:i + 1], s[:, 0:nk], AX_X, ALU.max, negate=True)\
                           .then_inc(sem("max_done"), 1)

                def probs(u):
                    nk, stt = units[u][2], stats[:, u % 2, :]
                    e = [tmp[2 * (u % 2) + i][:, 0:nk] for i in range(2)]
                    dve.wait_ge(sem("exp_done"), 2 * (base + u) + 2)
                    dve.reciprocal(stt[:, 4:6], stt[:, 2:4]).then_inc(*st.inc())
                    settle()
                    if l == 0:
                        dve.tensor_scalar(stt[:, 6:7], stt[:, 5:6], lamv[:, 4:5], None, ALU.mult).then_inc(*st.inc())
                        dve.tensor_scalar(e[0], e[0], stt[:, 4:5], None, ALU.mult).then_inc(*st.inc())
                        settle()
                        dve.scalar_tensor_tensor(e[0], e[1], stt[:, 6:7], e[0], ALU.mult, ALU.add)\
                           .then_inc(sem("probs_done"), 1)
                    else:
                        for i in range(2):
                            last = dve.tensor_scalar(e[i], e[i], stt[:, 4 + i:5 + i], None, ALU.mult)
                        last.then_inc(sem("probs_done"), 1)

                def heads(u):
                    j, qc = units[u][:2]
                    dve.wait_ge(sem("heads_done"), base + u + 1)
                    dve.tensor_copy(q_of[l][:, j, qc:qc + P], bank[6 + u % 2][:, 0:P]).then_inc(sem("heads_evac"), 1)

                maxima(0)
                for u in range(len(units)):
                    if u + 1 < len(units):
                        maxima(u + 1)
                    probs(u)
                    if u >= 2:
                        heads(u - 2)
                heads(len(units) - 2)
                heads(len(units) - 1)

            def subln():
                for h in range(6):
                    dve.wait_ge(sem("sub_std"), h + 1)
                    dve.reciprocal(std[h % 2], std[h % 2]).then_inc(*st.inc())
                    settle()
                    dve.scalar_tensor_tensor(q_of[0][:, h, :], q_of[0][:, h, :], sub8[:, 0:1], std[h % 2], ALU.mult,
                                             ALU.mult).then_inc(sem("sub_done"), 1)

            def mixed(l):
                c0 = first_col(l, True)
                for kt in range(KT):
                    dve.wait_ge(sem("yhi"), KT * l + kt + 1)
                    dve.tensor_tensor(h_lo[:, kt, c0:NT], mixer_out(l, kt), h_hi[:, kt, c0:NT],
                                      ALU.subtract).then_inc(sem("ylo"), 1)

            def residual(src, l, part, dt, c0):
                for s, lo, hi in streams(c0):
                    last = dve.scalar_tensor_tensor(x[:, dt, lo:hi], src(lo, hi),
                                                    mod[:, l, part * KT + dt, s:s + 1], x[:, dt, lo:hi], ALU.mult, ALU.add)
                return last

            def project_out(l):
                c0 = first_col(l, True)
                for c in range(OUT_CH):
                    if c + 1 < OUT_CH:
                        split_lo(dve, M0["out", l] + c + 1)
                    for dt in (2 * c, 2 * c + 1):
                        if dt % 2:
                            dve.wait_ge(sem("split_used"), M0["out", l] + c + 1)
                        else:
                            dve.wait_ge(sem("out_in"), 4 * l + c + 1)
                        residual(lambda lo, hi: bank[dt % 2][:, lo:hi], l, 2, dt, c0).then_inc(sem("out_evac"), 1)

            def choose(l):
                tokens = NT - first_col(l, True)
                ntt = tokens // P
                m0 = M0["wq", l]
                rep, cand, crep = view(A_REP, 4, KEYS), view(A_CAND, 4, N_CAND), view(A_CREP, 4, N_CAND)
                eq = masks(ntt)
                sv = view(A_SMALL, 4, 2, TOPK)
                tv = view(A_SMALL + 256, 4, TOPK)
                tp = view(A_SMALL + 320, 64).bitcast(U32).rearrange("p (t k) -> p t k", t=4)
                pab = [view(A_SMALL + 384 + 64 * a, 64).bitcast(U32) for a in range(2)]
                gsum = view(A_SMALL + 512, 4)
                gd = [view(A_SMALL + 576 + 64 * b, 4, TOPK)[:, 0:ntt, :] for b in range(2)]
                idxg = view(A_IDXG, 3, 4, P)
                ts = Steps(sem(f"tk_step{l}"))

                def top16(src, again, vals, idxs, after_reads=None):
                    for tt in range(ntt):
                        dve.max(vals(tt)[:, 0:8], src(tt)).then_inc(*ts.inc())
                    dve.wait_ge(ts.sem, ts.n)
                    for tt in range(ntt):
                        dve.max_index(idxs(tt)[:, 0:8], vals(tt)[:, 0:8], src(tt)).then_inc(*ts.inc())
                        dve.match_replace(again(tt), vals(tt)[:, 0:8], src(tt), NEG).then_inc(*ts.inc())
                    dve.wait_ge(ts.sem, ts.n)
                    for tt in range(ntt):
                        last = dve.max(vals(tt)[:, 8:16], again(tt)).then_inc(*ts.inc())
                    if after_reads is not None:
                        dve.tensor_copy(gate[:], ones[:, 0:1]).then_inc(after_reads, 1)
                    dve.wait_ge(ts.sem, ts.n)
                    for tt in range(ntt):
                        dve.max_index(idxs(tt)[:, 8:16], vals(tt)[:, 8:16], again(tt)).then_inc(*ts.inc())

                def finish(h, i):
                    g, col = gd[h % 2], ds(i * 64 + TOPK * h, TOPK)
                    dve.wait_ge(sem(f"gexp_done{l}"), i * 4 + (h + 1))
                    dve.tensor_reduce(gsum[:, 0:ntt], g, AX_X, ALU.add).then_inc(*ts.inc())
                    dve.wait_ge(sem(f"picked{l}"), i * 4 + (h + 1))
                    for a in range(2):
                        dve.tensor_reduce(idxg[:, a, 0:ntt, col], eq[h % 2][a].rearrange("p (t k) a -> p t k a", t=ntt),
                                          AX_X, ALU.add)
                    dve.wait_ge(ts.sem, ts.n)
                    dve.reciprocal(gsum[:, 0:ntt], gsum[:, 0:ntt]).then_inc(*ts.inc())
                    dve.wait_ge(ts.sem, ts.n)
                    dve.tensor_tensor(idxg[:, 2, 0:ntt, col], g,
                                      gsum[:, 0:ntt].rearrange("p (t k) -> p t k", k=1)
                                      .broadcast_to([P, ntt, TOPK]), ALU.mult).then_inc(sem(f"chosen{l}"), 1)

                dve.sem_inc(sem(f"sc_free{l}"), 2)
                if l == 0:
                    dve.sem_inc(sem("mod_evac1"), 1)
                with dve.Fori(0, 2) as i:
                    dve.sem_clear(ts.sem)
                    ts.restart()
                    for h in range(4):
                        for p in range(2):
                            j = 2 * h + p
                            dve.wait_ge(sem(f"sc_done{l}"), i * 8 + (j + 1 + 2))
                            dve.tensor_copy(gate[:], ones[:, 0:1])
                            top16(lambda tt: bank[2 + p][:, tt * P:tt * P + P], lambda tt: rep[:, tt, :],
                                  lambda tt: sv[:, tt, p, :], lambda tt: indices(h % 2)[:, tt, p, :], sem(f"sc_free{l}"))
                            dve.wait_ge(ts.sem, ts.n)
                            if h and not p:
                                finish(h - 1, i)
                        for a0, na, nb, at in ((0, A_WIDE, TOPK, 0), (A_WIDE, TOPK - A_WIDE, B_NARROW, A_WIDE * TOPK)):
                            dve.tensor_tensor(cand[:, 0:ntt, at:at + na * nb].rearrange("p t (a b) -> p t a b", b=nb),
                                              sv[:, 0:ntt, 0, a0:a0 + na].rearrange("p t (a b) -> p t a b", b=1)
                                              .broadcast_to([P, ntt, na, nb]),
                                              sv[:, 0:ntt, 1, 0:nb].rearrange("p t (a b) -> p t a b", a=1)
                                              .broadcast_to([P, ntt, na, nb]), ALU.add).then_inc(*ts.inc())
                        dve.wait_ge(ts.sem, ts.n)
                        top16(lambda tt: cand[:, tt, :], lambda tt: crep[:, tt, :], lambda tt: tv[:, tt, :],
                              lambda tt: tp[:, tt, :])
                        dve.wait_ge(ts.sem, ts.n)
                        dve.tensor_tensor(gd[h % 2], tv[:, 0:ntt, :], tv[:, 0:ntt, 0:1].broadcast_to([P, ntt, TOPK]),
                                          ALU.subtract).then_inc(sem(f"gd_done{l}"), 1)
                        tpf = tp[:, 0:ntt, :].rearrange("p t k -> p (t k)")
                        pa, pb = (w[:, 0:ntt * TOPK] for w in pab)
                        dve.tensor_scalar(pa, tpf, 2, None, ALU.logical_shift_right).then_inc(*ts.inc())
                        dve.wait_ge(ts.sem, ts.n)
                        step = TOPK - B_NARROW
                        dve.tensor_scalar(pa, pa, A_WIDE * TOPK // 4, step, ALU.max, ALU.mult).then_inc(*ts.inc())
                        dve.wait_ge(ts.sem, ts.n)
                        dve.scalar_tensor_tensor(tpf, pa, -step * A_WIDE * TOPK // 4, tpf, ALU.add,
                                                 ALU.add).then_inc(*ts.inc())
                        dve.wait_ge(ts.sem, ts.n)
                        dve.tensor_scalar(pa, tpf, 4, None, ALU.logical_shift_right).then_inc(*ts.inc())
                        dve.tensor_scalar(pb, tpf, 15, None, ALU.bitwise_and).then_inc(*ts.inc())
                        dve.wait_ge(ts.sem, ts.n)
                        index = indices(h % 2)[:, 0:ntt]
                        dve.tensor_copy(index.bitcast(F32), index)
                        for a in range(2):
                            last = dve.tensor_tensor(eq[h % 2][a], pab[a][:, 0:ntt * TOPK].rearrange("p (k a) -> p k a", a=1)
                                                     .broadcast_to([P, ntt * TOPK, TOPK]),
                                                     iota[:, 0:TOPK].rearrange("p (k a) -> p k a", k=1)
                                                     .broadcast_to([P, ntt * TOPK, TOPK]), ALU.is_equal)
                        last.then_inc(sem(f"eq_done{l}"), 1)
                    finish(3, i)
                    if l == 0:
                        modulation(1, i)

            def build(l):
                tokens = NT - first_col(l, True)
                idxt, oh = view(A_IDXT, 3, NT), view(A_ONEHOT, 4, 8, P)
                dve.wait_ge(sem("choices_evac"), 3 * (l + 1))
                with dve.Fori(0, tokens // (2 * TL)) as i:
                    for b in range(16):
                        dve.wait_ge(sem(f"w_done{l}"), i * 16 + (b + 1))
                        at = idxt[:, 0:2, ds(i * (2 * TL) + 4 * b, 4)].rearrange("p s (t n) -> p s t n", n=1)
                        dve.tensor_tensor(oh[:, b % 4].rearrange("p (s t) n -> p s t n", s=2),
                                          iota.rearrange("p (s t n) -> p s t n", s=1, t=1).broadcast_to([P, 2, 4, P]),
                                          at.broadcast_to([P, 2, 4, P]), ALU.is_equal).then_inc(sem(f"onehots{l}"), 1)
                dve.wait_ge(sem(f"w_done{l}"), 4 + tokens // 4)

            def experts(l):
                c0 = first_col(l, True)
                T = NT - c0
                m0, acc = M0["peer", l], view(A_ACC, KT, NT)
                done = sem(f"acc_done{l}")
                dve.memset(acc, 0.0).then_inc(done, 4)

                def add(g, i, dts, m):
                    for dt in dts:
                        if dt < KT - 1:
                            dve.wait_ge(sem(f"v_done{l}"), i * 28 + (7 * g + dt + 1))
                        else:
                            dve.wait_ge(sem("split_used"), i * 8 + (m + 1))
                        dve.tensor_tensor(acc[:, dt, 0:T], acc[:, dt, 0:T], bank[4 + dt % 4][:, 0:T],
                                          ALU.add).then_inc(done, 1)

                def step(g, i):
                    split_lo(dve, m0 + 2 + 2 * g, i, 8)
                    dve.wait_ge(done, i * 32 + (8 * g + 4))
                    add(g, i, range(2), m0 + 2 + 2 * g)
                    split_lo(dve, m0 + 3 + 2 * g, i, 8)
                    add(g, i, range(2, KT), m0 + 2 + 2 * g)

                split_lo(dve, m0 + 1)
                with dve.Fori(0, GROUPS // 4 - 1) as i:
                    for g in range(4):
                        step(g, i)
                r = GROUPS // 4 - 1
                for g in range(3):
                    step(g, r)
                dve.wait_ge(done, 32 * r + 8 * 3 + 4)
                add(3, r, range(KT), m0 + 2 + 5)
                if l == 0:
                    split_lo(dve, M0["in", 1])
                dve.wait_ge(done, 32 * r + 32 + 4)
                for dt in range(KT):
                    last = residual(lambda lo, hi: acc[:, dt, lo - c0:hi - c0], l, 5, dt, c0)
                last.then_inc(sem("x_done"), 1)

            dve.wait_ge(sem("small_in"), 16)
            lam = small_of("lam")
            dve.tensor_tensor(lamv[0:HD, 0:2], lam[0:HD, 0:2], lam[0:HD, 2:4], ALU.mult).then_inc(sem("lam_prod"), 1)
            dve.tensor_scalar(sub8[:], small_of("subln"), 1.0 - LAM_INIT, None, ALU.mult).then_inc(*st.inc())
            dve.wait_ge(sem("lam_exp"), 1)
            dve.tensor_tensor(lamv[:, 5:6], lamv[:, 3:4], lamv[:, 2:3], ALU.subtract).then_inc(*st.inc())
            settle()
            dve.tensor_scalar(lamv[:, 4:5], lamv[:, 5:6], -LAM_INIT, None, ALU.add).then_inc(*st.inc())
            dve.wait_ge(sem("x_in"), 16)
            inverse_deviation(0)
            dve.sem_inc(sem("mod_evac0"), 1)
            with dve.Fori(0, 2) as i:
                modulation(0, i)
            gains(0)
            split_lo(dve, 0)
            for l in range(2):
                if l:
                    inverse_deviation(2)
                norm(2 * l)
                project(l)
                attention(l)
                if l == 0:
                    subln()
                mixed(l)
                project_out(l)
                inverse_deviation(2 * l + 1)
                norm(2 * l + 1)
                choose(l)
                if l == 0:
                    gains(1)
                build(l)
                experts(l)

        @block.gpsimd
        def _(pool):
            def load_keys(l):
                pool.wait_ge(sem("ylo"), KT * (l + 1))
                pool.dma_start(view(A_KEYS, 2048), keys[l]).then_inc(sem(f"keys_in{l}"), 16)

            def choose(l):
                m0, ntt = M0["wq", l], (NT - first_col(l, True)) // P
                eq = masks(ntt)
                pool.wait_ge(sem("lo_done"), m0)
                split_lo(pool, m0)
                with pool.Fori(0, 2) as i:
                    for h in range(4):
                        split_lo(pool, m0 + h + 1, i, 4)
                        pool.wait_ge(sem(f"eq_done{l}"), i * 4 + (h + 1))
                        index = indices(h % 2).bitcast(F32)
                        for a in range(2):
                            e4 = eq[h % 2][a].rearrange("p (t k) a -> p t k a", t=ntt)
                            last = pool.tensor_tensor(e4, e4, index[:, 0:ntt, a, :]
                                                      .rearrange("p t (k a) -> p t k a", k=1)
                                                      .broadcast_to([P, ntt, TOPK, TOPK]), ALU.mult)
                        last.then_inc(sem(f"picked{l}"), 1)

            def build(l):
                tokens = NT - first_col(l, True)
                idxt, oh = view(A_IDXT, 3, NT), view(A_ONEHOT, 4, 8, P)
                with pool.Fori(0, tokens // (2 * TL)) as i:
                    for b in range(16):
                        pool.wait_ge(sem(f"onehots{l}"), i * 16 + (b + 1))
                        second = oh[:, b % 4, 4:8, :]
                        gates = idxt[:, 2, ds(i * (2 * TL) + 4 * b, 4)].rearrange("p (t n) -> p t n", n=1)
                        pool.tensor_tensor(second, second, gates.broadcast_to([P, 4, P]),
                                           ALU.mult).then_inc(sem(f"oh_gated{l}"), 1)

            def experts(l):
                T = NT - first_col(l, True)
                ntc = T // TL
                ge, pt = view(A_GE, 2, NT), view(A_PT, 2, NT)
                pool.sem_inc(sem(f"pm_done{l}"), 2)
                pool.sem_inc(sem(f"plo_done{l}"), 2)

                def gated(e, i, wr):
                    w = e // 4
                    if e % 4 == 0:
                        pool.wait_ge(sem(f"w_in{l}_{w % 2}"), wr * 16 + 16 * (w // 2 + 1))
                    pool.wait_ge(sem(f"ge_done{l}"), i * 8 + (e + 5))
                    pool.wait_ge(sem(f"plo_done{l}"), i * 8 + (e + 1))
                    wg = view(A_WG + 2048 * (w % 2), 16, 4, TL)[:, 0:ntc, e % 4, :]
                    pool.tensor_tensor(pt[:, e % 2, 0:T].rearrange("p (a b) -> p a b", b=TL),
                                       ge[:, e % 2, 0:T].rearrange("p (a b) -> p a b", b=TL), wg,
                                       ALU.mult).then_inc(sem(f"pm_done{l}"), 1)
                    pool.wait_ge(sem(f"phi_done{l}"), i * 8 + (e + 1))
                    pool.tensor_tensor(p_lo[:, e % 4, 0:T], pt[:, e % 2, 0:T], p_hi[:, e % 4, 0:T],
                                       ALU.subtract).then_inc(sem(f"plo_done{l}"), 1)

                with pool.Fori(0, GROUPS // 4) as i:
                    for e in range(8):
                        gated(e, i, i)

            load_keys(0)
            choose(0)
            build(0)
            for c in range(2):
                pool.wait_ge(sem(f"w_out0_{c}"), 16 + 16 * (NT // (2 * TL)))
            pool.dma_start(view(A_CS, 2 * NLAT), cs).then_inc(sem("cs_in1"), 16)
            pool.dma_start(view(A_BIAS, 4096), bias).then_inc(sem("bias_in"), 16)
            experts(0)
            load_keys(1)
            choose(1)
            build(1)
            experts(1)


def constants():
    f = np.float32
    ident = np.eye(P, dtype=f)
    r = np.arange(P)
    blockones = (r[:, None] // HD == r[None, :] // HD).astype(f)
    rot = np.zeros((P, P), f)
    for m in range(P):
        if m % 32 < 16:
            rot[m, m + 16] = -1.0
        else:
            rot[m, m - 16] = 1.0
    t = np.arange(NLAT)
    inv = (f(10000.0) ** (-np.arange(16, dtype=f) / f(16))).astype(f)
    pos = np.where((r[:, None] % HD) // 32 == 0, t[None] // GRID_W, t[None] % GRID_W).astype(f)
    ang = (pos * inv[r % 16][:, None]).astype(f)
    cs = np.stack([np.cos(ang), np.sin(ang)], 1).astype(f).reshape(P, 2 * NLAT)
    poolm = np.zeros((4, 256, 256), f)
    for g, win in enumerate((2, 4, 8, 16)):
        for i in range(256):
            lo, hi = max(i - win // 2, 0), min(i + win // 2, 256)
            poolm[g, lo:hi, i] = f(1.0) / f(hi - lo)
            poolm[g, i, i] -= f(1.0)
    poolm = np.ascontiguousarray(poolm.reshape(4, 2, P, 256).transpose(2, 0, 1, 3)).reshape(P, 2048)
    qc, kc = np.arange(P)[:, None] % GRID_W, np.arange(GRID_W)[None]
    start = np.clip(qc - NA_COLS // 2, 0, GRID_W - NA_COLS)
    namask = np.where((kc >= start) & (kc < start + NA_COLS), 0.0, -1e30).astype(f)
    iota = np.broadcast_to(np.arange(P, dtype=f), (P, P))
    eps = np.broadcast_to(np.array([EPS, EPS * HD], f), (P, 2))
    return dict(ident=ident, blockones=blockones, rotT=rot.T, iota=iota, ones=np.ones((P, P), f), namask=namask,
                eps=eps), cs, poolm


def chunks_of(w):
    n = w.shape[1] // CW
    return w.reshape(KT, P, n, CW).transpose(2, 1, 0, 3).reshape(n, P, CHUNK)


def pair_heads(w, axis):
    order = np.concatenate([np.arange(h * HD, h * HD + HD) for j in range(4) for h in (j, j + 4)])
    return np.take(w, order, axis)


def lay_out(a):
    f = np.float32
    cols = lambda v: np.asarray(v).reshape(-1, P).T
    parts = []
    for what, l, _ in PARTS:
        g = lambda n: np.asarray(a[f"l{l}_{n}"])
        if what == "ada":
            parts.append(chunks_of(g("ada_w")))
        elif what == "in":
            w = g("w_in")
            if l == 0:
                w = np.concatenate([w[:, 256:], w[:, :256]], 1)
            else:
                cq, ck, cv, nq, nk, nv = np.split(w, [512, 640, 768, 1280, 1792], 1)
                w = np.concatenate([pair_heads(cq, 1), nq, ck, nk, cv, nv], 1)
            parts.append(chunks_of(w))
        elif what == "out":
            w = g("w_out")
            if l == 1:
                w = np.concatenate([pair_heads(w[:512], 0), w[512:]], 0)
            parts.append(chunks_of(w))
        elif what == "wq":
            w = chunks_of(g("peer_wq"))
            if l == 0:
                ada = chunks_of(np.asarray(a["l1_ada_w"])).reshape(HEADS, ADA_HEAD, P, CHUNK)
                w = np.concatenate([w[:, None], ada], 1).reshape(-1, P, CHUNK)
            parts.append(w)
        else:
            u = g("peer_u").reshape(P, GROUPS, 2, KT, P).transpose(1, 4, 3, 2, 0).reshape(GROUPS, P, CHUNK)
            v = g("peer_v").reshape(P, GROUPS, 2, D).transpose(1, 0, 2, 3).reshape(GROUPS, P, CHUNK)
            order = np.empty((PEER_CH, P, CHUNK), f)
            order[0] = u[0]
            order[1:PEER_CH - 1:2] = u[1:]
            order[2:PEER_CH - 1:2] = v[:-1]
            order[PEER_CH - 1] = v[-1]
            parts.append(order)
    stream = np.concatenate(parts, 0)
    x = np.concatenate([np.asarray(a["ctx"])[0], np.asarray(a["x"])[0]], 0)
    xT = np.ascontiguousarray(x.T.reshape(KT, P, NT).transpose(1, 0, 2))
    consts, cs, poolm = constants()
    c2 = np.stack([np.asarray(a["c"])[0], np.asarray(a["c_ctx"])], 1)
    lam = np.zeros((P, 4), f)
    for i, n in enumerate(("q1", "q2", "k1", "k2")):
        lam[:HD, i] = a[f"l0_lambda_{n}"]
    twice = lambda v: np.concatenate([v, v])
    pw = np.asarray(a["l0_pool_w"]).reshape(2, 2, HD, HD).transpose(1, 2, 0, 3).reshape(P, 2 * HD)
    fields = dict(
        consts,
        c=c2.reshape(KT, P, 2).transpose(1, 0, 2).reshape(P, KT * 2),
        ada_b=np.concatenate([cols(a["l0_ada_b"]), cols(a["l1_ada_b"])], 1),
        norm=np.concatenate([cols(a[n]) for n in ("l0_norm1", "l0_norm2", "l1_norm1", "l1_norm2")], 1),
        gain=np.stack([twice(np.asarray(a[n])) for n in ("l0_diff_qnorm", "l0_diff_knorm", "l1_gqa_qnorm", "l1_gqa_knorm",
                                                         "l1_na_qnorm", "l1_na_knorm")], 1),
        subln=np.asarray(a["l0_diff_subln"])[:, None], pscale=cols(a["l0_pool_scale"]), poolw=pw, lam=lam)
    small = np.concatenate([np.asarray(fields[n], f).reshape(P, w) for n, w in SMALL_SIZES], 1)
    keys = np.stack([np.asarray(a[f"l{l}_peer_keys"]).reshape(16, KEYS, P).transpose(2, 0, 1).reshape(P, 2048)
                     for l in range(2)])
    t = np.arange(NLAT)
    dr = t[None] // GRID_W - t[:, None] // GRID_W + 7
    dc = t[None] % GRID_W - t[:, None] % GRID_W + NA_COLS - 1
    far = (dc < 0) | (dc > 2 * NA_COLS - 2)
    rpb = np.asarray(a["l1_na_rpb"])[:, dr, np.where(far, 0, dc)]
    rpb = np.where(far[None], f(0), rpb)
    bias = rpb.reshape(8, 2, P, 256).transpose(2, 0, 1, 3).reshape(P, 4096)
    return dict(xT=xT, small=small, stream=stream, poolm=poolm, cs=cs, bias=np.ascontiguousarray(bias),
                keys=np.ascontiguousarray(keys))


def kernel(**inputs):
    import concourse.bacc as bacc
    from concourse.bass_utils import run_bass_kernel_spmd

    arrays = {k: np.ascontiguousarray(v) for k, v in lay_out(inputs).items()}
    nc = bacc.Bacc("TRN2", target_bir_lowering=False, num_devices=1)
    args = {k: nc.dram_tensor(k, v.shape, F32, kind="ExternalInput").ap() for k, v in arrays.items()}
    out = nc.dram_tensor("y", (P, KT, NLAT), F32, kind="ExternalOutput").ap()
    backbone(nc, **args, out=out)
    r = run_bass_kernel_spmd(nc, [arrays], core_ids=[0])
    y = r.results[0]["y"]
    return np.ascontiguousarray(y.transpose(2, 1, 0)).reshape(1, NLAT, D)
```

```python
from contextlib import ExitStack

import numpy as np

import concourse.bass as bass
from concourse import mybir

F32 = mybir.dt.float32
F32R = mybir.dt.float32r
U32 = mybir.dt.uint32
ALU = mybir.AluOpType
ACT = mybir.ActivationFunctionType
AX_X = mybir.AxisListType.X
ds = bass.ds

P = 128
D = 1024
KT = D // P
NCTX, NLAT = 256, 256
NT = NCTX + NLAT
HD = 64
EPS = 1e-6
LAM_INIT = 0.2
HEADS = 8
KEYS = 128
TOPK = 16
NEG = -3.0e38

CW = 256
CHUNK = KT * CW
RAW = 4
ADA_CH = 6 * D // CW
IN_CH = (10, 9)
OUT_CH = D // CW
WQ_CH = HEADS
PEER_CH = 128
GROUPS = PEER_CH // 2

PARTS = [("ada", 0, ADA_CH), ("in", 0, IN_CH[0]), ("out", 0, OUT_CH), ("wq", 0, WQ_CH), ("peer", 0, PEER_CH),
         ("in", 1, IN_CH[1]), ("out", 1, OUT_CH), ("wq", 1, WQ_CH), ("peer", 1, PEER_CH)]
ADA_BODY = ADA_CH // 2
ADA_ROUNDS = 4 * (1 + ADA_CH // HEADS) // RAW
ADA_HEAD = ADA_CH // HEADS
N0, M0, KIND = {}, {}, []
_m = 0
for _what, _l, _k in PARTS:
    N0[_what, _l], M0[_what, _l] = len(KIND), _m
    for _j in range(_k):
        KIND.append((_what, _l, _j))
        if (_what, _l) == ("wq", 0):
            KIND += [("ada", 1, ADA_HEAD * _j + _i) for _i in range(ADA_HEAD)]
    _m += 0 if _what == "ada" else _k
N_CHUNKS = len(KIND)
N_OF_M = [n for n, k in enumerate(KIND) if k[0] != "ada"]
N_OF_ADA = [[n for n, k in enumerate(KIND) if k[:2] == ("ada", l)] for l in range(2)]

SMALL_SIZES = [("c", KT * 2), ("ada_b", 2 * 48), ("norm", 4 * KT), ("gain", 6), ("subln", 1), ("pscale", 2),
               ("poolw", 2 * HD), ("lam", 4), ("ident", P), ("blockones", P), ("rotT", P), ("iota", P),
               ("ones", P), ("namask", 64), ("eps", 2)]
SMALL, _at = {}, 0
for _n, _w in SMALL_SIZES:
    SMALL[_n] = (_at, _at + _w)
    _at += _w
SMALL_W = _at

ARENA = 18432
A_Q, A_K0, A_V0, A_U, A_YP = 0, 3072, 6144, 9216, 10240
A_K1, A_V1, A_BIAS = 2048, 4608, 7168
A_CS, A_TMP, A_POOLM = 11264, 11776, 15872
A_QJ, A_KEYS, A_REP, A_CAND, A_CREP, A_EQ = 0, 1024, 3072, 3584, 4608, 5632
A_SMALL, A_IDXG, A_IDXT = 7680, 8704, 10240
A_WCH, A_CUR, A_ONEHOT = 0, 8192, 11776
A_WG, A_W2, A_ACC, A_GE, A_PT = 0, 4096, 12288, 16384, 17408
A_REP1, A_EQ1 = 5120, 16384
A_WIDE, B_NARROW = 3, 4
N_CAND = A_WIDE * TOPK + (TOPK - A_WIDE) * B_NARROW
TL = 32
NA_COLS, GRID_W = 16, 64

TILES = {
    0: [("q", True, 0, False)] * 6 + [("k", True, 1, False)] * 6,
    1: [("q", True, 2, True)] * 4 + [("q", False, 4, True)] * 4 + [("k", True, 3, False)] + [("k", False, 5, False)] * 4,
}
VUNITS = {
    0: [(6, 0, 256, 0, False), (7, 0, 256, 256, False), (8, 0, 256, 512, False), (9, 0, 256, 0, True)],
    1: [(6, 128, 128, 0, False), (7, 0, 256, 128, False), (8, 0, 256, 384, False)],
}


UNITS, DONE = {}, {}
_post = _v = 0
for _l in range(2):
    for _c in range(IN_CH[_l]):
        _units = [("t", _j) for _j in (2 * _c, 2 * _c + 1) if _j < len(TILES[_l])]
        _units += [("v", _j) for _j, _u in enumerate(VUNITS[_l]) if _u[0] == _c]
        UNITS[_l, _c] = _units
        for _w, _j in _units:
            for _tt in range(1 if _w == "t" else 4):
                if (_w, _j) == _units[-1] and _tt == (0 if _w == "t" else 3):
                    DONE[_l, _w, _j, _tt] = ("split_used", M0["in", _l] + _c + 1)
                elif _w == "t":
                    _post += 1
                    DONE[_l, _w, _j, _tt] = ("post_in", _post)
                else:
                    _v += 1
                    DONE[_l, _w, _j, _tt] = ("v_in", _v)


class Steps:

    def __init__(self, sem):
        self.sem, self.n = sem, 0

    def inc(self):
        self.n += 1
        return self.sem, 1

    def restart(self):
        self.n = 0


def backbone(nc, xT, small, stream, poolm, cs, bias, keys, out):
    with ExitStack() as ctx:
        def sb(name, shape, dt=F32):
            return ctx.enter_context(nc.sbuf_tensor(name, shape, dt))

        sems = {}

        def sem(name):
            if name not in sems:
                sems[name] = ctx.enter_context(nc.semaphore(name))
            return sems[name]

        wdram = nc.dram_tensor("gate_matrix", (P, NT // TL, KEYS, TL), F32, kind="Internal").ap()

        x = sb("x", [P, KT, NT])
        h_hi = sb("h_hi", [P, KT, NT], F32R)
        h_lo = sb("h_lo", [P, KT, NT], F32R)
        raw = sb("raw", [P, RAW, CHUNK])
        w_hi = sb("w_hi", [P, 2, CHUNK], F32R)
        w_lo = sb("w_lo", [P, 2, CHUNK], F32R)
        p_hi = sb("p_hi", [P, 4, NT], F32R)
        p_lo = sb("p_lo", [P, 4, NT], F32R)
        sm = sb("sm", [P, SMALL_W])
        mod = sb("mod", [P, 2, 48, 2])
        gainmod = sb("gainmod", [P, 4, KT, 2])
        silu_c = sb("silu_c", [P, KT, 2])
        lamv = sb("lamv", [P, 8])
        sub8 = sb("sub8", [P, 1])
        ada_row = sb("ada_row", [2, 2, CW])
        stats = sb("stats", [P, 2, 8])
        gate = sb("gate", [P, 2])
        sub_ss = sb("sub_ss", [P, 24])[:]
        sub_dev = sb("sub_dev", [P, 24])[:]
        arena_at = (nc.sbuf_base + 31) // 32 * 32
        arena = sb("arena", [P, ARENA])
        w_more = nc.alloc_sbuf_tensor_at("w_more", [P, 4, CHUNK], F32R, offset=arena_at + 4 * A_W2)
        bank = [ctx.enter_context(nc.psum_tensor(f"bank{i}", [P, 512], F32)) for i in range(8)]

        def view(at, *shape):
            n = int(np.prod(shape))
            v = arena[:, at:at + n]
            if len(shape) == 2:
                v = v.rearrange("p (a b) -> p a b", a=shape[0])
            elif len(shape) == 3:
                v = v.rearrange("p (a b c) -> p a b c", a=shape[0], b=shape[1])
            return v

        def small_of(name, a=0, b=None):
            lo, hi = SMALL[name]
            return sm[:, lo + a:(hi if b is None else lo + b)]

        ident, blockones, rotT, iota, ones = (small_of(n) for n in ("ident", "blockones", "rotT", "iota", "ones"))
        c_in = small_of("c").rearrange("p (a s) -> p a s", s=2)
        rw = [raw[:, s, :].rearrange("p (k n) -> p k n", k=KT) for s in range(RAW)]
        wsplit = [(w_hi[:, s, :], w_lo[:, s, :]) for s in range(2)]
        wsplit += [(w_more[:, 2 * s, :], w_more[:, 2 * s + 1, :]) for s in (1, 0)]
        wk = [tuple(w.rearrange("p (k n) -> p k n", k=KT) for w in pair) for pair in wsplit]

        tmp = [view(A_TMP + 512 * i, 512) for i in range(8)]
        sq, qg, std = tmp[0:2], tmp[2:4], tmp[4:6]
        t1, t2 = [tmp[6][:, 0:256], tmp[6][:, 256:512]], [tmp[7][:, 0:256], tmp[7][:, 256:512]]
        cos_sin = view(A_CS, 2, NLAT)
        q_of = {0: view(A_Q, 6, NT), 1: view(A_Q, 8, NLAT)}
        k_of = {0: view(A_K0, 6, NT), 1: view(A_K1, 5, NT)}
        v_of = {0: view(A_V0, 4, 768), 1: view(A_V1, 4, 640)}
        u_tok, y_pool, pool_m = view(A_U, 4, 256), view(A_YP, 2, NT), view(A_POOLM, 4, 2, 256)
        na_bias = view(A_BIAS, 16, 256)

        STREAMS = ((0, NCTX, NT), (1, 0, NCTX))

        def streams(c0):
            return [s for s in STREAMS if s[1] >= c0]

        def first_col(l, peer):
            return NCTX if l == 1 else 0

        def slot_of(m):
            for l in range(2):
                k = m - M0["peer", l]
                if 0 <= k < PEER_CH and k // 2 % 2:
                    return 2 + k % 2
            return m % 2

        def chunk_ready(eng, n, i=0):
            eng.wait_ge(sem(f"raw_ready{n % RAW}"), i * 16 + 16 * (n // RAW + 1))

        def split_hi(act, m, i=0, per=0, rounds=None):
            chunk_ready(act, N_OF_M[m], i * (per // RAW if rounds is None else rounds))
            back = 4 if any(2 <= m - M0["peer", l] < PEER_CH for l in range(2)) else 2
            if m >= back:
                act.wait_ge(sem("split_used"), i * per + (m - back + 1))
            act.activation(wsplit[slot_of(m)][0], raw[:, N_OF_M[m] % RAW, :], ACT.Copy).then_inc(sem("hi_done"), 1)

        def split_lo(eng, m, i=0, per=0):
            eng.wait_ge(sem("hi_done"), i * per + (m + 1))
            hi, lo = wsplit[slot_of(m)]
            eng.tensor_tensor(lo, raw[:, N_OF_M[m] % RAW, :], hi, ALU.subtract).then_inc(sem(f"lo_done{m % 2}"), 1)

        def lo_ready(eng, m, i=0, per=0):
            eng.wait_ge(sem(f"lo_done{m % 2}"), i * (per // 2) + (m // 2 + 1))

        def split_ready(pe, m, i=0, per=0):
            lo_ready(pe, m, i, per)

        def mm3(pe, dst, pairs):
            last = None
            for k, ((ah, al), (bh, bl)) in enumerate(pairs):
                pe.matmul(dst, ah, bh, start=(k == 0), stop=False)
                pe.matmul(dst, al, bh, start=False, stop=False)
                last = pe.matmul(dst, ah, bl, start=False, stop=(k == len(pairs) - 1))
            return last

        def feature_tile(pe, dst, slot, col, c0, come=None):
            for k in range(KT):
                if come is not None:
                    pe.wait_ge(sem(come[0]), come[1] + k + 1)
                ah, al = (w[:, k, col:col + P] for w in wk[slot])
                pe.matmul(dst, ah, h_hi[:, k, c0:NT], start=(k == 0), stop=False)
                pe.matmul(dst, al, h_hi[:, k, c0:NT], start=False, stop=False)
                last = pe.matmul(dst, ah, h_lo[:, k, c0:NT], start=False, stop=(k == KT - 1))
            return last

        def norm_t(kt):
            return tmp[3 + kt % 3]

        def mixer_out(l, kt):
            if l == 1:
                return q_of[1][:, kt, :]
            return y_pool[:, kt, :] if kt < 2 else q_of[0][:, kt - 2, :]

        def masks(ntt):
            return [[view(at + 1024 * a, 64, TOPK)[:, 0:ntt * TOPK, :] for a in range(2)] for at in (A_EQ, A_EQ1)]

        def indices(b):
            return view(A_SMALL + 704 + 128 * b, 128).bitcast(U32).rearrange("p (t s k) -> p t s k", t=4, s=2)

        def attention_units(l):
            if l == 0:
                return [(h, c, NT if c >= NCTX else NCTX, h, (P * h,), None)
                        for h in range(6) for c in (NCTX, NCTX + P, 0, P)]
            units = [(j, c, NT, 0, (0, HD), None) for j in range(4) for c in (0, P)]
            return units + [(4 + j, P * b, NT, 1 + j, (P + P * j, P + P * j + HD), (4 * j + b, 4 * j + 2 + b))
                            for j in range(4) for b in range(2)]

        block = ctx.enter_context(nc.Block())

        @block.sync
        def _(sp):
            def raw_free(n, i=0, per=0):
                what, l, j = KIND[n - RAW]
                if what == "ada":
                    sp.wait_ge(sem("ada_used"), i * per + (ADA_CH * l + j + 1))
                else:
                    lo_ready(sp, M0[what, l] + j, i, per)

            def load(n, i=0, per=0):
                if n >= RAW:
                    raw_free(n, i, per)
                src = stream[n] if isinstance(i, int) else stream[ds(i * per + n, 1)].rearrange("a p n -> (a p) n")
                sp.dma_start(raw[:, n % RAW, :], src).then_inc(sem(f"raw_ready{n % RAW}"), 16)

            sp.dma_start(sm[:], small).then_inc(sem("small_in"), 16)
            sp.dma_start(x[:], xT).then_inc(sem("x_in"), 16)
            for n in range(RAW):
                load(n)
            sp.dma_start(view(A_CS, 2 * NLAT), cs).then_inc(sem("cs_in0"), 16)
            sp.dma_start(view(A_POOLM, 2048), poolm).then_inc(sem("poolm_in"), 16)
            with sp.Fori(0, ADA_CH // RAW - 1) as i:
                for k in range(RAW):
                    load(RAW + k, i, RAW)
            wq0 = N0["wq", 0]
            for n in range(ADA_CH, wq0 + 1):
                load(n)
            for h in range(HEADS):
                load(wq0 + (1 + ADA_HEAD) * (h + 1))
                for k in range(ADA_HEAD):
                    load(wq0 + (1 + ADA_HEAD) * h + 1 + k)

            def peer(l):
                n0 = N0["peer", l]
                tokens = NT - first_col(l, True)
                for n in range(n0 if l else n0 + 1, n0 + RAW):
                    load(n)

                def piece_out(c, i):
                    sp.wait_ge(sem(f"w_evac{l}"), i * 16 + (4 + 8 * c + 8))
                    sp.dma_start(wdram[:, ds(i * 2 + c, 1)].rearrange("p a b c -> p (a b c)"),
                                 view(A_WCH + 4096 * c, 4096)).then_inc(sem(f"w_out{l}_{c}"), 16)

                def gates(w, b):
                    ntc = tokens // TL
                    sp.dma_start(view(A_WG + 2048 * b, 16, 4 * TL)[:, 0:ntc, :],
                                 wdram[:, 0:ntc, ds(w * 4, 4), :].rearrange("p a b c -> p a (b c)"))\
                      .then_inc(sem(f"w_in{l}_{b}"), 16)

                rounds = tokens // (2 * TL)
                with sp.Fori(0, rounds - 1) as i:
                    for c in range(2):
                        piece_out(c, i)
                load(n0 + RAW)
                piece_out(0, rounds - 1)
                last, held = wdram[:, 2 * rounds - 1], view(A_WCH + 4096, KEYS, TL)
                sp.wait_ge(sem(f"w_evac{l}"), 16 * rounds + 4)
                sp.dma_start(last[:, 0:8], held[:, 0:8, :]).then_inc(sem(f"w_head{l}"), 16)
                sp.wait_ge(sem(f"w_head{l}"), 16)
                sp.wait_ge(sem(f"w_out{l}_0"), 16 * rounds + 16)
                sp.wait_ge(sem(f"w_out{l}_1"), 16 * rounds)
                gates(0, 0)
                sp.dma_start(last[:, 8:KEYS], held[:, 8:KEYS, :]).then_inc(sem(f"w_out{l}_1"), 16)
                gates(1, 1)
                sp.wait_ge(sem(f"w_out{l}_1"), 16 * rounds + 16)
                with sp.Fori(0, GROUPS // 4 - 1) as i:
                    for half in range(2):
                        for k in range(4):
                            load(n0 + RAW + 1 + 4 * half + k, i, 8)
                        sp.wait_ge(sem(f"pm_done{l}"), i * 8 + (2 + 4 * half + 4))
                        gates(i * 2 + (2 + half), half)
                for n in range(n0 + PEER_CH - 3, n0 + PEER_CH):
                    load(n)

            peer(0)
            for n in range(N0["in", 1], N0["peer", 1]):
                load(n)
            peer(1)
            for half in range(2):
                tiles = slice(KT // 2 * half, KT // 2 * (half + 1))
                sp.wait_ge(sem("x_done"), KT + KT // 2 * (half + 1))
                sp.dma_start(out[:, tiles, :], x[:, tiles, NCTX:NT]).then_inc(sem("out_done"), 16)
            sp.wait_ge(sem("out_done"), 32)

        @block.tensor
        def _(pe):
            def ada_chunk(l, c, i, rounds):
                n = N_OF_ADA[l][c]
                row = bank[6 if c % 2 else 4][0:2, 0:CW]
                chunk_ready(pe, n, i * rounds)
                pe.wait_ge(sem(f"row_evac{l}"), i * ADA_BODY + (c + 1))
                for kt in range(KT):
                    last = pe.matmul(row, silu_c[:, kt, :], rw[n % RAW][:, kt, :], start=(kt == 0), stop=(kt == KT - 1))
                last.then_inc(sem("ada_used"), 1)

            def ada_turn(l, c, i):
                if c == 0:
                    pe.wait_ge(sem(f"mod_evac{l}"), i + 1)
                pe.wait_ge(sem(f"row_evac{l}"), i * ADA_BODY + (c + 3))
                for half in range(2):
                    last = pe.matmul(bank[7][:, 4 * c + 2 * half:4 * c + 2 * half + 2],
                                     ada_row[0:2, c % 2, half * P:half * P + P], ident[0:2, 0:2], start=True, stop=True)
                last.then_inc(sem(f"mod_turned{l}"), 1)

            def ada(l):
                pe.wait_ge(sem("silu_done"), 1)
                pe.sem_inc(sem(f"mod_turned{l}"), 2)
                with pe.Fori(0, 2) as i:
                    ada_chunk(l, 0, i, ADA_BODY // RAW)
                    for c in range(1, ADA_BODY):
                        ada_chunk(l, c, i, ADA_BODY // RAW)
                        ada_turn(l, c - 1, i)
                    ada_turn(l, ADA_BODY - 1, i)

            def norm(q):
                c0 = 0 if q < 3 else NCTX
                if q == 2:
                    pe.wait_ge(sem("x_done"), 6)
                for kt in range(KT):
                    pe.wait_ge(sem("nsq"), KT * q + kt + 1)
                    pe.matmul(bank[5][:, c0:NT], ones, sq[kt % 2][:, c0:NT], start=(kt == 0),
                              stop=(kt == KT - 1)).then_inc(sem("nsq_used"), 1)

            def project(l):
                m0 = M0["in", l]
                tiles, vunits = TILES[l], VUNITS[l]
                nt = len(tiles)

                def heads_stats(j):
                    kind, rope, _, lat = tiles[j]
                    g, b, c0 = 13 * l + j - l, j % 2, NCTX if lat else 0
                    pe.wait_ge(sem("post_sq"), g + 1)
                    if j >= 2:
                        pe.wait_ge(sem("post_std"), g - 1)
                    pe.matmul(bank[2 + b][:, c0:NT], blockones, sq[b][:, c0:NT], start=True,
                              stop=True).then_inc(sem("post_ss"), 1)
                    pe.wait_ge(sem("post_qg"), g + 1)
                    if j >= 2:
                        pe.wait_ge(sem("post_done"), g - 1)
                    pe.matmul(bank[4 + b][:, 0:NLAT], rotT, qg[b][:, NCTX:NT], start=True,
                              stop=True).then_inc(sem("post_rot"), 1)

                for c in range(IN_CH[l]):
                    m = m0 + c
                    split_ready(pe, m)
                    for what, j in UNITS[l, c]:
                        if what == "t":
                            g = 13 * l + j - l
                            if j >= 2:
                                pe.wait_ge(sem("post_qg"), g - 1)
                            c0 = NCTX if tiles[j][3] else 0
                            last = feature_tile(pe, bank[j % 2][:, c0:NT], m % 2, P * (j % 2), c0,
                                                ("nlo", KT * 2 * l) if j == 0 else None)
                            last.then_inc(sem(DONE[l, "t", j, 0][0]), 1)
                            if j >= 1:
                                heads_stats(j - 1)
                        else:
                            _, col, width, _, _ = vunits[j]
                            if j == 0:
                                heads_stats(nt - 1)
                            for tt in range(4):
                                e = 16 * l + 4 * j + tt
                                if 4 * j + tt >= 2:
                                    pe.wait_ge(sem("v_evac"), e - 1)
                                tok = slice(P * tt, P * tt + P)
                                last = mm3(pe, bank[6 + tt % 2][:, 0:width],
                                           [((h_hi[:, k, tok], h_lo[:, k, tok]),
                                             (wk[m % 2][0][:, k, col:col + width], wk[m % 2][1][:, k, col:col + width]))
                                            for k in range(KT)])
                                last.then_inc(sem(DONE[l, "v", j, tt][0]), 1)

            def pool():
                pe.wait_ge(sem("v_evac"), 16)
                pe.wait_ge(sem("poolm_in"), 16)
                for pr in range(2):
                    for gi in range(2):
                        for s in range(2):
                            for tt in range(2):
                                last = pe.matmul(bank[6 + pr][HD * gi:HD * gi + HD, 256 * s:256 * s + 256],
                                                 u_tok[:, 2 * s + tt, (2 * pr + gi) * HD:(2 * pr + gi + 1) * HD],
                                                 pool_m[:, 2 * pr + gi, tt, :], start=(tt == 0), stop=(tt == 1))
                    last.then_inc(sem("pool_mean"), 1)
                poolw = small_of("poolw").rearrange("p (a b) -> p a b", a=2)
                pe.wait_ge(sem("post_done"), 12)
                for pr in range(2):
                    pe.wait_ge(sem("pool_evac"), pr + 1)
                    for gi in range(2):
                        rows = slice(HD * gi, HD * gi + HD)
                        last = pe.matmul(bank[4 + pr][rows, :], poolw[rows, pr, :], y_pool[rows, pr, :],
                                         start=True, stop=True)
                    last.then_inc(sem("pool_y"), 1)

            def attention(l):
                units, base = attention_units(l), 32 * l - 8 * l
                pe.wait_ge(sem("post_done"), 12 + 13 * l)
                pe.wait_ge(sem("v_evac"), 16 + 12 * l)
                if l == 0:
                    pe.wait_ge(sem("pool_evac"), 4)
                qv, kv, vv = q_of[l], k_of[l], v_of[l]

                def scores(u):
                    j, qc, nk, kj, _, _ = units[u]
                    if u >= 2:
                        pe.wait_ge(sem("exp_done"), 2 * (base + u - 1))
                    for i in range(2):
                        rows = slice(HD * i, HD * i + HD)
                        pe.matmul(bank[2 * (u % 2) + i][:, 0:nk], qv[rows, j, qc:qc + P], kv[rows, kj, 0:nk],
                                  start=True, stop=True).then_inc(sem("scores_done"), 1)

                def turn(u):
                    nk = units[u][2]
                    pe.wait_ge(sem("probs_done"), base + u + 1)
                    if u >= (2 if l == 0 else 1):
                        pe.wait_ge(sem("turned_evac"), base + u - 1 if l == 0 else base + u)
                    for i in range(1 + l):
                        for kb in range(nk // P):
                            dst = bank[4 + (u % 2 if l == 0 else i)][:, kb * P:kb * P + P]
                            last = pe.transpose(dst, tmp[2 * (u % 2) + i][:, kb * P:kb * P + P], ident)
                    last.then_inc(sem("turned"), 1)

                def values(u):
                    nk, cols = units[u][2], units[u][4]
                    pe.wait_ge(sem("turned_evac"), base + u + 1)
                    if u >= 2:
                        pe.wait_ge(sem("heads_evac"), base + u - 1)
                    wt = view(A_TMP + 2048 + 1024 * (u % 2), 2, 4, P)
                    for i in range(1 + l):
                        width = P if l == 0 else HD
                        for kb in range(nk // P):
                            if l == 0:
                                last = pe.matmul(bank[6 + u % 2][:, 0:P], wt[:, 0, kb, :], vv[:, kb, cols[0]:cols[0] + P],
                                                 start=(kb == 0), stop=(kb == nk // P - 1))
                                continue
                            last = pe.matmul(bank[6 + u % 2][width * i * l:width * i * l + width, 0:P],
                                             vv[:, kb, cols[i]:cols[i] + width], wt[:, i, kb, :],
                                             start=(kb == 0), stop=(kb == nk // P - 1))
                    last.then_inc(sem("heads_done"), 1)

                scores(0)
                scores(1)
                for u in range(len(units)):
                    if u + 2 < len(units):
                        scores(u + 2)
                    turn(u)
                    if u:
                        values(u - 1)
                values(len(units) - 1)

            def turn_heads():
                for h in range(6):
                    pe.wait_ge(sem("sub_diag"), h + 1)
                    if h >= 2:
                        pe.wait_ge(sem("ylo"), 2 + h - 1)
                    for qt in range(4):
                        cols = slice(P * qt, P * qt + P)
                        last = pe.matmul(bank[h % 2][:, cols], q_of[0][:, h, cols], sq[h % 2][:, cols],
                                         start=True, stop=True)
                    last.then_inc(sem("sub_turned"), 1)

            def project_out(l):
                c0 = first_col(l, True)
                for c in range(OUT_CH):
                    m = M0["out", l] + c
                    split_ready(pe, m)
                    for jj in range(2):
                        dt = 2 * c + jj
                        if dt >= 2:
                            pe.wait_ge(sem("out_evac"), KT * l + dt - 1)
                        last = feature_tile(pe, bank[2 + dt % 2][:, c0:NT], m % 2, P * jj, c0,
                                            None if dt else ("ylo", KT * l))
                        last.then_inc(sem("split_used" if jj else "out_in"), 1)

            def choose(l):
                c0 = first_col(l, True)
                tokens = NT - c0
                m0, qj = M0["wq", l], view(A_QJ, 2, NT)
                kv = view(A_KEYS, 16, KEYS)
                pe.wait_ge(sem(f"keys_in{l}"), 16)
                pe.sem_inc(sem(f"w_done{l}"), 4)
                pe.sem_inc(sem(f"sc_done{l}"), 2)
                if l == 0:
                    pe.sem_inc(sem("mod_turned1"), 2)
                with pe.Fori(0, 2) as i:
                    def query(j):
                        if j % 2 == 0:
                            split_ready(pe, m0 + j // 2, i, 4)
                        pe.wait_ge(sem(f"qj_done{l}"), i * 8 + (j + 1))
                        last = feature_tile(pe, bank[j % 2][:, 0:tokens], (m0 + j // 2) % 2, P * (j % 2), c0,
                                            ("nlo", KT * (2 * l + 1)) if j == 0 else None)
                        last.then_inc(sem("split_used" if j % 2 else f"qj_in{l}"), 1)

                    def score(j):
                        pe.wait_ge(sem(f"qj_done{l}"), i * 8 + (j + 3))
                        pe.wait_ge(sem(f"sc_free{l}"), i * 8 + (j + 1))
                        for tt in range(tokens // P):
                            last = pe.matmul(bank[2 + j % 2][:, tt * P:tt * P + P], qj[:, j % 2, tt * P:tt * P + P],
                                             kv[:, ds(i * 8 + j, 1), :].rearrange("p a b -> p (a b)"),
                                             start=True, stop=True)
                        last.then_inc(sem(f"sc_done{l}"), 1)

                    def ada_of(h):
                        for c in range(ADA_HEAD * h, ADA_HEAD * h + ADA_HEAD):
                            ada_chunk(1, c, i, ADA_ROUNDS)
                            if c:
                                ada_turn(1, c - 1, i)

                    for h in range(4):
                        query(2 * h)
                        query(2 * h + 1)
                        score(2 * h)
                        score(2 * h + 1)
                        if l == 0:
                            ada_of(h)
                    if l == 0:
                        ada_turn(1, ADA_BODY - 1, i)

            def turn_choices(l):
                ntt = (NT - first_col(l, True)) // P
                idxg = view(A_IDXG, 3, 4, P)
                pe.wait_ge(sem(f"chosen{l}"), HEADS)
                for a in range(3):
                    for tt in range(ntt):
                        last = pe.transpose(bank[4 + a][:, tt * P:tt * P + P], idxg[:, a, tt, :], ident)
                    last.then_inc(sem("choices_turned"), 1)

            def build(l):
                tokens = NT - first_col(l, True)
                oh = view(A_ONEHOT, 4, 8, P)
                with pe.Fori(0, tokens // (2 * TL)) as i:
                    for b in range(16):
                        pe.wait_ge(sem(f"oh_gated{l}"), i * 16 + (b + 1))
                        if b % 4 == 3:
                            pe.wait_ge(sem(f"oh_first{l}"), i * 4 + (b // 4 + 1))
                        pe.wait_ge(sem(f"w_evac{l}"), i * 16 + (b + 1))
                        for t in range(4):
                            last = pe.matmul(bank[4 + b % 4][:, t * P:t * P + P], oh[:, b % 4, t, :],
                                             oh[:, b % 4, 4 + t, :], start=True, stop=True)
                        last.then_inc(sem(f"w_done{l}"), 1)

            def up(l, g, i=0):
                c0 = first_col(l, True)
                m = M0["peer", l] + max(2 * g - 1, 0)
                split_ready(pe, m, i, 8)
                for a in range(2):
                    e = 2 * g + a
                    if e >= 4:
                        pe.wait_ge(sem(f"ge_done{l}"), i * 8 + (e - 3))
                    last = feature_tile(pe, bank[e % 4][:, 0:NT - c0], slot_of(m), P * a, c0)
                    last.then_inc(sem("split_used" if a else f"h_done{l}"), 1)

            def experts(l):
                c0 = first_col(l, True)
                T = NT - c0
                m0 = M0["peer", l]

                pe.wait_ge(sem(f"w_evac{l}"), 4 + T // 4)

                def down(m, g, i, mi):
                    split_ready(pe, m, mi, 8)
                    pe.wait_ge(sem(f"plo_done{l}"), i * 8 + (2 * g + 2 + 2))
                    hi, lo = wsplit[slot_of(m)]
                    for dt in range(KT):
                        pe.wait_ge(sem(f"acc_done{l}"), i * 32 + (8 * g + dt + 1))
                        cols = [slice(D * a + P * dt, D * a + P * dt + P) for a in range(2)]
                        last = mm3(pe, bank[4 + dt % 4][:, 0:T],
                                   [((hi[:, cols[a]], lo[:, cols[a]]),
                                     (p_hi[:, (2 * g + a) % 4, 0:T], p_lo[:, (2 * g + a) % 4, 0:T])) for a in range(2)])
                        last.then_inc(sem(f"v_done{l}" if dt < KT - 1 else "split_used"), 1)

                with pe.Fori(0, GROUPS // 4 - 1) as i:
                    for g in range(4):
                        down(m0 + 2 + 2 * g, g, i, i)
                        up(l, g + 2, i)
                r = GROUPS // 4 - 1
                for g in range(2):
                    down(m0 + 2 + 2 * g, g, r, r)
                    up(l, g + 2, r)
                down(m0 + 2 + 4, 2, r, r)
                down(m0 + PEER_CH - 1, 3, r, 0)

            pe.wait_ge(sem("small_in"), 16)
            pe.wait_ge(sem("lam_prod"), 1)
            pe.matmul(bank[6][:, 0:2], ones[0:HD, :], lamv[0:HD, 0:2], start=True, stop=True).then_inc(sem("lam_dot"), 1)
            norm(0)
            ada(0)
            for l in range(2):
                if l:
                    norm(2 * l)
                project(l)
                if l == 0:
                    pool()
                attention(l)
                if l == 0:
                    turn_heads()
                project_out(l)
                norm(2 * l + 1)
                choose(l)
                pe.wait_ge(sem(f"qj_done{l}"), 2 + 2 * HEADS)
                up(l, 0)
                turn_choices(l)
                build(l)
                up(l, 1)
                experts(l)

        @block.scalar
        def _(act):
            eps1, eps64 = small_of("eps", 0, 1), small_of("eps", 1, 2)

            def row(l, c, i):
                act.wait_ge(sem("ada_used"), i * ADA_BODY + (ADA_CH * l + c + 1))
                act.wait_ge(sem(f"mod_turned{l}"), i * ADA_BODY + (c + 1))
                act.activation(ada_row[0:2, c % 2, :], bank[6 if c % 2 else 4][0:2, 0:CW], ACT.Copy)\
                   .then_inc(sem(f"row_evac{l}"), 1)

            def deviation_all(q):
                c0, l, rstd = (0 if q < 3 else NCTX), q // 2, tmp[2]
                if q == 2:
                    act.wait_ge(sem("split_used"), M0["in", 1])
                for kt in range(KT):
                    if kt >= 2:
                        act.wait_ge(sem("nsq_used"), KT * q + kt - 1)
                    if q % 2:
                        act.wait_ge(sem("out_evac"), KT * l + kt + 1)
                    elif q == 2:
                        act.wait_ge(sem("x_done"), kt + 1)
                    act.activation(sq[kt % 2][:, c0:NT], x[:, kt, c0:NT], ACT.Square).then_inc(sem("nsq"), 1)
                act.wait_ge(sem("nsq_used"), KT * (q + 1))
                act.activation(rstd[:, c0:NT], bank[5][:, c0:NT], ACT.Sqrt, bias=eps1,
                               scale=1.0 / D).then_inc(sem("nstd"), 1)

            def norm(q):
                c0, l, part = (0 if q < 3 else NCTX), q // 2, 3 * (q % 2)
                for kt in range(KT):
                    act.wait_ge(sem("nt"), KT * q + kt + 1)
                    for s, lo, hi in streams(c0):
                        last = act.activation(h_hi[:, kt, lo:hi], norm_t(kt)[:, lo:hi], ACT.Identity,
                                              bias=mod[:, l, part * KT + kt, s:s + 1])
                    last.then_inc(sem("nhi"), 1)

            def project(l):
                tiles, vunits = TILES[l], VUNITS[l]
                nt = len(tiles)

                def deviation(j):
                    kind, _, _, lat = tiles[j]
                    g, b, c0 = 13 * l + j - l, j % 2, NCTX if lat else 0
                    act.wait_ge(sem("post_ss"), g + 1)
                    if j >= 2:
                        act.wait_ge(sem("post_done"), g - 1)
                    act.activation(std[b][:, c0:NT], bank[2 + b][:, c0:NT], ACT.Sqrt, bias=eps64 if kind == "q" else eps1,
                                   scale=1.0 if kind == "q" else 1.0 / HD).then_inc(sem("post_std"), 1)

                for c in range(IN_CH[l]):
                    split_hi(act, M0["in", l] + c + 1)
                    for what, j in UNITS[l, c]:
                        if what == "t":
                            _, _, gain, lat = tiles[j]
                            g, b, c0 = 13 * l + j - l, j % 2, NCTX if lat else 0
                            done, count = DONE[l, "t", j, 0]
                            act.wait_ge(sem(done), count)
                            if j >= 2:
                                act.wait_ge(sem("post_ss"), g - 1)
                            act.activation(sq[b][:, c0:NT], bank[b][:, c0:NT], ACT.Square).then_inc(sem("post_sq"), 1)
                            if j >= 2:
                                act.wait_ge(sem("post_done"), g - 1)
                                act.wait_ge(sem("post_rot"), g - 1)
                            act.activation(qg[b][:, c0:NT], bank[b][:, c0:NT], ACT.Identity,
                                           scale=small_of("gain", gain, gain + 1)).then_inc(sem("post_qg"), 1)
                            if j >= 1:
                                deviation(j - 1)
                        else:
                            _, _, width, at, is_pool = vunits[j]
                            if j == 0:
                                deviation(nt - 1)
                            for tt in range(4):
                                done, count = DONE[l, "v", j, tt]
                                act.wait_ge(sem(done), count)
                                dst = u_tok if is_pool else v_of[l]
                                act.activation(dst[:, tt, at:at + width], bank[6 + tt % 2][:, 0:width],
                                               ACT.Copy).then_inc(sem("v_evac"), 1)

            def pool():
                for pr in range(2):
                    act.wait_ge(sem("pool_mean"), pr + 1)
                    act.activation(y_pool[:, pr, :], bank[6 + pr][:], ACT.Copy).then_inc(sem("pool_evac"), 1)
                for pr in range(2):
                    act.wait_ge(sem("pool_y"), pr + 1)
                    act.activation(y_pool[:, pr, :], bank[4 + pr][:], ACT.Identity,
                                   scale=small_of("pscale", pr, pr + 1)).then_inc(sem("pool_evac"), 1)

            def attention(l):
                units, base = attention_units(l), 24 * l
                act.wait_ge(sem("post_done"), 12 + 13 * l)

                def exps(u):
                    nk, st = units[u][2], stats[:, u % 2, :]
                    if u >= 2:
                        act.wait_ge(sem("turned"), base + u - 1)
                    for i in range(2):
                        act.wait_ge(sem("max_done"), 2 * (base + u) + i + 1)
                        act.activation(tmp[2 * (u % 2) + i][:, 0:nk], bank[2 * (u % 2) + i][:, 0:nk], ACT.Exp,
                                       bias=st[:, i:i + 1], accum_out=st[:, 2 + i:3 + i]).then_inc(sem("exp_done"), 1)

                def evac(u):
                    nk = units[u][2]
                    act.wait_ge(sem("turned"), base + u + 1)
                    if u >= 2:
                        act.wait_ge(sem("heads_done"), base + u - 1)
                    for i in range(1 + l):
                        wt = view(A_TMP + 2048 + 1024 * (u % 2) + 512 * i, 512)
                        last = act.activation(wt[:, 0:nk], bank[4 + (u % 2 if l == 0 else i)][:, 0:nk], ACT.Copy)
                    last.then_inc(sem("turned_evac"), 1)

                def squares(u):
                    j, qc = units[u][:2]
                    act.wait_ge(sem("heads_evac"), u + 1)
                    at = 4 * j + qc // P
                    act.activation(h_hi[:, j, qc:qc + P], q_of[0][:, j, qc:qc + P], ACT.Square,
                                   accum_out=sub_ss[:, at:at + 1]).then_inc(sem("sub_sq"), 1)

                exps(0)
                for u in range(len(units)):
                    if u + 1 < len(units):
                        exps(u + 1)
                    evac(u)
                    if l == 0 and u >= 3:
                        squares(u - 3)
                if l == 0:
                    for u in range(len(units) - 3, len(units)):
                        squares(u)

            def mixed(l):
                c0 = first_col(l, True)
                if l == 0:
                    act.wait_ge(sem("sub_sq"), 24)
                    act.activation(sub_dev, sub_ss, ACT.Sqrt, bias=eps1, scale=1.0 / P).then_inc(sem("sub_std"), 1)
                for kt in range(KT):
                    if l == 0 and kt >= 2:
                        act.wait_ge(sem("sub_turned"), kt - 1)
                        act.activation(h_hi[:, kt, :], bank[kt % 2][:], ACT.Identity,
                                       scale=sub8[:, 0:1]).then_inc(sem("yhi"), 1)
                        continue
                    if l == 0:
                        act.wait_ge(sem("pool_evac"), 4)
                    else:
                        act.wait_ge(sem("heads_evac"), 40)
                    act.activation(h_hi[:, kt, c0:NT], mixer_out(l, kt), ACT.Copy).then_inc(sem("yhi"), 1)

            def project_out(l):
                for c in range(OUT_CH):
                    split_hi(act, M0["out", l] + c + 1)
                act.sem_inc(sem(f"qj_done{l}"), 2)

            def choose(l):
                tokens = NT - first_col(l, True)
                m0, qj = M0["wq", l], view(A_QJ, 2, NT)
                if l == 0:
                    act.sem_inc(sem("row_evac1"), 2)

                def exps(h, i):
                    gd = view(A_SMALL + 576 + 64 * (h % 2), 64)
                    act.wait_ge(sem(f"gd_done{l}"), i * 4 + (h + 1))
                    act.activation(gd[:, 0:tokens // P * TOPK], gd[:, 0:tokens // P * TOPK], ACT.Exp)\
                       .then_inc(sem(f"gexp_done{l}"), 1)

                if l == 1:
                    split_hi(act, m0 + 1)
                with act.Fori(0, 2) as i:
                    rounds = ADA_ROUNDS if l == 0 else 1
                    if l == 0:
                        split_hi(act, m0 + 1, i, 4, rounds)
                    for h in range(4):
                        for p in range(2):
                            j = 2 * h + p
                            if p:
                                act.wait_ge(sem("split_used"), i * 4 + (m0 + h + 1))
                            else:
                                act.wait_ge(sem(f"qj_in{l}"), i * 4 + (h + 1))
                            act.wait_ge(sem(f"sc_done{l}"), i * 8 + (j + 1))
                            act.activation(qj[:, p, 0:tokens], bank[p][:, 0:tokens], ACT.Copy)\
                               .then_inc(sem(f"qj_done{l}"), 1)
                        if l == 0:
                            for c in range(ADA_HEAD * h, ADA_HEAD * h + ADA_HEAD):
                                row(1, c, i)
                        if h < 3 or l == 1:
                            split_hi(act, m0 + h + 2, i, 4, rounds)
                        if h:
                            exps(h - 1, i)
                    exps(3, i)

            def turn_choices(l):
                tokens = NT - first_col(l, True)
                idxt = view(A_IDXT, 3, NT)
                for a in range(3):
                    act.wait_ge(sem("choices_turned"), 3 * l + a + 1)
                    act.activation(idxt[:, a, 0:tokens], bank[4 + a][:, 0:tokens], ACT.Copy)\
                       .then_inc(sem("choices_evac"), 1)
                if l == 0:
                    split_hi(act, M0["peer", l] + 1)

            def build(l):
                tokens = NT - first_col(l, True)
                act.sem_inc(sem(f"w_evac{l}"), 4)
                act.sem_inc(sem(f"oh_squares{l}"), 1)
                for c in range(2):
                    act.sem_inc(sem(f"w_out{l}_{c}"), 16)
                idxt, oh, cur = view(A_IDXT, 3, NT), view(A_ONEHOT, 4, 8, P), view(A_CUR, 2 * TL)

                def first_onehots(b, i):
                    act.wait_ge(sem(f"w_done{l}"), i * 16 + (b + 1))
                    for t in range(4):
                        last = act.activation(oh[:, b % 4, t, :], iota, ACT.Square, scale=-1.0,
                                              bias=cur[:, 4 * b + t:4 * b + t + 1])
                    last.then_inc(sem(f"oh_squares{l}"), 1)
                    act.wait_ge(sem(f"oh_squares{l}"), i * 4 + (b // 4 + 2))
                    act.activation(oh[:, b % 4, 0:4, :], oh[:, b % 4, 0:4, :], ACT.Relu, scale=-1.0,
                                   bias=ones[:, 0:1]).then_inc(sem(f"oh_first{l}"), 1)

                act.wait_ge(sem("choices_evac"), 3 * l + 3)
                with act.Fori(0, tokens // (2 * TL)) as i:
                    act.wait_ge(sem(f"oh_squares{l}"), i * 4 + 1)
                    act.activation(cur, idxt[:, 0, ds(i * (2 * TL), 2 * TL)], ACT.Copy).then_inc(sem(f"cur_done{l}"), 1)
                    act.wait_ge(sem(f"cur_done{l}"), i + 1)
                    for b in range(16):
                        if b % 4 == 0:
                            first_onehots(b + 3, i)
                        c = b // 8
                        if b % 8 == 0:
                            act.wait_ge(sem(f"w_out{l}_{c}"), i * 16 + 16)
                        act.wait_ge(sem(f"w_done{l}"), i * 16 + (b + 1 + 4))
                        piece = view(A_WCH + 4096 * c, KEYS, TL)[:, :, 4 * (b % 8):4 * (b % 8) + 4]
                        act.activation(piece.rearrange("p n t -> p t n"),
                                       bank[4 + b % 4][:].rearrange("p (t n) -> p t n", t=4), ACT.Copy)\
                           .then_inc(sem(f"w_evac{l}"), 1)

            def experts(l):
                T = NT - first_col(l, True)
                m0 = M0["peer", l]
                ge, pt = view(A_GE, 2, NT), view(A_PT, 2, NT)

                def gelu(e, i):
                    if e % 2:
                        act.wait_ge(sem("split_used"), i * 8 + (m0 + max(e - 2, 0) + 1))
                    else:
                        act.wait_ge(sem(f"h_done{l}"), i * 4 + (e // 2 + 1))
                    act.wait_ge(sem(f"pm_done{l}"), i * 8 + (e + 1))
                    act.activation(ge[:, e % 2, 0:T], bank[e % 4][:, 0:T], ACT.Gelu).then_inc(sem(f"ge_done{l}"), 1)
                    act.wait_ge(sem(f"pm_done{l}"), i * 8 + (e + 3))
                    act.wait_ge(sem("split_used"), i * 8 + (m0 - 1 + 2 * (e // 2)))
                    act.activation(p_hi[:, e % 4, 0:T], pt[:, e % 2, 0:T], ACT.Copy).then_inc(sem(f"phi_done{l}"), 1)

                def step(g, i):
                    if not (isinstance(i, int) and g > 1):
                        split_hi(act, m0 + 4 + 2 * g, i, 8)
                    gelu(2 * g + 2, i)
                    if not (isinstance(i, int) and g > 1):
                        split_hi(act, m0 + 5 + 2 * g, i, 8)
                    gelu(2 * g + 3, i)

                gelu(0, 0)
                split_hi(act, m0 + 2)
                gelu(1, 0)
                act.wait_ge(sem(f"w_head{l}"), 16)
                for c in range(2):
                    act.wait_ge(sem(f"w_out{l}_{c}"), 16 + 16 * (T // (2 * TL)))
                split_hi(act, m0 + 3)
                with act.Fori(0, GROUPS // 4 - 1) as i:
                    for g in range(4):
                        step(g, i)
                for g in range(3):
                    step(g, GROUPS // 4 - 1)
                if l == 0:
                    split_hi(act, M0["in", 1])

            act.wait_ge(sem("small_in"), 16)
            act.activation(silu_c[:], c_in, ACT.Silu).then_inc(sem("silu_done"), 1)
            act.wait_ge(sem("lam_dot"), 1)
            act.activation(lamv[:, 2:4], bank[6][:, 0:2], ACT.Exp).then_inc(sem("lam_exp"), 1)
            act.wait_ge(sem("x_in"), 16)
            deviation_all(0)
            act.sem_inc(sem("row_evac0"), 2)
            with act.Fori(0, 2) as i:
                for c in range(ADA_BODY):
                    row(0, c, i)
            split_hi(act, 0)
            for l in range(2):
                if l:
                    deviation_all(2)
                norm(2 * l)
                project(l)
                if l == 0:
                    pool()
                attention(l)
                mixed(l)
                project_out(l)
                deviation_all(2 * l + 1)
                norm(2 * l + 1)
                choose(l)
                turn_choices(l)
                build(l)
                experts(l)

        @block.vector
        def _(dve):
            st = Steps(sem("dve_step"))

            def settle():
                dve.wait_ge(st.sem, st.n)

            def modulation(l, i):
                n = 2 * ADA_BODY
                dve.wait_ge(sem(f"mod_turned{l}"), i * ADA_BODY + (ADA_BODY + 2))
                adab = small_of("ada_b", 48 * l, 48 * l + 48)[:, ds(i * n, n)]
                dve.tensor_tensor(mod[:, l, ds(i * n, n), :], bank[7][:, 0:2 * n].rearrange("p (j s) -> p j s", s=2),
                                  adab.rearrange("p (j s) -> p j s", s=1).broadcast_to([P, n, 2]),
                                  ALU.add).then_inc(sem(f"mod_evac{l}"), 1)

            def gains(l):
                dve.wait_ge(sem(f"mod_evac{l}"), 3)
                for w in range(2):
                    g = small_of("norm", KT * (2 * l + w), KT * (2 * l + w) + KT)
                    g = g.rearrange("p (j s) -> p j s", s=1).broadcast_to([P, KT, 2])
                    part = 3 * w + 1
                    dve.scalar_tensor_tensor(gainmod[:, 2 * l + w], mod[:, l, part * KT:part * KT + KT, :], 1.0, g,
                                             ALU.add, ALU.mult).then_inc(*st.inc())
                settle()

            def inverse_deviation(q):
                c0, rstd = (0 if q < 3 else NCTX), tmp[2]
                dve.wait_ge(sem("nstd"), q + 1)
                dve.reciprocal(rstd[:, c0:NT], rstd[:, c0:NT]).then_inc(*st.inc())
                settle()

            def norm(q):
                c0, l, part, rstd = (0 if q < 3 else NCTX), q // 2, 3 * (q % 2), tmp[2]

                def low(kt):
                    dve.wait_ge(sem("nhi"), KT * q + kt + 1)
                    for s, lo, hi in streams(c0):
                        last = dve.scalar_tensor_tensor(h_lo[:, kt, lo:hi], norm_t(kt)[:, lo:hi],
                                                        mod[:, l, part * KT + kt, s:s + 1], h_hi[:, kt, lo:hi],
                                                        ALU.add, ALU.subtract)
                    last.then_inc(sem("nlo"), 1)

                for kt in range(KT):
                    if kt >= 3:
                        dve.wait_ge(sem("nlo"), KT * q + kt - 2)
                    for s, lo, hi in streams(c0):
                        last = dve.scalar_tensor_tensor(norm_t(kt)[:, lo:hi], x[:, kt, lo:hi],
                                                        gainmod[:, q, kt, s:s + 1], rstd[:, lo:hi], ALU.mult, ALU.mult)
                    last.then_inc(sem("nt"), 1)
                    if kt:
                        low(kt - 1)
                low(KT - 1)

            def project(l):
                tiles, vunits = TILES[l], VUNITS[l]
                nt = len(tiles)
                dve.wait_ge(sem(f"cs_in{l}"), 16)

                def finish(j):
                    kind, rope, _, lat = tiles[j]
                    g, b, c0 = 13 * l + j - l, j % 2, NCTX if lat else 0
                    slot = sum(t[0] == kind for t in tiles[:j])
                    dst = (q_of if kind == "q" else k_of)[l][:, slot, :]
                    dlat = dst[:, 0:NLAT] if lat and l == 1 else dst[:, NCTX:NT]
                    dve.wait_ge(sem("post_std"), g + 1)
                    dve.reciprocal(std[b][:, c0:NT], std[b][:, c0:NT]).then_inc(*st.inc())
                    dve.wait_ge(sem("post_rot"), g + 1)
                    if rope:
                        dve.tensor_tensor(t1[b], qg[b][:, NCTX:NT], cos_sin[:, 0, :], ALU.mult).then_inc(*st.inc())
                        dve.tensor_tensor(t2[b], bank[4 + b][:, 0:NLAT], cos_sin[:, 1, :], ALU.mult).then_inc(*st.inc())
                        settle()
                        dve.tensor_tensor(t1[b], t1[b], t2[b], ALU.add).then_inc(*st.inc())
                        if not lat:
                            dve.tensor_tensor(dst[:, 0:NCTX], qg[b][:, 0:NCTX], std[b][:, 0:NCTX], ALU.mult)
                        settle()
                        dve.tensor_tensor(dlat, t1[b], std[b][:, NCTX:NT], ALU.mult).then_inc(sem("post_done"), 1)
                    else:
                        settle()
                        width = NT - c0
                        dve.tensor_tensor(dst[:, 0:width], qg[b][:, c0:NT], std[b][:, c0:NT],
                                          ALU.mult).then_inc(sem("post_done"), 1)

                for c in range(IN_CH[l]):
                    split_lo(dve, M0["in", l] + c + 1)
                    for j in (2 * c, 2 * c + 1):
                        if j < nt and j:
                            finish(j - 1)
                    if vunits[0][0] == c:
                        finish(nt - 1)

            def attention(l):
                units, base = attention_units(l), 24 * l
                if l == 1:
                    dve.wait_ge(sem("bias_in"), 16)
                    mask = small_of("namask").rearrange("p (a k) -> p a k", a=1).broadcast_to([P, 64, 64])
                    biasv = view(A_BIAS, 64, 64)
                    dve.tensor_tensor(biasv, biasv, mask, ALU.add).then_inc(*st.inc())
                    settle()

                def maxima(u):
                    nk, bj, stt = units[u][2], units[u][5], stats[:, u % 2, :]
                    for i in range(2):
                        dve.wait_ge(sem("scores_done"), 2 * (base + u) + i + 1)
                        s = bank[2 * (u % 2) + i]
                        if bj is not None:
                            dve.tensor_tensor(s[:, NCTX:NT], s[:, NCTX:NT], na_bias[:, bj[i], :],
                                              ALU.add).then_inc(*st.inc())
                            settle()
                        dve.tensor_reduce(stt[:, i:i + 1], s[:, 0:nk], AX_X, ALU.max, negate=True)\
                           .then_inc(sem("max_done"), 1)

                def probs(u):
                    nk, stt = units[u][2], stats[:, u % 2, :]
                    e = [tmp[2 * (u % 2) + i][:, 0:nk] for i in range(2)]
                    dve.wait_ge(sem("exp_done"), 2 * (base + u) + 2)
                    dve.reciprocal(stt[:, 4:6], stt[:, 2:4]).then_inc(*st.inc())
                    settle()
                    if l == 0:
                        dve.tensor_scalar(stt[:, 6:7], stt[:, 5:6], lamv[:, 4:5], None, ALU.mult).then_inc(*st.inc())
                        dve.tensor_scalar(e[0], e[0], stt[:, 4:5], None, ALU.mult).then_inc(*st.inc())
                        settle()
                        dve.scalar_tensor_tensor(e[0], e[1], stt[:, 6:7], e[0], ALU.mult, ALU.add)\
                           .then_inc(sem("probs_done"), 1)
                    else:
                        for i in range(2):
                            last = dve.tensor_scalar(e[i], e[i], stt[:, 4 + i:5 + i], None, ALU.mult)
                        last.then_inc(sem("probs_done"), 1)

                def heads(u):
                    j, qc = units[u][:2]
                    dve.wait_ge(sem("heads_done"), base + u + 1)
                    dve.tensor_copy(q_of[l][:, j, qc:qc + P], bank[6 + u % 2][:, 0:P]).then_inc(sem("heads_evac"), 1)

                maxima(0)
                for u in range(len(units)):
                    if u + 1 < len(units):
                        maxima(u + 1)
                    probs(u)
                    if u >= 2:
                        heads(u - 2)
                heads(len(units) - 2)
                heads(len(units) - 1)

            def mixed(l):
                c0 = first_col(l, True)

                def low(kt):
                    dve.wait_ge(sem("yhi"), KT * l + kt + 1)
                    if l == 0 and kt >= 2:
                        last = dve.scalar_tensor_tensor(h_lo[:, kt, :], bank[kt % 2][:], sub8[:, 0:1], h_hi[:, kt, :],
                                                        ALU.mult, ALU.subtract)
                    else:
                        last = dve.tensor_tensor(h_lo[:, kt, c0:NT], mixer_out(l, kt), h_hi[:, kt, c0:NT], ALU.subtract)
                    last.then_inc(sem("ylo"), 1)

                if l == 0:
                    dve.wait_ge(sem("sub_std"), 1)
                    dve.reciprocal(sub_dev, sub_dev).then_inc(*st.inc())
                    settle()
                    for h in range(6):
                        if h >= 2:
                            dve.wait_ge(sem("sub_turned"), h - 1)
                        for qt in range(4):
                            at = 4 * h + qt
                            last = dve.tensor_scalar(sq[h % 2][:, P * qt:P * qt + P], ident, sub_dev[:, at:at + 1],
                                                     None, ALU.mult)
                        last.then_inc(sem("sub_diag"), 1)
                        if h == 0:
                            low(0)
                            low(1)
                        else:
                            low(h + 1)
                    low(7)
                    return
                for kt in range(KT):
                    low(kt)

            def residual(src, l, part, dt, c0):
                for s, lo, hi in streams(c0):
                    last = dve.scalar_tensor_tensor(x[:, dt, lo:hi], src(lo, hi),
                                                    mod[:, l, part * KT + dt, s:s + 1], x[:, dt, lo:hi], ALU.mult, ALU.add)
                return last

            def project_out(l):
                c0 = first_col(l, True)
                for c in range(OUT_CH):
                    if c + 1 < OUT_CH:
                        split_lo(dve, M0["out", l] + c + 1)
                    for dt in (2 * c, 2 * c + 1):
                        if dt % 2:
                            dve.wait_ge(sem("split_used"), M0["out", l] + c + 1)
                        else:
                            dve.wait_ge(sem("out_in"), 4 * l + c + 1)
                        residual(lambda lo, hi: bank[2 + dt % 2][:, lo:hi], l, 2, dt, c0).then_inc(sem("out_evac"), 1)

            def choose(l):
                tokens = NT - first_col(l, True)
                ntt = tokens // P
                m0 = M0["wq", l]
                rep = [view(at, 4, KEYS) for at in (A_REP, A_REP1)]
                cand, crep = view(A_CAND, 4, N_CAND), view(A_CREP, 4, N_CAND)
                eq = masks(ntt)
                sv = view(A_SMALL, 4, 2, TOPK)
                tv = view(A_SMALL + 256, 4, TOPK)
                tp = view(A_SMALL + 320, 64).bitcast(U32).rearrange("p (t k) -> p t k", t=4)
                pab = [view(A_SMALL + 384 + 64 * a, 64).bitcast(U32) for a in range(2)]
                gsum = view(A_SMALL + 512, 4)
                gd = [view(A_SMALL + 576 + 64 * b, 4, TOPK)[:, 0:ntt, :] for b in range(2)]
                idxg = view(A_IDXG, 3, 4, P)
                ts = Steps(sem(f"tk_step{l}"))

                def top16(src, again, vals, idxs, after_reads=None):
                    for tt in range(ntt):
                        dve.max(vals(tt)[:, 0:8], src(tt)).then_inc(*ts.inc())
                    dve.wait_ge(ts.sem, ts.n)
                    for tt in range(ntt):
                        dve.max_index(idxs(tt)[:, 0:8], vals(tt)[:, 0:8], src(tt)).then_inc(*ts.inc())
                        dve.match_replace(again(tt), vals(tt)[:, 0:8], src(tt), NEG).then_inc(*ts.inc())
                    dve.wait_ge(ts.sem, ts.n)
                    for tt in range(ntt):
                        last = dve.max(vals(tt)[:, 8:16], again(tt)).then_inc(*ts.inc())
                    if after_reads is not None:
                        dve.tensor_copy(gate[:, 1:2], ones[:, 0:1]).then_inc(after_reads, 1)
                    dve.wait_ge(ts.sem, ts.n)
                    for tt in range(ntt):
                        dve.max_index(idxs(tt)[:, 8:16], vals(tt)[:, 8:16], again(tt)).then_inc(*ts.inc())

                def finish(h, i):
                    g, col = gd[h % 2], ds(i * 64 + TOPK * h, TOPK)
                    dve.wait_ge(sem(f"gexp_done{l}"), i * 4 + (h + 1))
                    dve.tensor_reduce(gsum[:, 0:ntt], g, AX_X, ALU.add).then_inc(*ts.inc())
                    dve.wait_ge(sem(f"picked{l}"), i * 4 + (h + 1))
                    for a in range(2):
                        dve.tensor_reduce(idxg[:, a, 0:ntt, col], eq[h % 2][a].rearrange("p (t k) a -> p t k a", t=ntt),
                                          AX_X, ALU.add)
                    dve.wait_ge(ts.sem, ts.n)
                    dve.reciprocal(gsum[:, 0:ntt], gsum[:, 0:ntt]).then_inc(*ts.inc())
                    dve.wait_ge(ts.sem, ts.n)
                    dve.tensor_tensor(idxg[:, 2, 0:ntt, col], g,
                                      gsum[:, 0:ntt].rearrange("p (t k) -> p t k", k=1)
                                      .broadcast_to([P, ntt, TOPK]), ALU.mult).then_inc(sem(f"chosen{l}"), 1)

                dve.sem_inc(sem(f"sc_free{l}"), 2)
                if l == 0:
                    dve.sem_inc(sem("mod_evac1"), 1)
                with dve.Fori(0, 2) as i:
                    dve.sem_clear(ts.sem)
                    ts.restart()
                    for h in range(4):
                        for p in range(2):
                            j = 2 * h + p
                            dve.wait_ge(sem(f"sc_done{l}"), i * 8 + (j + 1 + 2))
                            dve.tensor_copy(gate[:, 0:1], ones[:, 0:1])
                            top16(lambda tt: bank[2 + p][:, tt * P:tt * P + P], lambda tt: rep[p][:, tt, :],
                                  lambda tt: sv[:, tt, p, :], lambda tt: indices(h % 2)[:, tt, p, :], sem(f"sc_free{l}"))
                            if h and not p:
                                finish(h - 1, i)
                        for a0, na, nb, at in ((0, A_WIDE, TOPK, 0), (A_WIDE, TOPK - A_WIDE, B_NARROW, A_WIDE * TOPK)):
                            dve.tensor_tensor(cand[:, 0:ntt, at:at + na * nb].rearrange("p t (a b) -> p t a b", b=nb),
                                              sv[:, 0:ntt, 0, a0:a0 + na].rearrange("p t (a b) -> p t a b", b=1)
                                              .broadcast_to([P, ntt, na, nb]),
                                              sv[:, 0:ntt, 1, 0:nb].rearrange("p t (a b) -> p t a b", a=1)
                                              .broadcast_to([P, ntt, na, nb]), ALU.add).then_inc(*ts.inc())
                        dve.wait_ge(ts.sem, ts.n)
                        top16(lambda tt: cand[:, tt, :], lambda tt: crep[:, tt, :], lambda tt: tv[:, tt, :],
                              lambda tt: tp[:, tt, :])
                        dve.wait_ge(ts.sem, ts.n)
                        dve.tensor_tensor(gd[h % 2], tv[:, 0:ntt, :], tv[:, 0:ntt, 0:1].broadcast_to([P, ntt, TOPK]),
                                          ALU.subtract).then_inc(sem(f"gd_done{l}"), 1)
                        tpf = tp[:, 0:ntt, :].rearrange("p t k -> p (t k)")
                        pa, pb = (w[:, 0:ntt * TOPK] for w in pab)
                        dve.tensor_scalar(pa, tpf, 2, None, ALU.logical_shift_right).then_inc(*ts.inc())
                        dve.wait_ge(ts.sem, ts.n)
                        step = TOPK - B_NARROW
                        dve.tensor_scalar(pa, pa, A_WIDE * TOPK // 4, step, ALU.max, ALU.mult).then_inc(*ts.inc())
                        dve.wait_ge(ts.sem, ts.n)
                        dve.scalar_tensor_tensor(tpf, pa, -step * A_WIDE * TOPK // 4, tpf, ALU.add,
                                                 ALU.add).then_inc(*ts.inc())
                        dve.wait_ge(ts.sem, ts.n)
                        dve.tensor_scalar(pa, tpf, 4, None, ALU.logical_shift_right).then_inc(*ts.inc())
                        dve.tensor_scalar(pb, tpf, 15, None, ALU.bitwise_and).then_inc(*ts.inc())
                        dve.wait_ge(ts.sem, ts.n)
                        index = indices(h % 2)[:, 0:ntt]
                        dve.tensor_copy(index.bitcast(F32), index)
                        for a in range(2):
                            last = dve.tensor_tensor(eq[h % 2][a], pab[a][:, 0:ntt * TOPK].rearrange("p (k a) -> p k a", a=1)
                                                     .broadcast_to([P, ntt * TOPK, TOPK]),
                                                     iota[:, 0:TOPK].rearrange("p (k a) -> p k a", k=1)
                                                     .broadcast_to([P, ntt * TOPK, TOPK]), ALU.is_equal)
                        last.then_inc(sem(f"eq_done{l}"), 1)
                    finish(3, i)
                    if l == 0:
                        modulation(1, i)

            def build(l):
                tokens = NT - first_col(l, True)
                idxt, oh = view(A_IDXT, 3, NT), view(A_ONEHOT, 4, 8, P)
                dve.wait_ge(sem("choices_evac"), 3 * (l + 1))
                with dve.Fori(0, tokens // (2 * TL)) as i:
                    for b in range(16):
                        dve.wait_ge(sem(f"w_done{l}"), i * 16 + (b + 1))
                        s0 = 1 if b % 4 == 3 else 0
                        at = idxt[:, s0:2, ds(i * (2 * TL) + 4 * b, 4)].rearrange("p s (t n) -> p s t n", n=1)
                        dve.tensor_tensor(oh[:, b % 4, 4 * s0:8].rearrange("p (s t) n -> p s t n", t=4),
                                          iota.rearrange("p (s t n) -> p s t n", s=1, t=1)
                                          .broadcast_to([P, 2 - s0, 4, P]),
                                          at.broadcast_to([P, 2 - s0, 4, P]), ALU.is_equal)\
                           .then_inc(sem(f"onehots{l}"), 1)
                dve.wait_ge(sem(f"w_done{l}"), 4 + tokens // 4)

            def experts(l):
                c0 = first_col(l, True)
                T = NT - c0
                m0, acc = M0["peer", l], view(A_ACC, KT, NT)
                done = sem(f"acc_done{l}")
                dve.memset(acc, 0.0).then_inc(done, 4)

                def add(g, i, dts, m):
                    for dt in dts:
                        if dt < KT - 1:
                            dve.wait_ge(sem(f"v_done{l}"), i * 28 + (7 * g + dt + 1))
                        else:
                            dve.wait_ge(sem("split_used"), i * 8 + (m + 1))
                        dve.tensor_tensor(acc[:, dt, 0:T], acc[:, dt, 0:T], bank[4 + dt % 4][:, 0:T],
                                          ALU.add).then_inc(done, 1)

                def step(g, i):
                    if not (isinstance(i, int) and g > 1):
                        split_lo(dve, m0 + 4 + 2 * g, i, 8)
                    dve.wait_ge(done, i * 32 + (8 * g + 4))
                    add(g, i, range(KT), m0 + 2 + 2 * g)

                split_lo(dve, m0 + 2)
                with dve.Fori(0, GROUPS // 4 - 1) as i:
                    for g in range(4):
                        step(g, i)
                r = GROUPS // 4 - 1
                for g in range(3):
                    step(g, r)
                dve.wait_ge(done, 32 * r + 8 * 3 + 4)
                for dt in range(KT + 1):
                    if dt < KT:
                        add(3, r, [dt], m0 + 2 + 5)
                    if dt:
                        dve.wait_ge(done, 32 * r + 24 + 4 + dt)
                        residual(lambda lo, hi: acc[:, dt - 1, lo - c0:hi - c0], l, 5, dt - 1, c0).then_inc(sem("x_done"), 1)
                if l == 0:
                    split_lo(dve, M0["in", 1])

            dve.wait_ge(sem("small_in"), 16)
            lam = small_of("lam")
            dve.tensor_tensor(lamv[0:HD, 0:2], lam[0:HD, 0:2], lam[0:HD, 2:4], ALU.mult).then_inc(sem("lam_prod"), 1)
            dve.tensor_scalar(sub8[:], small_of("subln"), 1.0 - LAM_INIT, None, ALU.mult).then_inc(*st.inc())
            dve.wait_ge(sem("lam_exp"), 1)
            dve.tensor_tensor(lamv[:, 5:6], lamv[:, 3:4], lamv[:, 2:3], ALU.subtract).then_inc(*st.inc())
            settle()
            dve.tensor_scalar(lamv[:, 4:5], lamv[:, 5:6], -LAM_INIT, None, ALU.add).then_inc(*st.inc())
            dve.wait_ge(sem("x_in"), 16)
            inverse_deviation(0)
            dve.sem_inc(sem("mod_evac0"), 1)
            with dve.Fori(0, 2) as i:
                modulation(0, i)
            gains(0)
            split_lo(dve, 0)
            for l in range(2):
                if l:
                    inverse_deviation(2)
                norm(2 * l)
                project(l)
                attention(l)
                mixed(l)
                project_out(l)
                inverse_deviation(2 * l + 1)
                norm(2 * l + 1)
                choose(l)
                if l == 0:
                    gains(1)
                build(l)
                experts(l)

        @block.gpsimd
        def _(pool):
            def load_keys(l):
                pool.wait_ge(sem("ylo"), KT * (l + 1))
                pool.dma_start(view(A_KEYS, 2048), keys[l]).then_inc(sem(f"keys_in{l}"), 16)

            def choose(l):
                m0, ntt = M0["wq", l], (NT - first_col(l, True)) // P
                eq = masks(ntt)
                lo_ready(pool, m0 - 2)
                lo_ready(pool, m0 - 1)
                split_lo(pool, m0)
                if l == 1:
                    split_lo(pool, m0 + 1)
                with pool.Fori(0, 2) as i:
                    if l == 0:
                        split_lo(pool, m0 + 1, i, 4)
                    for h in range(4):
                        if h < 3 or l == 1:
                            split_lo(pool, m0 + h + 2, i, 4)
                        pool.wait_ge(sem(f"eq_done{l}"), i * 4 + (h + 1))
                        index = indices(h % 2).bitcast(F32)
                        for a in range(2):
                            e4 = eq[h % 2][a].rearrange("p (t k) a -> p t k a", t=ntt)
                            last = pool.tensor_tensor(e4, e4, index[:, 0:ntt, a, :]
                                                      .rearrange("p t (k a) -> p t k a", k=1)
                                                      .broadcast_to([P, ntt, TOPK, TOPK]), ALU.mult)
                        last.then_inc(sem(f"picked{l}"), 1)

            def build(l):
                tokens = NT - first_col(l, True)
                idxt, oh = view(A_IDXT, 3, NT), view(A_ONEHOT, 4, 8, P)
                with pool.Fori(0, tokens // (2 * TL)) as i:
                    for b in range(16):
                        pool.wait_ge(sem(f"onehots{l}"), i * 16 + (b + 1))
                        second = oh[:, b % 4, 4:8, :]
                        gates = idxt[:, 2, ds(i * (2 * TL) + 4 * b, 4)].rearrange("p (t n) -> p t n", n=1)
                        pool.tensor_tensor(second, second, gates.broadcast_to([P, 4, P]),
                                           ALU.mult).then_inc(sem(f"oh_gated{l}"), 1)
                if l == 0:
                    split_lo(pool, M0["peer", l] + 1)

            def experts(l):
                T = NT - first_col(l, True)
                ntc = T // TL
                ge, pt = view(A_GE, 2, NT), view(A_PT, 2, NT)
                pool.sem_inc(sem(f"pm_done{l}"), 2)
                pool.sem_inc(sem(f"plo_done{l}"), 2)

                def gated(e, i):
                    w = e // 4
                    if e % 4 == 0:
                        pool.wait_ge(sem(f"w_in{l}_{w % 2}"), i * 16 + 16 * (w // 2 + 1))
                    pool.wait_ge(sem(f"ge_done{l}"), i * 8 + (e + 1))
                    pool.wait_ge(sem(f"plo_done{l}"), i * 8 + (e + 1))
                    wg = view(A_WG + 2048 * (w % 2), 16, 4, TL)[:, 0:ntc, e % 4, :]
                    pool.tensor_tensor(pt[:, e % 2, 0:T].rearrange("p (a b) -> p a b", b=TL),
                                       ge[:, e % 2, 0:T].rearrange("p (a b) -> p a b", b=TL), wg,
                                       ALU.mult).then_inc(sem(f"pm_done{l}"), 1)
                    pool.wait_ge(sem(f"phi_done{l}"), i * 8 + (e + 1))
                    pool.tensor_tensor(p_lo[:, e % 4, 0:T], pt[:, e % 2, 0:T], p_hi[:, e % 4, 0:T],
                                       ALU.subtract).then_inc(sem(f"plo_done{l}"), 1)

                m0, r = M0["peer", l], GROUPS // 4 - 1
                gated(0, 0)
                gated(1, 0)
                split_lo(pool, m0 + 3)
                with pool.Fori(0, r) as i:
                    for g in range(4):
                        gated(2 * g + 2, i)
                        gated(2 * g + 3, i)
                        split_lo(pool, m0 + 5 + 2 * g, i, 8)
                for g in range(3):
                    gated(2 * g + 2, r)
                    gated(2 * g + 3, r)
                    if g < 2:
                        split_lo(pool, m0 + 5 + 2 * g, r, 8)

            load_keys(0)
            choose(0)
            build(0)
            experts(0)
            pool.wait_ge(sem("split_used"), M0["in", 1])
            pool.dma_start(view(A_CS, 2 * NLAT), cs).then_inc(sem("cs_in1"), 16)
            pool.dma_start(view(A_BIAS, 4096), bias).then_inc(sem("bias_in"), 16)
            load_keys(1)
            choose(1)
            build(1)
            experts(1)


def constants():
    f = np.float32
    ident = np.eye(P, dtype=f)
    r = np.arange(P)
    blockones = (r[:, None] // HD == r[None, :] // HD).astype(f)
    rot = np.zeros((P, P), f)
    for m in range(P):
        if m % 32 < 16:
            rot[m, m + 16] = -1.0
        else:
            rot[m, m - 16] = 1.0
    t = np.arange(NLAT)
    inv = (f(10000.0) ** (-np.arange(16, dtype=f) / f(16))).astype(f)
    pos = np.where((r[:, None] % HD) // 32 == 0, t[None] // GRID_W, t[None] % GRID_W).astype(f)
    ang = (pos * inv[r % 16][:, None]).astype(f)
    cs = np.stack([np.cos(ang), np.sin(ang)], 1).astype(f).reshape(P, 2 * NLAT)
    poolm = np.zeros((4, 256, 256), f)
    for g, win in enumerate((2, 4, 8, 16)):
        for i in range(256):
            lo, hi = max(i - win // 2, 0), min(i + win // 2, 256)
            poolm[g, lo:hi, i] = f(1.0) / f(hi - lo)
            poolm[g, i, i] -= f(1.0)
    poolm = np.ascontiguousarray(poolm.reshape(4, 2, P, 256).transpose(2, 0, 1, 3)).reshape(P, 2048)
    qc, kc = np.arange(P)[:, None] % GRID_W, np.arange(GRID_W)[None]
    start = np.clip(qc - NA_COLS // 2, 0, GRID_W - NA_COLS)
    namask = np.where((kc >= start) & (kc < start + NA_COLS), 0.0, -1e30).astype(f)
    iota = np.broadcast_to(np.arange(P, dtype=f), (P, P))
    eps = np.broadcast_to(np.array([EPS, EPS * HD], f), (P, 2))
    return dict(ident=ident, blockones=blockones, rotT=rot.T, iota=iota, ones=np.ones((P, P), f), namask=namask,
                eps=eps), cs, poolm


def chunks_of(w):
    n = w.shape[1] // CW
    return w.reshape(KT, P, n, CW).transpose(2, 1, 0, 3).reshape(n, P, CHUNK)


def pair_heads(w, axis):
    order = np.concatenate([np.arange(h * HD, h * HD + HD) for j in range(4) for h in (j, j + 4)])
    return np.take(w, order, axis)


def lay_out(a):
    f = np.float32
    cols = lambda v: np.asarray(v).reshape(-1, P).T
    parts = []
    for what, l, _ in PARTS:
        g = lambda n: np.asarray(a[f"l{l}_{n}"])
        if what == "ada":
            parts.append(chunks_of(g("ada_w")))
        elif what == "in":
            w = g("w_in")
            if l == 0:
                w = np.concatenate([w[:, 256:], w[:, :256]], 1)
            else:
                cq, ck, cv, nq, nk, nv = np.split(w, [512, 640, 768, 1280, 1792], 1)
                w = np.concatenate([pair_heads(cq, 1), nq, ck, nk, cv, nv], 1)
            parts.append(chunks_of(w))
        elif what == "out":
            w = g("w_out")
            if l == 1:
                w = np.concatenate([pair_heads(w[:512], 0), w[512:]], 0)
            parts.append(chunks_of(w))
        elif what == "wq":
            w = chunks_of(g("peer_wq"))
            if l == 0:
                ada = chunks_of(np.asarray(a["l1_ada_w"])).reshape(HEADS, ADA_HEAD, P, CHUNK)
                w = np.concatenate([w[:, None], ada], 1).reshape(-1, P, CHUNK)
            parts.append(w)
        else:
            u = g("peer_u").reshape(P, GROUPS, 2, KT, P).transpose(1, 4, 3, 2, 0).reshape(GROUPS, P, CHUNK)
            v = g("peer_v").reshape(P, GROUPS, 2, D).transpose(1, 0, 2, 3).reshape(GROUPS, P, CHUNK)
            order = np.empty((PEER_CH, P, CHUNK), f)
            order[0] = u[0]
            order[1:PEER_CH - 1:2] = u[1:]
            order[2:PEER_CH - 1:2] = v[:-1]
            order[PEER_CH - 1] = v[-1]
            parts.append(order)
    stream = np.concatenate(parts, 0)
    x = np.concatenate([np.asarray(a["ctx"])[0], np.asarray(a["x"])[0]], 0)
    xT = np.ascontiguousarray(x.T.reshape(KT, P, NT).transpose(1, 0, 2))
    consts, cs, poolm = constants()
    c2 = np.stack([np.asarray(a["c"])[0], np.asarray(a["c_ctx"])], 1)
    lam = np.zeros((P, 4), f)
    for i, n in enumerate(("q1", "q2", "k1", "k2")):
        lam[:HD, i] = a[f"l0_lambda_{n}"]
    twice = lambda v: np.concatenate([v, v])
    pw = np.asarray(a["l0_pool_w"]).reshape(2, 2, HD, HD).transpose(1, 2, 0, 3).reshape(P, 2 * HD)
    fields = dict(
        consts,
        c=c2.reshape(KT, P, 2).transpose(1, 0, 2).reshape(P, KT * 2),
        ada_b=np.concatenate([cols(a["l0_ada_b"]), cols(a["l1_ada_b"])], 1),
        norm=np.concatenate([cols(a[n]) for n in ("l0_norm1", "l0_norm2", "l1_norm1", "l1_norm2")], 1),
        gain=np.stack([twice(np.asarray(a[n])) for n in ("l0_diff_qnorm", "l0_diff_knorm", "l1_gqa_qnorm", "l1_gqa_knorm",
                                                         "l1_na_qnorm", "l1_na_knorm")], 1),
        subln=np.asarray(a["l0_diff_subln"])[:, None], pscale=cols(a["l0_pool_scale"]), poolw=pw, lam=lam)
    small = np.concatenate([np.asarray(fields[n], f).reshape(P, w) for n, w in SMALL_SIZES], 1)
    keys = np.stack([np.asarray(a[f"l{l}_peer_keys"]).reshape(16, KEYS, P).transpose(2, 0, 1).reshape(P, 2048)
                     for l in range(2)])
    t = np.arange(NLAT)
    dr = t[None] // GRID_W - t[:, None] // GRID_W + 7
    dc = t[None] % GRID_W - t[:, None] % GRID_W + NA_COLS - 1
    far = (dc < 0) | (dc > 2 * NA_COLS - 2)
    rpb = np.asarray(a["l1_na_rpb"])[:, dr, np.where(far, 0, dc)]
    rpb = np.where(far[None], f(0), rpb)
    bias = rpb.reshape(8, 2, P, 256).transpose(2, 0, 1, 3).reshape(P, 4096)
    return dict(xT=xT, small=small, stream=stream, poolm=poolm, cs=cs, bias=np.ascontiguousarray(bias),
                keys=np.ascontiguousarray(keys))


def kernel(**inputs):
    import concourse.bacc as bacc
    from concourse.bass_utils import run_bass_kernel_spmd

    arrays = {k: np.ascontiguousarray(v) for k, v in lay_out(inputs).items()}
    nc = bacc.Bacc("TRN2", target_bir_lowering=False, num_devices=1)
    args = {k: nc.dram_tensor(k, v.shape, F32, kind="ExternalInput").ap() for k, v in arrays.items()}
    out = nc.dram_tensor("y", (P, KT, NLAT), F32, kind="ExternalOutput").ap()
    backbone(nc, **args, out=out)
    r = run_bass_kernel_spmd(nc, [arrays], core_ids=[0])
    y = r.results[0]["y"]
    return np.ascontiguousarray(y.transpose(2, 1, 0)).reshape(1, NLAT, D)
```
